# Optimizing a Trainium2 kernel written in Bass

```python
import math
import jax, jax.numpy as jnp
from jax import lax
import numpy as np

D_MODEL = 1024
BATCH = 1
SEQ = 256
DEPTH = 2
DEC_BATCH = 8
DEC_SEQ = 8
PAST_LEN = 1024
PAGE_SIZE = 128

HEAD_DIM = 64
N_MIX_HEADS = D_MODEL // HEAD_DIM
POOL_GROUPS = 4
POOL_WINDOWS = (2, 4, 8, 16)
POOL_GRP = HEAD_DIM
POOL_DIM = POOL_GROUPS * POOL_GRP
POOL_PAST = max(POOL_WINDOWS) - 1
ATT_HEADS = (N_MIX_HEADS - POOL_GROUPS) // 2
ATT_DIM = ATT_HEADS * HEAD_DIM
RET_HEADS = N_MIX_HEADS - POOL_GROUPS - ATT_HEADS
RET_DIM = RET_HEADS * HEAD_DIM
MIX_DIM = POOL_DIM + ATT_DIM + RET_DIM
IN_COLS = POOL_DIM + 3 * ATT_DIM + 4 * RET_DIM
MOBA_BLOCK = 256
MOBA_TOPK = 3
Q_BLOCK = 128
RET_CHUNK = 128
D_FF = ((8 * D_MODEL // 3 + 127) // 128) * 128
EPS = 1e-6

kernel_name = "hybrid_pool_moba_retention_step"

def rmsnorm(x, g):
    xf = x.astype(jnp.float32)
    y = xf * lax.rsqrt(jnp.mean(xf * xf, axis=-1, keepdims=True) + EPS)
    return (y * g.astype(jnp.float32)).astype(x.dtype)

def swiglu(h, w_in, w_out):
    gate, up = jnp.split(h @ w_in, 2, axis=-1)
    return (jax.nn.silu(gate) * up) @ w_out

def alibi_slopes():
    return jnp.exp2(-8.0 * jnp.arange(1, ATT_HEADS + 1, dtype=jnp.float32) / ATT_HEADS)

def retention_log_decay():
    return jnp.log1p(-jnp.exp2(-5.0 - jnp.arange(RET_HEADS, dtype=jnp.float32)))

def pool_mixer(u, prefix, pos, w_grp, scale):
    n, t, _ = u.shape
    ext = jnp.concatenate([prefix.astype(u.dtype), u], axis=1)
    cs = jnp.pad(jnp.cumsum(ext.astype(jnp.float32), axis=1), ((0, 0), (1, 0), (0, 0)))
    p = POOL_PAST
    end = cs[:, p + 1:p + 1 + t]
    pooled = []
    for g, w in enumerate(POOL_WINDOWS):
        sl = slice(g * POOL_GRP, (g + 1) * POOL_GRP)
        start = cs[:, p + 1 - w:p + 1 - w + t, sl]
        cnt = jnp.minimum(w, pos + 1).astype(jnp.float32)[None, :, None]
        pooled.append((end[..., sl] - start) / cnt)
    d = (jnp.concatenate(pooled, axis=-1) - u.astype(jnp.float32)).astype(u.dtype)
    d = d.reshape(n, t, POOL_GROUPS, POOL_GRP)
    y = jnp.einsum('ntgc,gcd->ntgd', d, w_grp).reshape(n, t, POOL_DIM) * scale
    return y, ext[:, -POOL_PAST:]

def moba_seq(q, k, v, q_pos):
    t = q.shape[0]
    l_keys = k.shape[0]
    nb = -(-l_keys // MOBA_BLOCK)
    pad = nb * MOBA_BLOCK - l_keys
    kb = jnp.pad(k, ((0, pad), (0, 0), (0, 0))).reshape(nb, MOBA_BLOCK, ATT_HEADS, HEAD_DIM).transpose(2, 0, 1, 3)
    vb = jnp.pad(v, ((0, pad), (0, 0), (0, 0))).reshape(nb, MOBA_BLOCK, ATT_HEADS, HEAD_DIM).transpose(2, 0, 1, 3)
    k_mean = jnp.mean(kb.astype(jnp.float32), axis=2)
    n_top = min(MOBA_TOPK, nb)
    qc = math.gcd(t, Q_BLOCK)
    qs = q.reshape(t // qc, qc, ATT_HEADS, HEAD_DIM).transpose(0, 2, 1, 3)
    ps = q_pos.reshape(t // qc, qc)
    blk_ids = jnp.arange(nb, dtype=jnp.int32)
    h_idx = jnp.arange(ATT_HEADS)[:, None, None]
    slopes = alibi_slopes()
    scale = HEAD_DIM ** -0.5

    def one_block(args):
        qh, pos = args
        own = pos // MOBA_BLOCK
        gate = jnp.einsum('hqd,hnd->hqn', qh.astype(jnp.float32), k_mean)
        fully_past = blk_ids[None, :] < own[:, None]
        gate = jnp.where(fully_past[None], gate, -jnp.inf)
        _, top = lax.top_k(gate, n_top)
        slot_ok = jnp.arange(n_top)[None, :] < jnp.minimum(own, MOBA_TOPK)[:, None]
        sel = jnp.concatenate([top.astype(jnp.int32), jnp.broadcast_to(own[None, :, None], (ATT_HEADS, qc, 1))], axis=-1)
        ok = jnp.concatenate([jnp.broadcast_to(slot_ok[None], (ATT_HEADS, qc, n_top)),
                              jnp.ones((ATT_HEADS, qc, 1), dtype=bool)], axis=-1)
        kg = kb[h_idx, sel]
        vg = vb[h_idx, sel]
        key_pos = sel[..., None] * MOBA_BLOCK + jnp.arange(MOBA_BLOCK, dtype=jnp.int32)
        qpos = pos[None, :, None, None]
        valid = ok[..., None] & (key_pos <= qpos)
        s = jnp.einsum('hqd,hqskd->hqsk', qh, kg, preferred_element_type=jnp.float32) * scale
        s = s - slopes[:, None, None, None] * (qpos - key_pos).astype(jnp.float32)
        s = jnp.where(valid, s, -jnp.inf)
        pr = jax.nn.softmax(s.reshape(ATT_HEADS, qc, -1), axis=-1).reshape(s.shape)
        return jnp.einsum('hqsk,hqskd->hqd', pr.astype(vg.dtype), vg)

    out = lax.map(one_block, (qs, ps))
    return out.transpose(0, 2, 1, 3).reshape(t, ATT_DIM)

def retention(q, k, v, s0):
    n, t, h, _ = q.shape
    dv = v.shape[-1]
    c = math.gcd(t, RET_CHUNK)
    nc = t // c
    lg = retention_log_decay()
    idx = jnp.arange(c, dtype=jnp.float32)
    diff = idx[:, None] - idx[None, :]
    d_in = jnp.exp(jnp.where(diff >= 0, lg[:, None, None] * diff, -jnp.inf))
    q_dec = jnp.exp(lg[:, None] * (idx + 1.0))
    k_dec = jnp.exp(lg[:, None] * (c - 1.0 - idx))
    c_dec = jnp.exp(lg * c)

    def chunks(a):
        return a.astype(jnp.float32).reshape(n, nc, c, h, a.shape[-1]).transpose(1, 0, 3, 2, 4)

    def step(s, xs):
        qc_, kc_, vc_ = xs
        att = jnp.einsum('nhid,nhjd->nhij', qc_, kc_) * d_in
        o = jnp.einsum('nhij,nhjv->nhiv', att, vc_) + jnp.einsum('nhid,nhdv->nhiv', qc_ * q_dec[..., None], s)
        s = s * c_dec[:, None, None] + jnp.einsum('nhjd,nhjv->nhdv', kc_ * k_dec[..., None], vc_)
        return s, o

    s, o = lax.scan(step, s0.astype(jnp.float32), (chunks(q), chunks(k), chunks(v)))
    return o.transpose(1, 0, 3, 2, 4).reshape(n, t, h, dv), s

def layer_fwd(x, pos0, pool_prefix, ret_s0, past_k, past_v,
              g_ffn1, f1_in, f1_out, g_mix, w_in, pool_w, pool_scale, w_out, g_ffn2, f2_in, f2_out):
    n, t, _ = x.shape
    pos = pos0 + jnp.arange(t, dtype=jnp.int32)
    x = x + 0.5 * swiglu(rmsnorm(x, g_ffn1), f1_in, f1_out)
    z = rmsnorm(x, g_mix) @ w_in
    sizes = (POOL_DIM, ATT_DIM, ATT_DIM, ATT_DIM, RET_DIM, RET_DIM, RET_DIM, RET_DIM)
    offs = [sum(sizes[:i + 1]) for i in range(len(sizes) - 1)]
    u, qa, ka, va, qr, kr, vr, gr = jnp.split(z, offs, axis=-1)
    y_pool, pool_new = pool_mixer(u, pool_prefix, pos, pool_w, pool_scale)
    qa = qa.reshape(n, t, ATT_HEADS, HEAD_DIM)
    ka = ka.reshape(n, t, ATT_HEADS, HEAD_DIM)
    va = va.reshape(n, t, ATT_HEADS, HEAD_DIM)
    if past_k is None:
        kf, vf = ka, va
    else:
        kf = jnp.concatenate([past_k.astype(ka.dtype), ka], axis=1)
        vf = jnp.concatenate([past_v.astype(va.dtype), va], axis=1)
    y_att = lax.map(lambda a: moba_seq(a[0], a[1], a[2], pos), (qa, kf, vf))
    o_r, ret_new = retention(qr.reshape(n, t, RET_HEADS, HEAD_DIM),
                             kr.reshape(n, t, RET_HEADS, HEAD_DIM) * (HEAD_DIM ** -0.5),
                             vr.reshape(n, t, RET_HEADS, HEAD_DIM), ret_s0)
    o_r = o_r * lax.rsqrt(jnp.mean(o_r * o_r, axis=-1, keepdims=True) + EPS)
    y_ret = (jax.nn.silu(gr.astype(jnp.float32)) * o_r.reshape(n, t, RET_DIM)).astype(x.dtype)
    x = x + jnp.concatenate([y_pool.astype(x.dtype), y_att.astype(x.dtype), y_ret], axis=-1) @ w_out
    x = x + 0.5 * swiglu(rmsnorm(x, g_ffn2), f2_in, f2_out)
    return x, ka, va, pool_new, ret_new.astype(x.dtype)

def setup_inputs(seed: int = 0) -> dict:
    key = jax.random.key(seed)
    ks = jax.random.split(key, 20)
    f32 = jnp.float32
    n_pages = PAST_LEN // PAGE_SIZE
    n_pool = (DEC_BATCH * n_pages * 5 + 3) // 4

    def nrm(k, shape, s):
        return jax.random.normal(k, shape, f32) * s

    page_table = jax.random.permutation(ks[6], n_pool)[:DEC_BATCH * n_pages].reshape(DEC_BATCH, n_pages).astype(jnp.int32)
    return {
        "x_prompt": nrm(ks[0], (BATCH, SEQ, D_MODEL), 1.0),
        "x_sample": nrm(ks[1], (DEC_BATCH, DEC_SEQ, D_MODEL), 1.0),
        "cache_k": nrm(ks[2], (DEPTH, n_pool, PAGE_SIZE, ATT_HEADS, HEAD_DIM), 1.0),
        "cache_v": nrm(ks[3], (DEPTH, n_pool, PAGE_SIZE, ATT_HEADS, HEAD_DIM), 1.0),
        "state_pool": nrm(ks[4], (DEPTH, DEC_BATCH, POOL_PAST, POOL_DIM), 1.0),
        "state_ret": nrm(ks[5], (DEPTH, DEC_BATCH, RET_HEADS, HEAD_DIM, HEAD_DIM), 0.1),
        "page_table": page_table,
        "norm_ffn1": 1.0 + nrm(ks[7], (DEPTH, D_MODEL), 0.02),
        "ffn1_w_in": nrm(ks[8], (DEPTH, D_MODEL, 2 * D_FF), D_MODEL ** -0.5),
        "ffn1_w_out": nrm(ks[9], (DEPTH, D_FF, D_MODEL), D_FF ** -0.5),
        "norm_mix": 1.0 + nrm(ks[10], (DEPTH, D_MODEL), 0.02),
        "w_in": nrm(ks[11], (DEPTH, D_MODEL, IN_COLS), D_MODEL ** -0.5),
        "pool_w": nrm(ks[12], (DEPTH, POOL_GROUPS, POOL_GRP, POOL_GRP), POOL_GRP ** -0.5),
        "pool_scale": 1.0 + nrm(ks[13], (DEPTH, POOL_DIM), 0.1),
        "w_out": nrm(ks[14], (DEPTH, MIX_DIM, D_MODEL), MIX_DIM ** -0.5),
        "norm_ffn2": 1.0 + nrm(ks[15], (DEPTH, D_MODEL), 0.02),
        "ffn2_w_in": nrm(ks[16], (DEPTH, D_MODEL, 2 * D_FF), D_MODEL ** -0.5),
        "ffn2_w_out": nrm(ks[17], (DEPTH, D_FF, D_MODEL), D_FF ** -0.5),
        "norm_final": 1.0 + nrm(ks[18], (D_MODEL,), 0.02),
    }

def reference(x_prompt, x_sample, cache_k, cache_v, state_pool, state_ret, page_table,
              norm_ffn1, ffn1_w_in, ffn1_w_out, norm_mix, w_in, pool_w, pool_scale, w_out,
              norm_ffn2, ffn2_w_in, ffn2_w_out, norm_final):
    n_seq_dec, n_pages = page_table.shape
    past_len = n_pages * PAGE_SIZE
    n_prompt = x_prompt.shape[0]
    hp, hs = x_prompt, x_sample
    kp_l, vp_l, pp_l, rp_l, ks_l, vs_l, ps_l, rs_l = [], [], [], [], [], [], [], []
    for l in range(DEPTH):
        w = (norm_ffn1[l], ffn1_w_in[l], ffn1_w_out[l], norm_mix[l], w_in[l], pool_w[l],
             pool_scale[l], w_out[l], norm_ffn2[l], ffn2_w_in[l], ffn2_w_out[l])
        hp, kp, vp, pp, rp = layer_fwd(
            hp, 0, jnp.zeros((n_prompt, POOL_PAST, POOL_DIM), hp.dtype),
            jnp.zeros((n_prompt, RET_HEADS, HEAD_DIM, HEAD_DIM), jnp.float32), None, None, *w)
        past_k = cache_k[l][page_table].reshape(n_seq_dec, past_len, ATT_HEADS, HEAD_DIM)
        past_v = cache_v[l][page_table].reshape(n_seq_dec, past_len, ATT_HEADS, HEAD_DIM)
        hs, ks_, vs_, ps_, rs_ = layer_fwd(hs, past_len, state_pool[l], state_ret[l], past_k, past_v, *w)
        kp_l.append(kp); vp_l.append(vp); pp_l.append(pp); rp_l.append(rp)
        ks_l.append(ks_); vs_l.append(vs_); ps_l.append(ps_); rs_l.append(rs_)
    return (rmsnorm(hp, norm_final), rmsnorm(hs, norm_final),
            jnp.stack(kp_l), jnp.stack(vp_l), jnp.stack(pp_l), jnp.stack(rp_l),
            jnp.stack(ks_l), jnp.stack(vs_l), jnp.stack(ps_l), jnp.stack(rs_l))


_drawn_inputs = setup_inputs


def setup_inputs(seed=0):
    import zlib

    import numpy as np

    out = dict(_drawn_inputs(seed))
    spreads = {}
    factors = {'norm_ffn1': 3.554, 'norm_final': 8.431, 'pool_scale': 4.111, 'norm_ffn2': 8.0}
    for name, (base, spread) in spreads.items():
        noise = np.random.default_rng([zlib.crc32(name.encode()), seed]).standard_normal(out[name].shape)
        drawn = base * np.exp(spread * noise) if base else spread * noise
        out[name] = __import__('jax').numpy.asarray(drawn.astype(out[name].dtype))
    for name, factor in factors.items():
        out[name] = (out[name] * factor).astype(out[name].dtype)
    return out
```

```python
from contextlib import ExitStack

import numpy as np
import concourse.bass as bass
from concourse import mybir

F32 = mybir.dt.float32
F32R = mybir.dt.float32r
I32 = mybir.dt.int32
ALU = mybir.AluOpType
ACT = mybir.ActivationFunctionType
AX = mybir.AxisListType.X

P = 128
D = 1024
KT = D // P
DEPTH = 2
SEQ = 256
NB, NT = 8, 8
SMP = NB * NT
TOK = SEQ + SMP
HD = 64
H = 6
HDIM = H * HD
POOL = 256
WINDOWS = (2, 4, 8, 16)
PAST = 15
PAGE = 128
PAGES = 8
PAST_LEN = PAGE * PAGES
POOL_PAGES = 80
FF = 2816
FT = FF // P
ZT = 23
EPS = 1e-6
BIG = 1.0e30
ATT_SCALE = HD ** -0.5
SLOPES = [2.0 ** (-8.0 * (h + 1) / H) for h in range(H)]
GAMMAS = [1.0 - 2.0 ** (-5.0 - h) for h in range(H)]
NORMS = 3 * DEPTH + 1
ZU, ZQA, ZKA, ZVA, ZQR, ZKR, ZVR, ZG = 0, 2, 5, 8, 11, 14, 17, 20

OUT_K = ((0, 8), (8, 15), (15, 22))
C_F1I, C_F1O, C_MIX, C_WO, C_F2I, C_F2O, C_ALL = 0, 22, 34, 46, 50, 72, 84
G_F1I, G_F1O, G_MIX, G_WO, G_F2I, G_F2O, G_ALL = 0, 22, 26, 38, 42, 64, 68
GROUPS0 = 4


def constants():
    f = np.float32
    c = {}
    c["ident"] = np.eye(P, dtype=f)
    q = np.arange(P)[:, None]
    dist = np.zeros((P, 3 * P))
    k = np.arange(2 * P)[None, :]
    dist[:, :256] = np.where(k <= q + P, q + P - k, BIG)
    k = np.arange(P)[None, :]
    dist[:, 256:] = np.where(k <= q, q - k, BIG)
    c["dist_p"] = dist.astype(f)
    g = np.array(GAMMAS)
    i = np.arange(SEQ)[None, None, :]
    j = np.arange(P)[:, None, None]
    c["decay_p"] = np.where(i >= j, ATT_SCALE * g[None, :, None] ** np.maximum(i - j, 0), 0.0).astype(f)
    row_q = np.tile(np.arange(NT), 2 * H)
    row_h = np.tile(np.repeat(np.arange(H), NT), 2)
    row_b = np.repeat(np.arange(2), H * NT)
    sl = np.array(SLOPES)[row_h]
    c["alibi_s"] = (-sl[:, None] * (PAST_LEN + row_q[:, None] - np.arange(PAST_LEN)[None, :])).astype(f)
    key_b, key_j = np.divmod(np.arange(SMP), NT)
    own = np.full((2 * H * NT, NB // 2, SMP), -BIG)
    for p in range(NB // 2):
        ok = (key_b[None, :] == 2 * p + row_b[:, None]) & (key_j[None, :] <= row_q[:, None])
        own[:, p][ok] = (-sl[:, None] * (row_q[:, None] - key_j[None, :]))[ok]
    c["alibi_own"] = own.astype(f)
    same = (key_b[:, None] == key_b[None, :]) & (key_j[None, :] >= key_j[:, None])
    diff = np.maximum(key_j[None, :] - key_j[:, None], 0)
    c["decay_s"] = np.where(same[:, None, :], ATT_SCALE * g[None, :, None] ** diff[:, None, :], 0.0).astype(f)
    kd = np.zeros((P, 3, H))
    kd[:, 0] = ATT_SCALE * g[None] ** (SEQ - 1 - np.arange(P))[:, None]
    kd[:, 1] = ATT_SCALE * g[None] ** (P - 1 - np.arange(P))[:, None]
    kd[:SMP, 2] = ATT_SCALE * g[None] ** (NT - 1 - key_j)[:, None]
    c["k_decay"] = kd.astype(f)
    head = 2 * np.arange(3)[None, :] + (np.arange(P) // HD)[:, None]
    c["q_decay"] = (g[head][:, :, None] ** (key_j + 1)[None, None, :]).astype(f)
    c["c_decay"] = (g[head] ** NT).astype(f)
    c["own_b"] = (key_b[:, None] == np.arange(NB)[None, :]).astype(f)
    w = np.array(WINDOWS)[2 * np.arange(2)[None, :] + (np.arange(P) // HD)[:, None]]
    c["inv_cnt"] = (1.0 / np.minimum(w[:, :, None], np.arange(1, SEQ + 1)[None, None, :])).astype(f)
    c["rank"] = np.tile(np.arange(1, 5, dtype=f), (2 * H * NT, 1))
    hs = np.zeros((P, P), f)
    hs[:HD, :HD] = 1.0 / HD
    hs[HD:, HD:] = 1.0 / HD
    c["head_mean"] = hs
    return c


def build(nc, A, C, O):
    ctx = ExitStack()

    def sb(name, shape, dt=F32):
        return ctx.enter_context(nc.sbuf_tensor(name, shape, dt))

    def sem(name):
        return ctx.enter_context(nc.semaphore(name))

    with ctx:
        x = sb("x", [P, KT, TOK])
        h_hi = sb("h_hi", [P, KT, TOK], F32R)
        h_lo = sb("h_lo", [P, KT, TOK], F32R)
        w_raw = sb("w_raw", [P, 2, 16 * P])
        w_hi = sb("w_hi", [P, 2, 16 * P], F32R)
        w_lo = sb("w_lo", [P, 2, 16 * P], F32R)
        rstd = sb("rstd", [P, TOK])
        ssq = sb("ssq", [P, 2, TOK])
        gains = sb("gains", [P, NORMS * KT + 4])
        cst = {n: sb(n, list(C[n].shape)) for n in C}
        ident, head_mean = cst["ident"], cst["head_mean"]
        ones = sb("ones", [P, P])
        eps = sb("eps", [P, 1])
        pages = sb("pages", [1, NB * PAGES], I32)
        wbd = sb("wbd", [P, 2, P])
        q_hi = sb("q_hi", [P, 480], F32R)
        q_lo = sb("q_lo", [P, 480], F32R)
        st = sb("st", [P, 32])
        ss = sb("ss", [96, 48])
        tmp = sb("tmp", [P, 2460])
        t_gate = tmp[:, 0:640].rearrange("p (a n) -> p a n", a=2)
        t_up = tmp[:, 640:1280].rearrange("p (a n) -> p a n", a=2)
        t_sil = tmp[:, 1280:1920].rearrange("p (a n) -> p a n", a=2)
        sq_slot = [t_gate, t_up]

        zone_offset = (nc.sbuf_base + 31) // 32 * 32
        zone = sb("zone", [P, 5120 + 8])
        arena_offset = (nc.sbuf_base + 31) // 32 * 32
        arena = sb("arena", [P, 18496 + 8])
        zone_at, arena_at = zone_offset, arena_offset

        def at(name, shape, dt, base, kb):
            return nc.alloc_sbuf_tensor_at(name, shape, dt, offset=base + int(kb * 1024))

        kbuf = at("kbuf", [P, 2, 4, HDIM], F32, zone_at, 0)
        q_smp = at("q_smp", [P, 3, SMP], F32, zone_at, 12)
        k_own_hi = at("k_own_hi", [P, 3, SMP], F32R, zone_at, 12.75)
        k_own_lo = at("k_own_lo", [P, 3, SMP], F32R, zone_at, 13.5)
        v_own = at("v_own", [SMP, HDIM], F32, zone_at, 14.25)
        sp = at("sp", [96, PAST_LEN + SMP], F32, zone_at, 15.75)
        g_hi = at("g_hi", [P, KT, TOK], F32R, zone_at, 0)
        g_lo = at("g_lo", [P, KT, TOK], F32R, zone_at, 10)

        act_hi = at("act_hi", [P, FT, TOK], F32R, arena_at, 0)
        act_lo = at("act_lo", [P, FT, TOK], F32R, arena_at, 27.5)
        z = at("z", [P, ZT, TOK], F32, arena_at, 0)
        vbuf = at("vbuf", [P, 2, PAGES, HDIM], F32, arena_at, 0)
        kr_tok = at("kr_tok", [P, 3, HDIM], F32, arena_at, 28.75)
        vr_tok = at("vr_tok", [P, 3, HDIM], F32, arena_at, 33.25)
        va_tok = at("va_tok", [P, 2, HDIM], F32, arena_at, 37.75)
        ka_tok = at("ka_tok", [P, 3, HDIM], F32, arena_at, 40.75)
        u_tok = at("u_tok", [P, 2, POOL], F32, arena_at, 45.25)
        ext = at("ext", [P, 912], F32, arena_at, 47.25)
        s_p = at("s_p", [P, 2, 3 * P], F32, arena_at, 51)
        pt_p = at("pt_p", [P, 2, 3 * P], F32, arena_at, 54)
        kt_hi = at("kt_hi", [P, 2, 3, 512], F32R, arena_at, 28.75)
        kt_lo = at("kt_lo", [P, 2, 3, 512], F32R, arena_at, 40.75)
        pt_s = at("pt_s", [P, 9, 96], F32, arena_at, 53.5)
        o_tok = at("o_tok", [HDIM // NT, 2, HDIM], F32, arena_at, 57)
        v_bd = at("v_bd", [SMP, NB, HD], F32, arena_at, 57)
        att_p = at("att_p", [P, 3 * P], F32, arena_at, 59)
        att_s = at("att_s", [SMP, SMP], F32, arena_at, 60.5)
        s0 = at("s0", [P, 3, NB, HD], F32, arena_at, 60.75)
        o_sq = at("o_sq", [P, 3, TOK], F32, arena_at, 66.75)
        pre_tok = at("pre_tok", [NB * PAST, POOL], F32, arena_at, 70.5)
        sp_new = at("sp_new", [P, 3, HD], F32, arena_at, 71.5)
        q_dec = at("q_dec", [P, 3, SMP], F32, zone_at, 15.75)
        x_tok = at("x_tok", [P, 3, D], F32, arena_at, 0)
        g_rows = at("g_rows", [NORMS * KT + 4, P], F32, arena_at, 14)
        y_fin = at("y_fin", [P, KT, TOK], F32, arena_at, 0)
        y_tok = at("y_tok", [P, 3, D], F32, arena_at, 14)

        ps = ctx.enter_context(nc.psum_tensor("ps", [P, 8, 512], F32))

        w_landed = [sem("w_landed0"), sem("w_landed1")]
        hi_done = sem("hi_done")
        split_done = sem("split_done")
        chunk_used = sem("chunk_used")
        evac_done = sem("evac_done")
        silu_ready = sem("silu_ready")
        a_ready = sem("a_ready")
        a_hi = sem("a_hi")
        act_ready = sem("act_ready")
        g_hi_done = sem("g_hi_done")
        gx_ready = sem("gx_ready")
        sq_done = sem("sq_done")
        ssq_done = sem("ssq_done")
        stat_done = sem("stat_done")
        std_done = sem("std_done")
        loaded = sem("loaded")
        x_loaded = sem("x_loaded")
        prep = sem("prep")
        x_tr = sem("x_tr")
        gain_tr = sem("gain_tr")
        gain_ok = sem("gain_ok")
        aux_loaded = sem("aux_loaded")
        u_tr, pre_tr = sem("u_tr"), sem("pre_tr")
        u_out, pre_in = sem("u_out"), sem("pre_in")
        tr_done, tr_act, tr_dve = sem("tr_done"), sem("tr_act"), sem("tr_dve")
        s_done, s_max, s_exp, p_norm = sem("s_done"), sem("s_max"), sem("s_exp"), sem("p_norm")
        pt_done, pt_evac, oa_done, oa_hi = sem("pt_done"), sem("pt_evac"), sem("oa_done"), sem("oa_hi")
        r_done, r_mask, or_own, or_done = sem("r_done"), sem("r_mask"), sem("or_own"), sem("or_done")
        o_gated, o_sqd, g_silu, q_dec_ok = sem("o_gated"), sem("o_sqd"), sem("g_silu"), sem("q_dec_ok")
        mean_done, o_std, or_ready, or_hi = sem("mean_done"), sem("o_std"), sem("or_ready"), sem("or_hi")
        vbd_ok, vbd_used, sp_done = sem("vbd_ok"), sem("vbd_used"), sem("sp_done")
        st_smp, st_prm = sem("st_smp"), sem("st_prm")
        u_ext, pool_d, pool_mm, pool_hi = sem("u_ext"), sem("pool_d"), sem("pool_mm"), sem("pool_hi")
        kown_hi_s, kown_ok = sem("kown_hi_s"), sem("kown_ok")
        y_ready = sem("y_ready")
        k_landed = [sem("k_landed0"), sem("k_landed1")]
        v_landed = [sem("v_landed0"), sem("v_landed1")]
        qp_hi, qp_ok = sem("qp_hi"), sem("qp_ok")
        kt_tr, kt_hi_s, kt_ok, sc_done = sem("kt_tr"), sem("kt_hi_s"), sem("kt_ok"), sem("sc_done")
        own_done, sm_in, sm_bias, sm_exp, sm_ok = (sem("own_done"), sem("sm_in"), sem("sm_bias"),
                                                   sem("sm_exp"), sem("sm_ok"))
        pt2_done, pt2_evac, pv_done, ys_hi = sem("pt2_done"), sem("pt2_evac"), sem("pv_done"), sem("ys_hi")
        o_evac, ot_done = sem("o_evac"), sem("ot_done")
        stored_kv, stored_st = sem("stored_kv"), sem("stored_st")
        y_fin_ok, y_tr, y_tok_ok, stored_y = sem("y_fin_ok"), sem("y_tr"), sem("y_tok_ok"), sem("stored_y")
        waited = sem("waited")
        KV_STORES, ST_STORES, AUX_LOADS = 7, 8, 11

        def y_smp(buf, half, p):
            return buf[HD * half:HD * half + HD, 2:5, bass.ds(p * 16 + SEQ, 16)].rearrange("p f (b q) -> p b f q", b=2)

        def o_smp(half):
            return ps[HD * half:HD * half + HD, 7, 0:384].rearrange("p (b f x) -> p b f x", b=2, f=3)[:, :, :, 8 * half:8 * half + 8]

        def wait_apart(engine, semaphore, value):
            engine.wait_ge(semaphore, value)
            engine.sem_inc(waited, 1)

        block = ctx.enter_context(nc.Block())
        bc2 = lambda ap: ap.unsqueeze(1).to_broadcast([P, 2, TOK])

        @block.sync
        def _(sp_e):
            def load(src, slot, half, tiles, nk):
                sp_e.wait_ge(split_done, half * 2 + (slot + 1))
                dst = w_raw[:, slot, 0:tiles * P].rearrange("p (k c) -> p k c", k=nk)
                sp_e.dma_start(dst, src).then_inc(w_landed[slot], 16)

            def ffn_in(w, L, c0):
                with sp_e.Fori(0, FT // 2) as i:
                    for slot in range(2):
                        cols = bass.ds(i * 256 + slot * FF, 256)
                        load(w[bass.ds(L, 1), :, cols].rearrange("a (k p) c -> p (a k) c", p=P),
                             slot, L * (C_ALL // 2) + i + c0 // 2, 16, 8)

            def ffn_out(w, L, c0):
                with sp_e.Fori(0, 2) as i:
                    for g in range(2):
                        for n, (a, b) in enumerate(OUT_K):
                            c = 3 * g + n
                            src = w[bass.ds(L, 1), a * P:b * P, bass.ds(i * 512 + 256 * g, 256)]
                            load(src.rearrange("a (k p) c -> p (a k) c", p=P), c % 2,
                                 L * (C_ALL // 2) + i * 3 + (c0 + c) // 2, 2 * (b - a), b - a)

            def square(w, L, c0, at_c, slot, cols=256):
                src = w[bass.ds(L, 1), :, at_c].rearrange("a (k p) c -> p (a k) c", p=P)
                load(src, slot, c0, 8 * cols // P, 8)

            sp_e.dma_start(x_tok[:, 0:2, :], A["x_prompt"][0].rearrange("(t p) d -> p t d", p=P)).then_inc(x_loaded, 16)
            sp_e.dma_start(x_tok[0:SMP, 2, :], A["x_sample"].rearrange("b t d -> (b t) d")).then_inc(x_loaded, 16)
            sp_e.dma_start(ident[:], C["ident"]).then_inc(x_loaded, 16)
            for n, name in enumerate(("norm_ffn1", "norm_mix", "norm_ffn2")):
                for l in range(DEPTH):
                    r0 = (3 * l + n) * KT
                    sp_e.dma_start(g_rows[r0:r0 + KT, :], A[name][l].rearrange("(k p) -> k p", p=P)).then_inc(x_loaded, 16)
            sp_e.dma_start(g_rows[NORMS * KT - KT:NORMS * KT, :],
                           A["norm_final"].rearrange("(k p) -> k p", p=P)).then_inc(x_loaded, 16)
            sp_e.dma_start(g_rows[NORMS * KT:NORMS * KT + 4, :],
                           A["pool_scale"].rearrange("l (k p) -> (l k) p", p=P)).then_inc(x_loaded, 16)
            with sp_e.Fori(0, DEPTH) as L:
                half0 = L * (C_ALL // 2)
                ffn_in(A["ffn1_w_in"], L, C_F1I)
                ffn_out(A["ffn1_w_out"], L, C_F1O)
                with sp_e.Fori(0, 5) as i:
                    for slot in range(2):
                        square(A["w_in"], L, half0 + i + C_MIX // 2, bass.ds(i * 512 + 256 * slot, 256), slot)
                square(A["w_in"], L, half0 + (C_MIX // 2 + 5), slice(2560, 2816), 0)
                square(A["w_in"], L, half0 + (C_MIX // 2 + 5), slice(2816, 2944), 1, cols=P)
                for slot in range(2):
                    square(A["w_out"], L, half0 + C_WO // 2, slice(256 * slot, 256 * slot + 256), slot)
                sp_e.wait_ge(u_out, 2 * L + 2)
                sp_e.dma_start(O["pool_prompt"][bass.ds(L, 1), 0].rearrange("a t c -> (a t) c"),
                               u_tok[P - PAST:P, 0, :]).then_inc(stored_kv, 16)
                sp_e.dma_start(O["pool_sample"][bass.ds(L, 1), :, PAST - NT:PAST, :].rearrange("a b t c -> (a b) t c"),
                               u_tok[0:SMP, 1, :]).then_inc(stored_kv, 16)
                sp_e.dma_start(O["pool_sample"][bass.ds(L, 1), :, 0:PAST - NT, :].rearrange("a b t c -> (a b) t c"),
                               A["state_pool"][bass.ds(L, 1), :, NT:PAST, :].rearrange("a b t c -> (a b) t c")
                               ).then_inc(stored_kv, 16)
                sp_e.wait_ge(tr_act, 9 * L + 9)
                for name, src, own in (("k", ka_tok, ka_tok[0:SMP, 2, :]), ("v", va_tok, v_own[:, :])):
                    sp_e.dma_start(O[name + "_prompt"][bass.ds(L, 1), 0].rearrange("a (t p) h d -> p (a t) (h d)", p=P),
                                   src[:, 0:2, :]).then_inc(stored_kv, 16)
                    sp_e.dma_start(O[name + "_sample"][bass.ds(L, 1)].rearrange("a b t h d -> (a b t) (h d)"),
                                   own).then_inc(stored_kv, 16)

                def load_v(p, first):
                    for bb in range(2):
                        if not first:
                            wait_apart(sp_e, pv_done, L * NB + p * 2 + (bb - 1))
                        for j in range(PAGES):
                            page = sp_e.value_load(pages[0:1, bass.ds(p * 16 + (8 * bb + j), 1)],
                                                   min_val=0, max_val=POOL_PAGES - 1)
                            sp_e.dma_start(vbuf[:, bb, j, :],
                                           A["cache_v"][L, page].rearrange("t h d -> t (h d)")).then_inc(v_landed[bb], 16)

                sp_e.wait_ge(kown_ok, L + 1)
                sp_e.wait_ge(pool_d, L + 1)
                wait_apart(sp_e, vbd_used, H * L + H)
                load_v(0, True)
                sp_e.wait_ge(st_prm, L + 1)
                for half in range(2):
                    sp_e.dma_start(O["ret_prompt"][L, 0].rearrange("(f a) d v -> a d f v", a=2)[half],
                                   sp_new[HD * half:HD * half + HD, :, :]).then_inc(stored_st, 16)
                sp_e.wait_ge(st_smp, 3 * L + 3)
                for half in range(2):
                    for f in range(3):
                        sp_e.dma_start(O["ret_sample"][L, :, 2 * f + half].rearrange("b d v -> d b v"),
                                       s0[HD * half:HD * half + HD, f, :, :]).then_inc(stored_st, 16)
                with sp_e.Fori(1, 4) as p:
                    load_v(p, False)
                for slot in range(2):
                    square(A["w_out"], L, half0 + (C_WO // 2 + 1), slice(512 + 256 * slot, 768 + 256 * slot), slot)
                ffn_in(A["ffn2_w_in"], L, C_F2I)
                ffn_out(A["ffn2_w_out"], L, C_F2O)
            sp_e.wait_ge(y_tok_ok, 3)
            sp_e.dma_start(O["y_prompt"][0].rearrange("(t p) d -> p t d", p=P), y_tok[:, 0:2, :]).then_inc(stored_y, 16)
            sp_e.dma_start(O["y_sample"].rearrange("b t d -> (b t) d"), y_tok[0:SMP, 2, :]).then_inc(stored_y, 16)
            sp_e.wait_ge(stored_y, 32)
            sp_e.wait_ge(stored_kv, 16 * KV_STORES * DEPTH)
            sp_e.wait_ge(stored_st, 16 * ST_STORES * DEPTH)

        @block.gpsimd
        def _(pool):
            pool.dma_start(pages[:], A["page_table"].rearrange("b n -> (b n)").unsqueeze(0)).then_inc(loaded, 16)
            for n in C:
                if n != "ident":
                    pool.dma_start(cst[n][:], C[n]).then_inc(loaded, 16)
            pool.memset(wbd[:], 0.0).then_inc(prep, 1)
            pool.memset(q_hi[:].bitcast(F32), 0.0).then_inc(prep, 1)
            pool.memset(q_lo[:].bitcast(F32), 0.0).then_inc(prep, 1)

            def add_squares(q):
                for j in range(4):
                    s = sq_slot[j % 2]
                    if j == 0:
                        wait_apart(pool, sq_done, q + (j + 1))
                        pool.tensor_copy(ssq[:], s).then_inc(ssq_done, 1)
                    else:
                        pool.drain()
                        pool.wait_ge(sq_done, q + (j + 1))
                        pool.tensor_tensor(ssq[:], ssq[:], s, ALU.add).then_inc(ssq_done, 1)

            def load_k(L, g, slot, first=False):
                if not first:
                    wait_apart(pool, kt_tr, L * 48 + g * 3 - 3)
                for j in range(4):
                    page = pool.value_load(pages[0:1, bass.ds(g * 4 + j, 1)], min_val=0, max_val=POOL_PAGES - 1)
                    pool.dma_start(kbuf[:, slot, j, :],
                                   A["cache_k"][L, page].rearrange("t h d -> t (h d)")).then_inc(k_landed[slot], 16)

            add_squares(0)
            with pool.Fori(0, DEPTH) as L:
                add_squares(L * 12 + 4)
                pool.wait_ge(chunk_used, L * C_ALL + (C_MIX + 2))
                for t in range(2):
                    for a in range(2):
                        o = HD * a
                        pool.dma_start(wbd[o:o + HD, t, o:o + HD], A["pool_w"][L, 2 * t + a]).then_inc(aux_loaded, 16)
                for half in range(2):
                    for f in range(3):
                        pool.dma_start(s0[HD * half:HD * half + HD, f, :, :],
                                       A["state_ret"][L, :, 2 * f + half].rearrange("b d v -> d b v")).then_inc(aux_loaded, 16)
                pool.dma_start(pre_tok[:], A["state_pool"][L].rearrange("b t c -> (b t) c")).then_inc(aux_loaded, 16)
                load_k(L, 0, 0, True)
                load_k(L, 1, 1, True)

                ep = ext[:, 0:542].rearrange("p (t n) -> p t n", t=2)
                es = ext[:, 542:910].rearrange("p (t b n) -> p t b n", t=2, b=NB)
                sums = [(tmp[:, a:a + 542].rearrange("p (t n) -> p t n", t=2),
                         tmp[:, a + 542:a + 910].rearrange("p (t b n) -> p t b n", t=2, b=NB)) for a in (0, 910)]
                dm = tmp[:, 1820:2460].rearrange("p (t n) -> p t n", t=2)
                wait_apart(pool, evac_done, L * G_ALL + (GROUPS0 + G_MIX + 12))
                pool.memset(ep[:, :, 0:PAST], 0.0)
                pool.tensor_copy(ep[:, :, PAST:], z[:, ZU:ZU + 2, 0:SEQ])
                for t in range(2):
                    pool.tensor_copy(es[:, t, :, PAST:], z[:, ZU + t, SEQ:].rearrange("p (b n) -> p b n", b=NB)).then_inc(u_ext, 1)
                wait_apart(pool, pre_in, L + 1)
                src_p, src_s = ep, es
                for n, w in enumerate(WINDOWS):
                    s = w // 2
                    dst_p, dst_s = sums[n % 2]
                    pool.drain()
                    pool.tensor_tensor(dst_p[:, :, w - 1:], src_p[:, :, w - 1:], src_p[:, :, w - 1 - s:PAST + SEQ - s], ALU.add)
                    for t in range(2):
                        pool.tensor_tensor(dst_s[:, t, :, w - 1:], src_s[:, t, :, w - 1:],
                                           src_s[:, t, :, w - 1 - s:PAST + NT - s], ALU.add)
                    pool.drain()
                    o, t = HD * (n % 2), n // 2
                    d_p, d_s = dm[o:o + HD, t, 0:SEQ], dm[o:o + HD, t, SEQ:]
                    pool.tensor_tensor(d_p, dst_p[o:o + HD, t, PAST:], cst["inv_cnt"][o:o + HD, t, :], ALU.mult)
                    d_s3 = d_s.rearrange("p (b n) -> p b n", b=NB)
                    pool.tensor_scalar(d_s3, dst_s[o:o + HD, t, :, PAST:], 1.0 / w, None, ALU.mult)
                    pool.drain()
                    pool.tensor_tensor(d_p, d_p, z[o:o + HD, ZU + t, 0:SEQ], ALU.subtract)
                    ins = pool.tensor_tensor(d_s, d_s, z[o:o + HD, ZU + t, SEQ:], ALU.subtract)
                    src_p, src_s = dst_p, dst_s
                ins.then_inc(pool_d, 1)
                pool.wait_ge(tr_act, 9 * L + 9)
                for h in range(H):
                    if h:
                        pool.wait_ge(vbd_used, H * L + h)
                    pool.tensor_tensor(v_bd[:], vr_tok[0:SMP, 2, h * HD:h * HD + HD].unsqueeze(1).to_broadcast([SMP, NB, HD]),
                                       cst["own_b"][:].unsqueeze(2).to_broadcast([SMP, NB, HD]), ALU.mult).then_inc(vbd_ok, 1)
                with pool.Fori(1, 8) as i:
                    for slot in range(2):
                        load_k(L, i * 2 + slot, slot)
                add_squares(L * 12 + 8)
                add_squares(L * 12 + 12)

        @block.scalar
        def _(act):
            def hi_split(half, slot):
                act.wait_ge(w_landed[slot], half * 16 + 16)
                act.wait_ge(chunk_used, half * 2 + (slot + 1))
                act.activation(w_hi[:, slot, :], w_raw[:, slot, :], ACT.Copy).then_inc(hi_done, 1)

            def ffn_in(L, c0, g0, f):
                with act.Fori(0, FT // 2) as i:
                    half = L * (C_ALL // 2) + i + (c0 // 2 + 1)
                    n = f * (FT // 2) + i + 1
                    hi_split(half, 0)
                    act.wait_ge(evac_done, L * G_ALL + i * 2 + (GROUPS0 + g0 + 1))
                    act.activation(t_sil, t_gate, ACT.Silu).then_inc(silu_ready, 1)
                    hi_split(half, 1)
                    act.wait_ge(a_ready, n)
                    act.activation(act_hi[:, bass.ds(i * 2, 2), :], t_up, ACT.Copy).then_inc(a_hi, 1)

            def gx_pair(dst, norm, o, groups):
                act.wait_ge(evac_done, groups)
                for k in (2 * o, 2 * o + 1):
                    ins = act.activation(dst[:, k, :], x[:, k, :], ACT.Copy, scale=gains[:, bass.ds(norm * KT + k, 1)])
                ins.then_inc(g_hi_done, 1)

            def squares(norm, o):
                if o >= 2:
                    act.wait_ge(ssq_done, norm * 4 + (o - 1))
                act.activation(sq_slot[o % 2], x[:, 2 * o:2 * o + 2, :], ACT.Square).then_inc(sq_done, 1)

            def root(n):
                act.wait_ge(stat_done, n)
                act.activation(rstd[:], ps[:, 4, 0:TOK], ACT.Sqrt, scale=1.0 / D, bias=eps[:, 0:1]).then_inc(std_done, 1)

            def ffn_out(L, c0, g0, norm, dst, ahead):
                for g in range(4):
                    for n in range(3):
                        if n == 2:
                            gx_pair(dst, norm, g, L * G_ALL + (GROUPS0 + g0 + g + 1))
                            squares(norm, g)
                        c = 3 * g + n + 2
                        if ahead or c < 12:
                            hi_split(L * (C_ALL // 2) + (c0 + c) // 2, c % 2)

            act.wait_ge(gain_ok, 1)
            for j in range(4):
                gx_pair(h_hi, 0, j, j + 1)
                squares(0, j)
            with act.Fori(0, DEPTH) as L:
                half0 = L * (C_ALL // 2)
                norm = L * 3
                hi_split(half0, 0)
                hi_split(half0, 1)
                root(norm + 1)
                ffn_in(L, C_F1I, G_F1I, L * 2)
                ffn_out(L, C_F1O, G_F1O, norm + 1, h_hi, True)
                root(norm + 2)
                with act.Fori(0, 6) as i:
                    for slot in range(2):
                        hi_split(half0 + i + (C_MIX // 2 + 1), slot)

                act.wait_ge(evac_done, L * G_ALL + (GROUPS0 + G_MIX + 12))
                act.activation(z[:, ZG:ZG + 3, :], z[:, ZG:ZG + 3, :], ACT.Silu).then_inc(g_silu, 1)
                act.activation(k_own_hi[:], z[:, ZKA:ZKA + 3, SEQ:], ACT.Copy).then_inc(kown_hi_s, 1)
                act.wait_ge(u_tr, L + 1)
                act.activation(u_tok[:, 0, :], ps[:, 2, 0:POOL], ACT.Copy).then_inc(u_out, 1)
                act.activation(u_tok[0:SMP, 1, :], ps[0:SMP, 2, POOL:2 * POOL], ACT.Copy).then_inc(u_out, 1)
                for t in range(3):
                    n = P if t < 2 else SMP
                    for kind, bank, dst in ((0, 4, ka_tok[0:n, t, :]),
                                            (1, 5, va_tok[:, t, :] if t < 2 else v_own[:, :]),
                                            (3, 7, vr_tok[0:n, t, :])):
                        act.wait_ge(tr_done, 12 * L + (4 * t + kind + 1))
                        act.activation(dst, ps[0:n, bank, 0:HDIM], ACT.Copy).then_inc(tr_act, 1)
                for h in range(H):
                    f, s = h // 2, h % 2
                    act.wait_ge(s_max, 6 * L + (h + 1))
                    act.activation(s_p[:, s, 0:256], s_p[:, s, 0:256], ACT.Exp, scale=ATT_SCALE, bias=st[:, 0 + 2 * s:1 + 2 * s],
                                   accum_out=st[:, 4 + 2 * s:5 + 2 * s])
                    act.activation(s_p[:, s, 256:384], s_p[:, s, 256:384], ACT.Exp, scale=ATT_SCALE, bias=st[:, 1 + 2 * s:2 + 2 * s],
                                   accum_out=st[:, 5 + 2 * s:6 + 2 * s]).then_inc(s_exp, 1)
                    act.wait_ge(pt_done, 6 * L + (h + 1))
                    act.activation(pt_p[:, s, :], ps[:, 2 + s, 0:384], ACT.Copy).then_inc(pt_evac, 1)
                    if s:
                        act.wait_ge(o_gated, 3 * L + (f + 1))
                        act.activation(o_sq[:, f, :], ps[:, 7, 0:TOK], ACT.Square).then_inc(o_sqd, 1)
                        act.wait_ge(oa_done, 3 * L + (f + 1))
                        act.activation(h_hi[:, 2 + f, 0:SEQ], ps[:, 4, 0:SEQ], ACT.Copy).then_inc(oa_hi, 1)
                for t in range(2):
                    act.wait_ge(pool_mm, 2 * L + (t + 1))
                    act.activation(h_hi[:, t, :], ps[:, 5 + t, 0:TOK], ACT.Copy, scale=gains[:, bass.ds(L * 2 + (NORMS * KT + t), 1)]).then_inc(pool_hi, 1)
                act.wait_ge(sp_done, L + 1)
                act.activation(sp_new[:], ps[:, 0, 0:192].rearrange("p (f v) -> p f v", f=3), ACT.Copy).then_inc(st_prm, 1)
                for f in range(3):
                    act.wait_ge(mean_done, 3 * L + (f + 1))
                    act.activation(o_sq[:, f, :], ps[:, (4, 7, 5)[f], 0:TOK], ACT.Sqrt, bias=eps[:, 0:1]).then_inc(o_std, 1)
                for f in range(3):
                    act.wait_ge(or_ready, 3 * L + (f + 1))
                    act.activation(h_hi[:, 5 + f, :], z[:, ZG + f, :], ACT.Copy).then_inc(or_hi, 1)

                def qprep(p):
                    for half in range(2):
                        for bb in range(2):
                            ins = act.activation(
                                q_hi[HD * half:HD * half + HD, :].rearrange("p (f c) -> p f c", f=3)[:, :, 8 * half + 96 * bb:8 * half + 96 * bb + 8],
                                q_smp[HD * half:HD * half + HD, :, bass.ds(p * 16 + 8 * bb, 8)], ACT.Copy)
                    ins.then_inc(qp_hi, 1)

                def kt_evac(p, i):
                    act.wait_ge(sc_done, L * 16 + p * 4 + (i + 1))
                    for f in range(3):
                        act.wait_ge(kt_tr, L * 48 + p * 12 + (3 * i + f + 1))
                        act.activation(kt_hi[:, i % 2, f, :], ps[:, 4 + f, :], ACT.Copy).then_inc(kt_hi_s, 1)

                def exps(p):
                    act.wait_ge(sm_bias, L * 4 + p + 1)
                    for n in range(5):
                        a, b = (256 * n, 256 * n + 256) if n < 4 else (PAST_LEN, PAST_LEN + SMP)
                        ins = act.activation(sp[:, a:b], sp[:, a:b], ACT.Exp, bias=ss[:, 32 + n:33 + n],
                                             accum_out=ss[:, 40 + n:41 + n])
                    ins.then_inc(sm_exp, 1)

                def outs(p):
                    act.wait_ge(pt2_done, L * 8 + p * 2 + 2)
                    act.activation(pt_s[:, 0:5, :], ps[:, 3, 0:480].rearrange("p (n c) -> p n c", c=96), ACT.Copy).then_inc(pt2_evac, 1)
                    act.wait_ge(pt2_done, L * 8 + p * 2 + 3)
                    act.activation(pt_s[:, 5:8, :], ps[:, 2, 0:288].rearrange("p (n c) -> p n c", c=96), ACT.Copy)
                    act.activation(pt_s[0:SMP, 8, :], ps[0:SMP, 2, 288:384], ACT.Copy).then_inc(pt2_evac, 1)
                    for bb in range(2):
                        act.wait_ge(pv_done, L * NB + p * 2 + (bb + 1))
                        act.activation(o_tok[:, bb, :], ps[0:48, (7, 3)[bb], 0:HDIM], ACT.Copy).then_inc(o_evac, 1)
                    act.wait_ge(ot_done, L * 4 + p + 1)
                    for half in range(2):
                        ins = act.activation(y_smp(h_hi, half, p), o_smp(half), ACT.Copy)
                    ins.then_inc(ys_hi, 1)

                act.wait_ge(stored_kv, L * (16 * KV_STORES) + 16 * KV_STORES)
                act.wait_ge(kown_ok, L + 1)

                def body(p, first):
                    kt_evac(p, 0)
                    if not first:
                        act.wait_ge(own_done, L * 4 + p)
                    qprep(p)
                    kt_evac(p, 1)
                    if not first:
                        exps(p - 1)
                    for i in range(2, 4):
                        kt_evac(p, i)
                    if not first:
                        outs(p - 1)
                body(0, True)
                with act.Fori(1, 4) as p:
                    body(p, False)
                exps(3)
                outs(3)

                for g in range(4):
                    gx_pair(g_hi, norm + 2, g, L * G_ALL + (GROUPS0 + G_WO + 1 + g))
                    squares(norm + 2, g)
                    hi_split(half0 + (C_WO // 2 + 1 + g // 2), g % 2)
                root(norm + 3)
                ffn_in(L, C_F2I, G_F2I, L * 2 + 1)
                ffn_out(L, C_F2O, G_F2O, norm + 3, h_hi, False)
            root(NORMS)
            for t in range(3):
                n = P if t < 2 else SMP
                for j in range(2):
                    act.wait_ge(y_tr, 2 * t + j + 1)
                    ins = act.activation(y_tok[0:n, t, 512 * j:512 * j + 512], ps[0:n, 2 * t + j, :], ACT.Copy)
                ins.then_inc(y_tok_ok, 1)


        @block.vector
        def _(dve):
            def lo_split(half, slot):
                dve.wait_ge(hi_done, half * 2 + (slot + 1))
                dve.tensor_tensor(w_lo[:, slot, :], w_raw[:, slot, :], w_hi[:, slot, :].bitcast(F32),
                                  ALU.subtract).then_inc(split_done, 1)

            def gx_pair(hi, lo, norm, o):
                dve.wait_ge(g_hi_done, norm * 4 + (o + 1))
                for k in (2 * o, 2 * o + 1):
                    ins = dve.scalar_tensor_tensor(out=lo[:, k, :], in0=x[:, k, :], scalar=gains[:, bass.ds(norm * KT + k, 1)],
                                                   in1=hi[:, k, :].bitcast(F32), op0=ALU.mult, op1=ALU.subtract)
                ins.then_inc(gx_ready, 1)

            def invert(n):
                dve.wait_ge(std_done, n)
                dve.reciprocal(rstd[:], rstd[:])
                dve.drain()

            def ffn_in(L, c0, g0, f):
                with dve.Fori(0, FT // 2) as i:
                    half = L * (C_ALL // 2) + i + (c0 // 2 + 1)
                    n = f * (FT // 2) + i + 1
                    dve.wait_ge(chunk_used, L * C_ALL + i * 2 + (c0 + 3))
                    dve.tensor_tensor(t_gate, ps[:, 0:2, 0:TOK], bc2(rstd[:]), ALU.mult).then_inc(evac_done, 1)
                    lo_split(half, 0)
                    dve.drain()
                    dve.wait_ge(chunk_used, L * C_ALL + i * 2 + (c0 + 4))
                    dve.tensor_tensor(t_up, ps[:, 2:4, 0:TOK], bc2(rstd[:]), ALU.mult).then_inc(evac_done, 1)
                    dve.drain()
                    dve.wait_ge(silu_ready, n)
                    dve.tensor_tensor(t_up, t_up, t_sil, ALU.mult).then_inc(a_ready, 1)
                    lo_split(half, 1)
                    dve.wait_ge(a_hi, n)
                    dve.tensor_tensor(act_lo[:, bass.ds(i * 2, 2), :], t_up, act_hi[:, bass.ds(i * 2, 2), :].bitcast(F32),
                                      ALU.subtract).then_inc(act_ready, 1)

            def add_to_x(L, g, chunks, scale):
                dve.wait_ge(chunk_used, L * C_ALL + (chunks + 2))
                b = 2 * (g % 2)
                dve.scalar_tensor_tensor(out=x[:, 2 * g:2 * g + 2, :], in0=ps[:, b:b + 2, 0:TOK], scalar=scale,
                                         in1=x[:, 2 * g:2 * g + 2, :], op0=ALU.mult, op1=ALU.add).then_inc(evac_done, 1)
                dve.drain()

            def ffn_out(L, c0, norm, ahead):
                for g in range(4):
                    for n in range(3):
                        if n == 2:
                            add_to_x(L, g, c0 + 3 * g + 3, 0.5)
                            gx_pair(h_hi, h_lo, norm, g)
                        c = 3 * g + n + 2
                        if ahead or c < 12:
                            lo_split(L * (C_ALL // 2) + (c0 + c) // 2, c % 2)

            dve.memset(ones[:], 1.0).then_inc(prep, 1)
            dve.memset(eps[:], EPS).then_inc(prep, 1)
            dve.memset(ss[:], 0.0).then_inc(prep, 1)
            dve.sem_inc(split_done, 2)
            dve.sem_inc(kt_ok, 3)
            dve.wait_ge(gain_tr, 1)
            dve.tensor_copy(gains[:], ps[:, 4, 0:NORMS * KT + 4]).then_inc(gain_ok, 1)
            dve.drain()
            for j in range(4):
                dve.wait_ge(x_tr, j + 1)
                b = 2 * (j % 2)
                dve.tensor_copy(x[:, 2 * j:2 * j + 2, :], ps[:, b:b + 2, 0:TOK]).then_inc(evac_done, 1)
                dve.drain()
                gx_pair(h_hi, h_lo, 0, j)
            dve.wait_ge(loaded, 16 * len(C))
            with dve.Fori(0, DEPTH) as L:
                half0 = L * (C_ALL // 2)
                norm = L * 3
                lo_split(half0, 0)
                lo_split(half0, 1)
                invert(norm + 1)
                ffn_in(L, C_F1I, G_F1I, L * 2)
                ffn_out(L, C_F1O, norm + 1, True)
                invert(norm + 2)
                with dve.Fori(0, 5) as i:
                    for slot in range(2):
                        dve.wait_ge(chunk_used, L * C_ALL + i * 2 + (C_MIX + slot + 3))
                        dve.tensor_tensor(z[:, bass.ds(i * 4 + 2 * slot, 2), :], ps[:, 2 * slot:2 * slot + 2, 0:TOK],
                                          bc2(rstd[:]), ALU.mult).then_inc(evac_done, 1)
                        lo_split(half0 + i + (C_MIX // 2 + 1), slot)
                dve.wait_ge(chunk_used, L * C_ALL + (C_MIX + 13))
                dve.tensor_tensor(z[:, 20:22, :], ps[:, 0:2, 0:TOK], bc2(rstd[:]), ALU.mult).then_inc(evac_done, 1)
                lo_split(half0 + (C_WO // 2), 0)
                dve.wait_ge(chunk_used, L * C_ALL + (C_MIX + 14))
                dve.tensor_tensor(z[:, 22, :], ps[:, 2, 0:TOK], rstd[:], ALU.mult).then_inc(evac_done, 1)
                lo_split(half0 + (C_WO // 2), 1)
                dve.drain()

                es = ext[:, 542:910].rearrange("p (t b n) -> p t b n", t=2, b=NB)
                dve.wait_ge(pre_tr, L + 1)
                for t in range(2):
                    ins = dve.tensor_copy(es[:, t, :, 0:PAST], ps[:, 3, 120 * t:120 * t + 120].rearrange("p (b n) -> p b n", b=NB))
                ins.then_inc(pre_in, 1)
                dve.tensor_copy(q_smp[:], z[:, ZQA:ZQA + 3, SEQ:])
                dve.tensor_tensor(q_dec[:], z[:, ZQR:ZQR + 3, SEQ:], cst["q_decay"][:], ALU.mult).then_inc(q_dec_ok, 1)
                dve.wait_ge(kown_hi_s, L + 1)
                dve.tensor_tensor(k_own_lo[:], z[:, ZKA:ZKA + 3, SEQ:], k_own_hi[:].bitcast(F32), ALU.subtract).then_inc(kown_ok, 1)
                for t in range(3):
                    n = P if t < 2 else SMP
                    dve.wait_ge(tr_done, 12 * L + (4 * t + 3))
                    dve.tensor_tensor(kr_tok[0:n, t, :].rearrange("p (h d) -> p h d", h=H),
                                      ps[0:n, 6, 0:HDIM].rearrange("p (h d) -> p h d", h=H),
                                      cst["k_decay"][0:n, t, :].unsqueeze(2).to_broadcast([n, H, HD]), ALU.mult).then_inc(tr_dve, 1)

                def smax(h):
                    s = h % 2
                    dve.wait_ge(s_done, H * L + (h + 1))
                    if h >= 2:
                        dve.wait_ge(pt_done, H * L + (h - 1))
                    dve.scalar_tensor_tensor(out=s_p[:, s, :], in0=cst["dist_p"][:], scalar=-SLOPES[h] / ATT_SCALE,
                                             in1=ps[:, s, 0:384], op0=ALU.mult, op1=ALU.add)
                    dve.drain()
                    dve.tensor_reduce(st[:, 8:9], s_p[:, s, 0:256], AX, ALU.max)
                    dve.tensor_reduce(st[:, 9:10], s_p[:, s, 256:384], AX, ALU.max)
                    dve.drain()
                    dve.tensor_scalar(st[:, 2 * s:2 * s + 2], st[:, 8:10], -ATT_SCALE, None, ALU.mult).then_inc(s_max, 1)

                def decay_mask(h):
                    dve.wait_ge(r_done, H * L + (h + 1))
                    dve.tensor_tensor(att_p[:, 0:256], ps[:, 5, 0:256], cst["decay_p"][:, h, :], ALU.mult)
                    dve.tensor_tensor(att_p[:, 256:384], ps[:, 5, 256:384], cst["decay_p"][:, h, 0:P], ALU.mult)
                    dve.tensor_tensor(att_s[:], ps[0:SMP, 5, 384:448], cst["decay_s"][:, h, :], ALU.mult).then_inc(r_mask, 1)

                def normalise(h):
                    s = h % 2
                    dve.wait_ge(s_exp, H * L + (h + 1))
                    dve.reciprocal(st[:, 12:14], st[:, 4 + 2 * s:6 + 2 * s])
                    dve.drain()
                    dve.tensor_scalar(s_p[:, s, 0:256], s_p[:, s, 0:256], st[:, 12:13], None, ALU.mult)
                    dve.tensor_scalar(s_p[:, s, 256:384], s_p[:, s, 256:384], st[:, 13:14], None, ALU.mult).then_inc(p_norm, 1)

                dve.wait_ge(g_silu, L + 1)
                smax(0)
                decay_mask(0)
                for h in range(H):
                    if h + 1 < H:
                        dve.drain()
                        smax(h + 1)
                    normalise(h)
                    if h + 1 < H:
                        decay_mask(h + 1)
                    if h % 2:
                        f = h // 2
                        dve.wait_ge(or_done, 3 * L + (f + 1))
                        dve.tensor_tensor(z[:, ZG + f, :], ps[:, 7, 0:TOK], z[:, ZG + f, :], ALU.mult).then_inc(o_gated, 1)
                        dve.wait_ge(oa_hi, 3 * L + (f + 1))
                        dve.tensor_tensor(h_lo[:, 2 + f, 0:SEQ], ps[:, 4, 0:SEQ], h_hi[:, 2 + f, 0:SEQ].bitcast(F32),
                                          ALU.subtract).then_inc(y_ready, 1)
                for t in range(2):
                    dve.wait_ge(pool_hi, 2 * L + (t + 1))
                    dve.scalar_tensor_tensor(out=h_lo[:, t, :], in0=ps[:, 5 + t, 0:TOK],
                                             scalar=gains[:, bass.ds(L * 2 + (NORMS * KT + t), 1)],
                                             in1=h_hi[:, t, :].bitcast(F32), op0=ALU.mult, op1=ALU.subtract).then_inc(y_ready, 1)
                for f in range(3):
                    dve.wait_ge(vbd_used, H * L + (2 * f + 2))
                    dve.scalar_tensor_tensor(out=s0[:, f, :, :].rearrange("p b v -> p (b v)"),
                                             in0=s0[:, f, :, :].rearrange("p b v -> p (b v)"), scalar=cst["c_decay"][:, f:f + 1],
                                             in1=ps[:, 1 + f, :], op0=ALU.mult, op1=ALU.add).then_inc(st_smp, 1)
                for f in range(3):
                    dve.wait_ge(o_std, 3 * L + (f + 1))
                    dve.reciprocal(o_sq[:, f, :], o_sq[:, f, :])
                    dve.drain()
                    dve.tensor_tensor(z[:, ZG + f, :], z[:, ZG + f, :], o_sq[:, f, :], ALU.mult).then_inc(or_ready, 1)
                for f in range(3):
                    dve.wait_ge(or_hi, 3 * L + (f + 1))
                    dve.tensor_tensor(h_lo[:, 5 + f, :], z[:, ZG + f, :], h_hi[:, 5 + f, :].bitcast(F32),
                                      ALU.subtract).then_inc(y_ready, 1)

                def qprep(p):
                    dve.wait_ge(qp_hi, L * 4 + p + 1)
                    for half in range(2):
                        o = HD * half
                        for bb in range(2):
                            c = 8 * half + 96 * bb
                            ins = dve.tensor_tensor(q_lo[o:o + HD, :].rearrange("p (f c) -> p f c", f=3)[:, :, c:c + 8],
                                                    q_smp[o:o + HD, :, bass.ds(p * 16 + 8 * bb, 8)],
                                                    q_hi[o:o + HD, :].rearrange("p (f c) -> p f c", f=3)[:, :, c:c + 8].bitcast(F32),
                                                    ALU.subtract)
                    ins.then_inc(qp_ok, 1)

                def kt_rest(p, i):
                    for f in range(3):
                        dve.wait_ge(kt_hi_s, L * 48 + p * 12 + (3 * i + f + 1))
                        dve.tensor_tensor(kt_lo[:, i % 2, f, :], ps[:, 4 + f, :], kt_hi[:, i % 2, f, :].bitcast(F32),
                                          ALU.subtract).then_inc(kt_ok, 1)

                def soft_in(p):
                    R = slice(0, 96)
                    dve.wait_ge(own_done, L * 4 + p + 1)
                    dve.wait_ge(pt2_done, L * 8 + p * 2 + 1)
                    for c in range(2):
                        dve.tensor_reduce(ss[:, 2 * c:2 * c + 2], ps[R, c, :].rearrange("p (a n) -> p a n", a=2), AX, ALU.add)
                        dve.scalar_tensor_tensor(out=sp[:, 512 * c:512 * c + 512], in0=ps[R, c, :], scalar=ATT_SCALE,
                                                 in1=cst["alibi_s"][:, 512 * c:512 * c + 512], op0=ALU.mult, op1=ALU.add)
                    dve.scalar_tensor_tensor(out=sp[:, PAST_LEN:], in0=ps[R, 2, 0:SMP], scalar=ATT_SCALE,
                                             in1=cst["alibi_own"][:, bass.ds(p, 1), :].rearrange("p a n -> p (a n)"),
                                             op0=ALU.mult, op1=ALU.add).then_inc(sm_in, 1)
                    dve.drain()

                def soft_bias():
                    dve.tensor_reduce(ss[:, 5:6], ss[:, 0:4], AX, ALU.min)
                    dve.tensor_reduce(ss[:, 25:29], sp[:, 0:PAST_LEN].rearrange("p (a n) -> p a n", a=4), AX, ALU.max)
                    dve.tensor_reduce(ss[:, 29:30], sp[:, PAST_LEN:], AX, ALU.max)
                    dve.drain()
                    dve.tensor_scalar(ss[:, 8:12], ss[:, 0:4], ss[:, 5:6], None, ALU.is_le)
                    dve.drain()
                    dve.tensor_tensor(ss[:, 12:16], ss[:, 8:12], cst["rank"][:], ALU.mult)
                    dve.drain()
                    dve.tensor_reduce(ss[:, 16:17], ss[:, 12:16], AX, ALU.max)
                    dve.drain()
                    dve.tensor_scalar(ss[:, 20:24], ss[:, 12:16], ss[:, 16:17], -BIG, ALU.is_equal, ALU.mult)
                    dve.drain()
                    dve.tensor_tensor(ss[:, 25:30], ss[:, 25:30], ss[:, 20:25], ALU.add)
                    dve.drain()
                    dve.tensor_reduce(ss[:, 30:31], ss[:, 25:30], AX, ALU.max)
                    dve.drain()
                    dve.tensor_scalar(ss[:, 32:37], ss[:, 20:25], ss[:, 30:31], None, ALU.subtract).then_inc(sm_bias, 1)

                def soft_b(p):
                    dve.wait_ge(sm_exp, L * 4 + p + 1)
                    dve.tensor_reduce(ss[:, 45:46], ss[:, 40:45], AX, ALU.add)
                    dve.drain()
                    dve.reciprocal(ss[:, 46:47], ss[:, 45:46])
                    dve.drain()
                    dve.tensor_scalar(sp[:], sp[:], ss[:, 46:47], None, ALU.mult).then_inc(sm_ok, 1)

                def y_rest(p):
                    dve.wait_ge(ys_hi, L * 4 + p + 1)
                    for half in range(2):
                        ins = dve.tensor_tensor(y_smp(h_lo, half, p), o_smp(half), y_smp(h_hi, half, p).bitcast(F32), ALU.subtract)
                    ins.then_inc(y_ready, 1)

                kt_rest(0, 0)
                qprep(0)
                for i in range(1, 4):
                    kt_rest(0, i)
                with dve.Fori(1, 4) as p:
                    kt_rest(p, 0)
                    soft_in(p - 1)
                    qprep(p)
                    kt_rest(p, 1)
                    soft_bias()
                    kt_rest(p, 2)
                    soft_b(p - 1)
                    kt_rest(p, 3)
                    y_rest(p - 1)
                soft_in(3)
                soft_bias()
                soft_b(3)
                y_rest(3)

                for g in range(4):
                    add_to_x(L, g, C_WO + g + 1, 1.0)
                    gx_pair(g_hi, g_lo, norm + 2, g)
                    lo_split(half0 + (C_WO // 2 + 1 + g // 2), g % 2)
                invert(norm + 3)
                ffn_in(L, C_F2I, G_F2I, L * 2 + 1)
                ffn_out(L, C_F2O, norm + 3, False)
            invert(NORMS)
            for k in range(KT):
                c = (NORMS - 1) * KT + k
                ins = dve.scalar_tensor_tensor(out=y_fin[:, k, :], in0=x[:, k, :], scalar=gains[:, c:c + 1], in1=rstd[:],
                                               op0=ALU.mult, op1=ALU.mult)
            ins.then_inc(y_fin_ok, 1)

        @block.tensor
        def _(pe):
            def products(slot, nk, cols, k0, k_all, hi, lo, bank, ready=None):
                for a in range(cols):
                    for kk in range(nk):
                        k = k0 + kk
                        if a == 0 and ready and kk in ready:
                            pe.wait_ge(*ready[kk])
                        w = slice((kk * cols + a) * P, (kk * cols + a + 1) * P)
                        out = ps[:, bank + a, 0:TOK]
                        pe.matmul(out, w_hi[:, slot, w], hi[:, k, :], start=(k == 0), stop=False)
                        pe.matmul(out, w_hi[:, slot, w], lo[:, k, :], start=False, stop=False)
                        ins = pe.matmul(out, w_lo[:, slot, w], hi[:, k, :], start=False, stop=(k == k_all - 1))
                ins.then_inc(chunk_used, 1)

            def chunk_split(half, slot):
                pe.wait_ge(split_done, half * 2 + (slot + 3))

            def banks_free(L, g):
                pe.wait_ge(evac_done, L * G_ALL + (GROUPS0 - 1) + g)

            def sum_squares(n):
                pe.wait_ge(ssq_done, n * 4)
                pe.matmul(ps[:, 4, 0:TOK], ones[:], ssq[:, 0, :], start=True, stop=False)
                pe.matmul(ps[:, 4, 0:TOK], ones[:], ssq[:, 1, :], start=False, stop=True).then_inc(stat_done, 1)

            def square_group(L, half, g, slot, hi, lo, ready, cols=2):
                chunk_split(half, slot)
                banks_free(L, g)
                products(slot, KT, cols, 0, KT, hi, lo, 2 * slot, ready)

            def gx(norm):
                return {0: (gx_ready, norm * 4 + 3), 6: (gx_ready, norm * 4 + 4)}

            def ffn_in(L, c0, g0, norm, hi, lo):
                half = L * (C_ALL // 2) + c0 // 2
                square_group(L, half, g0, 0, hi, lo, gx(norm))
                sum_squares(norm + 1)
                square_group(L, half, g0 + 1, 1, hi, lo, None)
                with pe.Fori(1, FT // 2) as i:
                    for slot in range(2):
                        square_group(L, half + i, i * 2 + (g0 + slot), slot, hi, lo, None)

            def ffn_out(L, c0, g0, f):
                with pe.Fori(0, 2) as i:
                    for g in range(2):
                        for n, (a, b) in enumerate(OUT_K):
                            c = 3 * g + n
                            chunk_split(L * (C_ALL // 2) + i * 3 + (c0 + c) // 2, c % 2)
                            pe.wait_ge(act_ready, f * (FT // 2) + (b + 1) // 2)
                            if n == 0:
                                banks_free(L, i * 2 + (g0 + g))
                            products(c % 2, b - a, 2, a, FT, act_hi, act_lo, 2 * g)

            for s, n in ((chunk_used, 2), (sc_done, 2), (pt2_done, 1)):
                pe.sem_inc(s, n)
            pe.wait_ge(x_loaded, 16 * 11)
            pe.transpose(ps[:, 4, 0:NORMS * KT + 4], g_rows[:], ident[0:NORMS * KT + 4, 0:NORMS * KT + 4]).then_inc(gain_tr, 1)
            for j in range(4):
                if j >= 2:
                    pe.wait_ge(evac_done, j - 1)
                for a in range(2):
                    k = 2 * j + a
                    for t in range(3):
                        n = P if t < 2 else SMP
                        ins = pe.transpose(ps[:, 2 * (j % 2) + a, t * P:t * P + n], x_tok[0:n, t, k * P:k * P + P], ident[0:n, 0:n])
                ins.then_inc(x_tr, 1)
            pe.wait_ge(prep, 6)
            with pe.Fori(0, DEPTH) as L:
                half0 = L * (C_ALL // 2)
                norm = L * 3
                ffn_in(L, C_F1I, G_F1I, norm, h_hi, h_lo)
                ffn_out(L, C_F1O, G_F1O, L * 2)
                square_group(L, half0 + C_MIX // 2, G_MIX, 0, h_hi, h_lo, gx(norm + 1))
                sum_squares(norm + 2)
                square_group(L, half0 + C_MIX // 2, G_MIX + 1, 1, h_hi, h_lo, None)
                with pe.Fori(1, 5) as i:
                    for slot in range(2):
                        square_group(L, half0 + i + C_MIX // 2, i * 2 + (G_MIX + slot), slot, h_hi, h_lo, None)
                square_group(L, half0 + (C_MIX // 2 + 5), G_MIX + 10, 0, h_hi, h_lo, None)
                square_group(L, half0 + (C_MIX // 2 + 5), G_MIX + 11, 1, h_hi, h_lo, None, cols=1)

                pe.wait_ge(evac_done, L * G_ALL + (GROUPS0 + G_MIX + 12))
                for t in range(2):
                    pe.transpose(ps[:, 2, P * t:P * t + P], z[:, ZU + t, P:2 * P], ident[:])
                for t in range(2):
                    ins = pe.transpose(ps[0:SMP, 2, POOL + P * t:POOL + P * t + P], z[:, ZU + t, SEQ:], ident[:])
                ins.then_inc(u_tr, 1)
                pe.wait_ge(aux_loaded, L * (16 * AUX_LOADS) + 16 * AUX_LOADS)
                for t in range(2):
                    ins = pe.transpose(ps[:, 3, 120 * t:120 * t + 120], pre_tok[:, P * t:P * t + P], ident[0:120, 0:120])
                ins.then_inc(pre_tr, 1)
                for t in range(3):
                    n = P if t < 2 else SMP
                    if t:
                        wait_apart(pe, tr_act, 9 * L + 3 * t)
                        wait_apart(pe, tr_dve, 3 * L + t)
                    for kind, zt in enumerate((ZKA, ZVA, ZKR, ZVR)):
                        for f in range(3):
                            ins = pe.transpose(ps[0:n, 4 + kind, P * f:P * f + P], z[:, zt + f, P * t:P * t + n], ident[:])
                        ins.then_inc(tr_done, 1)

                def scores(h):
                    f, o, s = h // 2, HD * (h % 2), h % 2
                    if h >= 2:
                        wait_apart(pe, s_max, H * L + (h - 1))
                    q, k = z[o:o + HD, ZQA + f, :], z[o:o + HD, ZKA + f, :]
                    pe.matmul(ps[:, s, 0:256], q[:, P:2 * P], k[:, 0:SEQ], start=True, stop=True)
                    pe.matmul(ps[:, s, 256:384], q[:, 0:P], k[:, 0:P], start=True, stop=True).then_inc(s_done, 1)

                def ret_scores(h):
                    f, o = h // 2, HD * (h % 2)
                    if h:
                        wait_apart(pe, r_mask, H * L + h)
                    q, k = z[o:o + HD, ZQR + f, :], z[o:o + HD, ZKR + f, :]
                    pe.matmul(ps[:, 5, 0:256], k[:, 0:P], q[:, 0:SEQ], start=True, stop=True)
                    pe.matmul(ps[:, 5, 256:384], k[:, P:2 * P], q[:, P:2 * P], start=True, stop=True)
                    pe.matmul(ps[0:SMP, 5, 384:448], k[:, SEQ:], q[:, SEQ:], start=True, stop=True).then_inc(r_done, 1)

                def ret_out(h):
                    f, o, c = h // 2, HD * (h % 2), slice(h * HD, h * HD + HD)
                    pe.wait_ge(r_mask, H * L + (h + 1))
                    if h % 2 == 0 and f:
                        pe.wait_ge(o_sqd, 3 * L + f)
                    pe.matmul(ps[o:o + HD, 7, 0:256], vr_tok[:, 0, c], att_p[:, 0:256], start=True, stop=False)
                    pe.matmul(ps[o:o + HD, 7, 128:256], vr_tok[:, 1, c], att_p[:, 256:384], start=False, stop=True)
                    pe.matmul(ps[o:o + HD, 7, 256:320], vr_tok[0:SMP, 2, c], att_s[:], start=True, stop=False).then_inc(or_own, 1)
                    wait_apart(pe, or_own, H * L + (h + 1))
                    for b in range(NB):
                        ins = pe.matmul(ps[o:o + HD, 7, 256 + 8 * b:264 + 8 * b], s0[o:o + HD, f, b, :],
                                        q_dec[o:o + HD, f, 8 * b:8 * b + 8], start=False, stop=(b == NB - 1))
                    if h % 2:
                        ins.then_inc(or_done, 1)

                def transpose_p(h):
                    s = h % 2
                    pe.wait_ge(p_norm, H * L + (h + 1))
                    if h >= 2:
                        pe.wait_ge(pt_evac, H * L + (h - 1))
                    for n, c in enumerate((256, 0, 128)):
                        ins = pe.transpose(ps[:, 2 + s, P * n:P * n + P], s_p[:, s, c:c + P], ident[:])
                    ins.then_inc(pt_done, 1)

                def att_out(h):
                    f, o, s, c = h // 2, HD * (h % 2), h % 2, slice(h * HD, h * HD + HD)
                    pe.wait_ge(pt_evac, H * L + (h + 1))
                    if s == 0 and f:
                        pe.wait_ge(y_ready, 12 * L + f)
                    pe.matmul(ps[o:o + HD, 4, 0:256], va_tok[:, 0, c], pt_p[:, s, 0:256], start=True, stop=False)
                    ins = pe.matmul(ps[o:o + HD, 4, 128:256], va_tok[:, 1, c], pt_p[:, s, 256:384], start=False, stop=True)
                    if s:
                        ins.then_inc(oa_done, 1)

                scores(0)
                pe.wait_ge(tr_act, 9 * L + 9)
                pe.wait_ge(tr_dve, 3 * L + 3)
                pe.wait_ge(q_dec_ok, L + 1)
                pe.wait_ge(u_out, 2 * L + 2)
                pe.wait_ge(pre_in, L + 1)
                ret_scores(0)
                for h in range(H):
                    if h + 1 < H:
                        scores(h + 1)
                    ret_out(h)
                    if h + 1 < H:
                        ret_scores(h + 1)
                    transpose_p(h)
                    att_out(h)
                pe.wait_ge(pool_d, L + 1)
                for t in range(2):
                    pe.matmul(ps[:, 5 + t, 0:TOK], wbd[:, t, :], tmp[:, 1820 + TOK * t:1820 + TOK * t + TOK],
                              start=True, stop=True).then_inc(pool_mm, 1)
                for h in range(H):
                    f, o, c = h // 2, HD * (h % 2), slice(h * HD, h * HD + HD)
                    for t in range(2):
                        ins = pe.matmul(ps[o:o + HD, 0, HD * f:HD * f + HD], kr_tok[:, t, c], vr_tok[:, t, c],
                                        start=(t == 0), stop=(t == 1))
                ins.then_inc(sp_done, 1)
                for h in range(H):
                    f, o, c = h // 2, HD * (h % 2), slice(h * HD, h * HD + HD)
                    wait_apart(pe, vbd_ok, H * L + (h + 1))
                    pe.matmul(ps[o:o + HD, 1 + f, :], kr_tok[0:SMP, 2, c], v_bd[:].rearrange("p b v -> p (b v)"),
                              start=True, stop=True).then_inc(vbd_used, 1)
                pe.wait_ge(o_sqd, 3 * L + 3)
                for f, bank in enumerate((4, 7, 5)):
                    pe.wait_ge(y_ready, 12 * L + (4 if f == 2 else 3))
                    pe.matmul(ps[:, bank, 0:TOK], head_mean[:], o_sq[:, f, :], start=True, stop=True).then_inc(mean_done, 1)

                def transpose_k(p, i):
                    pe.wait_ge(k_landed[i % 2], L * 512 + p * 128 + 64 * (i // 2 + 1))
                    for f in range(3):
                        pe.wait_ge(kt_ok, L * 48 + p * 12 + (3 * i + f + 1))
                        for j in range(4):
                            ins = pe.transpose(ps[:, 4 + f, P * j:P * j + P], kbuf[:, i % 2, j, P * f:P * f + P], ident[:])
                        ins.then_inc(kt_tr, 1)

                def key_scores(p, i):
                    bb, c = i // 2, i % 2
                    pe.wait_ge(kt_ok, L * 48 + p * 12 + (3 * i + 6))
                    for f in range(3):
                        q = slice(144 * f + 48 * bb, 144 * f + 48 * bb + 96)
                        out = ps[0:96, c, :]
                        pe.matmul(out, q_hi[:, q], kt_hi[:, i % 2, f, :], start=(bb == 0 and f == 0), stop=False)
                        pe.matmul(out, q_hi[:, q], kt_lo[:, i % 2, f, :], start=False, stop=False)
                        ins = pe.matmul(out, q_lo[:, q], kt_hi[:, i % 2, f, :], start=False, stop=(bb == 1 and f == 2))
                    ins.then_inc(sc_done, 1)

                def own_scores():
                    for bb in range(2):
                        for f in range(3):
                            q = slice(144 * f + 48 * bb, 144 * f + 48 * bb + 96)
                            out = ps[0:96, 2, 0:SMP]
                            pe.matmul(out, q_hi[:, q], k_own_hi[:, f, :], start=(bb == 0 and f == 0), stop=False)
                            pe.matmul(out, q_hi[:, q], k_own_lo[:, f, :], start=False, stop=False)
                            ins = pe.matmul(out, q_lo[:, q], k_own_hi[:, f, :], start=False, stop=(bb == 1 and f == 2))
                    ins.then_inc(own_done, 1)

                def transpose_probs(p, first):
                    pe.wait_ge(sm_ok, L * 4 + p + 1)
                    if not first:
                        pe.wait_ge(y_ready, 12 * L + p + 8)
                    for j in range(5):
                        ins = pe.transpose(ps[:, 3, 96 * j:96 * j + 96], sp[:, P * j:P * j + P], ident[0:96, 0:96])
                    ins.then_inc(pt2_done, 1)
                    for j in range(5, 8):
                        pe.transpose(ps[:, 2, 96 * (j - 5):96 * (j - 4)], sp[:, P * j:P * j + P], ident[0:96, 0:96])
                    pe.transpose(ps[0:SMP, 2, 288:384], sp[:, PAST_LEN:], ident[0:96, 0:96]).then_inc(pt2_done, 1)

                def smp_out(p):
                    pe.wait_ge(pt2_evac, L * 8 + p * 2 + 2)
                    for bb in range(2):
                        pe.wait_ge(v_landed[bb], L * 512 + p * 128 + 128)
                        out, c = ps[0:48, (7, 3)[bb], 0:HDIM], slice(48 * bb, 48 * bb + 48)
                        for j in range(PAGES):
                            pe.matmul(out, pt_s[:, j, c], vbuf[:, bb, j, :], start=(j == 0), stop=False)
                        pe.matmul(out, pt_s[0:SMP, 8, c], v_own[:, :], start=False, stop=True).then_inc(pv_done, 1)

                def transpose_out(p):
                    for bb in range(2):
                        wait_apart(pe, o_evac, L * NB + p * 2 + (bb + 1))
                        for f in range(3):
                            c = 192 * bb + 48 * f
                            ins = pe.transpose(ps[:, 7, c:c + 48], o_tok[:, bb, P * f:P * f + P], ident[0:48, 0:48])
                    ins.then_inc(ot_done, 1)

                def body(p, first, last):
                    transpose_k(p, 1)
                    pe.wait_ge(qp_ok, L * 4 + p + 1)
                    if not first:
                        pe.wait_ge(sm_in, L * 4 + p)
                    key_scores(p, 0)
                    transpose_k(p, 2)
                    key_scores(p, 1)
                    transpose_k(p, 3)
                    key_scores(p, 2)
                    if not first:
                        transpose_probs(p - 1, False)
                        smp_out(p - 1)
                    if not last:
                        transpose_k(p + 1, 0)
                    if not first:
                        transpose_out(p - 1)
                    key_scores(p, 3)
                    own_scores()

                pe.wait_ge(st_prm, L + 1)
                pe.wait_ge(st_smp, 3 * L + 3)
                pe.wait_ge(o_std, 3 * L + 3)
                pe.wait_ge(y_ready, 12 * L + 5)
                pe.wait_ge(kown_ok, L + 1)
                transpose_k(0, 0)
                body(0, True, False)
                with pe.Fori(1, 3) as p:
                    body(p, False, False)
                body(3, False, True)
                transpose_probs(3, False)
                smp_out(3)
                transpose_out(3)

                wait_apart(pe, y_ready, 12 * L + 12)
                with pe.Fori(0, 2) as i:
                    for slot in range(2):
                        square_group(L, half0 + i + C_WO // 2, i * 2 + (G_WO + slot), slot, h_hi, h_lo, None)
                ffn_in(L, C_F2I, G_F2I, norm + 2, g_hi, g_lo)
                ffn_out(L, C_F2O, G_F2O, L * 2 + 1)
            sum_squares(NORMS)
            pe.wait_ge(y_fin_ok, 1)
            for t in range(3):
                n = P if t < 2 else SMP
                for j in range(2):
                    for k in range(4):
                        ins = pe.transpose(ps[0:n, 2 * t + j, P * k:P * k + P], y_fin[:, 4 * j + k, t * P:t * P + n], ident[:])
                    ins.then_inc(y_tr, 1)


_INS = ["x_prompt", "x_sample", "cache_k", "cache_v", "state_pool", "state_ret", "page_table", "norm_ffn1", "ffn1_w_in",
        "ffn1_w_out", "norm_mix", "w_in", "pool_w", "pool_scale", "w_out", "norm_ffn2", "ffn2_w_in", "ffn2_w_out",
        "norm_final"]
_OUTS = [("y_prompt", (1, SEQ, D)), ("y_sample", (NB, NT, D)),
         ("k_prompt", (DEPTH, 1, SEQ, H, HD)), ("v_prompt", (DEPTH, 1, SEQ, H, HD)),
         ("pool_prompt", (DEPTH, 1, PAST, POOL)), ("ret_prompt", (DEPTH, 1, H, HD, HD)),
         ("k_sample", (DEPTH, NB, NT, H, HD)), ("v_sample", (DEPTH, NB, NT, H, HD)),
         ("pool_sample", (DEPTH, NB, PAST, POOL)), ("ret_sample", (DEPTH, NB, H, HD, HD))]


def kernel(**inputs):
    import concourse.bacc as _bacc
    from concourse.bass_utils import run_bass_kernel_spmd as _run

    nc = _bacc.Bacc("TRN2", target_bir_lowering=False, num_devices=1)
    arrays, A, C, O = {}, {}, {}, {}
    for name in _INS:
        a = np.ascontiguousarray(inputs[name])
        arrays["in_" + name] = a
        A[name] = nc.dram_tensor("in_" + name, a.shape, mybir.dt.from_np(a.dtype), kind="ExternalInput").ap()
    for name, a in constants().items():
        arrays["c_" + name] = a
        C[name] = nc.dram_tensor("c_" + name, a.shape, F32, kind="ExternalInput").ap()
    for name, shape in _OUTS:
        O[name] = nc.dram_tensor("out_" + name, shape, F32, kind="ExternalOutput").ap()
    build(nc, A, C, O)
    r = _run(nc, [arrays], core_ids=[0])
    return tuple(r.results[0]["out_" + name] for name, _ in _OUTS)
```

```python
from contextlib import ExitStack

import numpy as np
import concourse.bass as bass
from concourse import mybir

F32 = mybir.dt.float32
F32R = mybir.dt.float32r
I32 = mybir.dt.int32
ALU = mybir.AluOpType
ACT = mybir.ActivationFunctionType
AX = mybir.AxisListType.X

P = 128
D = 1024
KT = D // P
DEPTH = 2
SEQ = 256
NB, NT = 8, 8
SMP = NB * NT
TOK = SEQ + SMP
HD = 64
H = 6
HDIM = H * HD
POOL = 256
WINDOWS = (2, 4, 8, 16)
PAST = 15
PAGE = 128
PAGES = 8
PAST_LEN = PAGE * PAGES
POOL_PAGES = 80
FF = 2816
FT = FF // P
ZT = 23
EPS = 1e-6
BIG = 1.0e30
ATT_SCALE = HD ** -0.5
SLOPES = [2.0 ** (-8.0 * (h + 1) / H) for h in range(H)]
GAMMAS = [1.0 - 2.0 ** (-5.0 - h) for h in range(H)]
NORMS = 3 * DEPTH + 1
ZU, ZQA, ZKA, ZVA, ZQR, ZKR, ZVR, ZG = 0, 2, 5, 8, 11, 14, 17, 20

OUT_K = ((0, 8), (8, 15), (15, 22))
C_F1I, C_F1O, C_MIX, C_WO, C_F2I, C_F2O, C_ALL = 0, 22, 34, 46, 50, 72, 84
G_F1I, G_F1O, G_MIX, G_WO, G_F2I, G_F2O, G_ALL = 0, 22, 26, 38, 42, 64, 68
GROUPS0 = 4


def constants():
    f = np.float32
    c = {}
    c["ident"] = np.eye(P, dtype=f)
    q = np.arange(P)[:, None]
    dist = np.zeros((P, 3 * P))
    k = np.arange(2 * P)[None, :]
    dist[:, :256] = np.where(k <= q + P, q + P - k, BIG)
    k = np.arange(P)[None, :]
    dist[:, 256:] = np.where(k <= q, q - k, BIG)
    c["dist_p"] = dist.astype(f)
    g = np.array(GAMMAS)
    i = np.arange(SEQ)[None, None, :]
    j = np.arange(P)[:, None, None]
    c["decay_p"] = np.where(i >= j, ATT_SCALE * g[None, :, None] ** np.maximum(i - j, 0), 0.0).astype(f)
    row_q = np.tile(np.arange(NT), 2 * H)
    row_h = np.tile(np.repeat(np.arange(H), NT), 2)
    row_b = np.repeat(np.arange(2), H * NT)
    sl = np.array(SLOPES)[row_h]
    c["alibi_s"] = (-sl[:, None] * (PAST_LEN + row_q[:, None] - np.arange(PAST_LEN)[None, :])).astype(f)
    key_b, key_j = np.divmod(np.arange(SMP), NT)
    own = np.full((2 * H * NT, NB // 2, SMP), -BIG)
    for p in range(NB // 2):
        ok = (key_b[None, :] == 2 * p + row_b[:, None]) & (key_j[None, :] <= row_q[:, None])
        own[:, p][ok] = (-sl[:, None] * (row_q[:, None] - key_j[None, :]))[ok]
    c["alibi_own"] = own.astype(f)
    same = (key_b[:, None] == key_b[None, :]) & (key_j[None, :] >= key_j[:, None])
    diff = np.maximum(key_j[None, :] - key_j[:, None], 0)
    c["decay_s"] = np.where(same[:, None, :], ATT_SCALE * g[None, :, None] ** diff[:, None, :], 0.0).astype(f)
    kd = np.zeros((P, 3, H))
    kd[:, 0] = ATT_SCALE * g[None] ** (SEQ - 1 - np.arange(P))[:, None]
    kd[:, 1] = ATT_SCALE * g[None] ** (P - 1 - np.arange(P))[:, None]
    kd[:SMP, 2] = ATT_SCALE * g[None] ** (NT - 1 - key_j)[:, None]
    c["k_decay"] = kd.astype(f)
    head = 2 * np.arange(3)[None, :] + (np.arange(P) // HD)[:, None]
    c["q_decay"] = (g[head][:, :, None] ** (key_j + 1)[None, None, :]).astype(f)
    c["c_decay"] = (g[head] ** NT).astype(f)
    c["own_b"] = (key_b[:, None] == np.arange(NB)[None, :]).astype(f)
    w = np.array(WINDOWS)[2 * np.arange(2)[None, :] + (np.arange(P) // HD)[:, None]]
    c["inv_cnt"] = (1.0 / np.minimum(w[:, :, None], np.arange(1, SEQ + 1)[None, None, :])).astype(f)
    c["rank"] = np.tile(np.arange(1, 5, dtype=f), (2 * H * NT, 1))
    hs = np.zeros((P, P), f)
    hs[:HD, :HD] = 1.0 / HD
    hs[HD:, HD:] = 1.0 / HD
    c["head_mean"] = hs
    return c


def build(nc, A, C, O):
    ctx = ExitStack()

    def sb(name, shape, dt=F32):
        return ctx.enter_context(nc.sbuf_tensor(name, shape, dt))

    def sem(name):
        return ctx.enter_context(nc.semaphore(name))

    with ctx:
        x = sb("x", [P, KT, TOK])
        h_hi = sb("h_hi", [P, KT, TOK], F32R)
        h_lo = sb("h_lo", [P, KT, TOK], F32R)
        w_raw = sb("w_raw", [P, 2, 16 * P])
        w_hi = sb("w_hi", [P, 2, 16 * P], F32R)
        w_lo = sb("w_lo", [P, 2, 16 * P], F32R)
        rstd = sb("rstd", [P, TOK])
        ssq = sb("ssq", [P, 2, TOK])
        gains = sb("gains", [P, NORMS * KT + 4])
        cst = {n: sb(n, list(C[n].shape)) for n in C}
        ident, head_mean = cst["ident"], cst["head_mean"]
        ones = sb("ones", [P, P])
        eps = sb("eps", [P, 1])
        pages = sb("pages", [1, NB * PAGES], I32)
        wbd = sb("wbd", [P, 2, P])
        q_hi = sb("q_hi", [P, 480], F32R)
        q_lo = sb("q_lo", [P, 480], F32R)
        st = sb("st", [P, 32])
        rstd_tok = sb("rstd_tok", [P, 4])
        ss = sb("ss", [96, 48])
        tmp = sb("tmp", [P, 2460])
        t_gate = tmp[:, 0:640].rearrange("p (a n) -> p a n", a=2)
        t_up = tmp[:, 640:1280].rearrange("p (a n) -> p a n", a=2)
        t_sil = tmp[:, 1280:1920].rearrange("p (a n) -> p a n", a=2)
        sq_slot = [t_gate, t_up]

        zone_offset = (nc.sbuf_base + 31) // 32 * 32
        zone = sb("zone", [P, 5120 + 8])
        arena_offset = (nc.sbuf_base + 31) // 32 * 32
        arena = sb("arena", [P, 18496 + 8])
        zone_at, arena_at = zone_offset, arena_offset

        def at(name, shape, dt, base, kb):
            return nc.alloc_sbuf_tensor_at(name, shape, dt, offset=base + int(kb * 1024))

        kbuf = at("kbuf", [P, 2, 4, HDIM], F32, zone_at, 0)
        q_smp = at("q_smp", [P, 3, SMP], F32, zone_at, 12)
        k_own_hi = at("k_own_hi", [P, 3, SMP], F32R, zone_at, 12.75)
        k_own_lo = at("k_own_lo", [P, 3, SMP], F32R, zone_at, 13.5)
        v_own = at("v_own", [SMP, HDIM], F32, zone_at, 14.25)
        sp = at("sp", [96, PAST_LEN + SMP], F32, zone_at, 15.75)
        g_hi = at("g_hi", [P, KT, TOK], F32R, zone_at, 0)
        g_lo = at("g_lo", [P, KT, TOK], F32R, zone_at, 10)

        act_hi = at("act_hi", [P, FT, TOK], F32R, arena_at, 0)
        act_lo = at("act_lo", [P, FT, TOK], F32R, arena_at, 27.5)
        z = at("z", [P, ZT, TOK], F32, arena_at, 0)
        vbuf = at("vbuf", [P, 2, PAGES, HDIM], F32, arena_at, 0)
        kr_tok = at("kr_tok", [P, 3, HDIM], F32, arena_at, 28.75)
        vr_tok = at("vr_tok", [P, 3, HDIM], F32, arena_at, 33.25)
        va_tok = at("va_tok", [P, 2, HDIM], F32, arena_at, 37.75)
        ka_tok = at("ka_tok", [P, 3, HDIM], F32, arena_at, 40.75)
        u_tok = at("u_tok", [P, 2, POOL], F32, arena_at, 45.25)
        ext = at("ext", [P, 912], F32, arena_at, 47.25)
        s_p = at("s_p", [P, 2, 3 * P], F32, arena_at, 51)
        pt_p = at("pt_p", [P, 2, 3 * P], F32, arena_at, 54)
        kt_hi = at("kt_hi", [P, 2, 3, 512], F32R, arena_at, 28.75)
        kt_lo = at("kt_lo", [P, 2, 3, 512], F32R, arena_at, 40.75)
        pt_s = at("pt_s", [P, 9, 96], F32, arena_at, 53.5)
        o_tok = at("o_tok", [HDIM // NT, 2, HDIM], F32, arena_at, 57)
        v_bd = at("v_bd", [SMP, NB, HD], F32, arena_at, 57)
        att_p = [at("att_p0", [P, 3 * P], F32, arena_at, 59), at("att_p1", [P, 3 * P], F32, zone_at, 16.5)]
        att_s = [at("att_s0", [SMP, SMP], F32, arena_at, 60.5), at("att_s1", [SMP, SMP], F32, zone_at, 18)]
        s0 = at("s0", [P, 3, NB, HD], F32, arena_at, 60.75)
        o_sq = at("o_sq", [P, 3, TOK], F32, arena_at, 66.75)
        pre_tok = at("pre_tok", [NB * PAST, POOL], F32, arena_at, 70.5)
        sp_new = at("sp_new", [P, 3, HD], F32, arena_at, 71.5)
        q_dec = at("q_dec", [P, 3, SMP], F32, zone_at, 15.75)
        x_tok = at("x_tok", [P, 3, D], F32, arena_at, 0)
        g_rows = at("g_rows", [NORMS * KT + 4, P], F32, arena_at, 14)
        y_fin = at("y_fin", [P, KT, TOK], F32, arena_at, 0)
        y_tok = at("y_tok", [P, 3, D], F32, arena_at, 14)

        ps = ctx.enter_context(nc.psum_tensor("ps", [P, 8, 512], F32))

        w_landed = [sem("w_landed0"), sem("w_landed1")]
        hi_done = sem("hi_done")
        split_done = sem("split_done")
        chunk_used = sem("chunk_used")
        evac_done = sem("evac_done")
        silu_ready = sem("silu_ready")
        a_ready = sem("a_ready")
        a_hi = sem("a_hi")
        act_ready = sem("act_ready")
        g_hi_done = sem("g_hi_done")
        gx_ready = sem("gx_ready")
        sq_done = sem("sq_done")
        ssq_done = sem("ssq_done")
        stat_done = sem("stat_done")
        std_done = sem("std_done")
        loaded = sem("loaded")
        x_loaded, gain_loaded = sem("x_loaded"), sem("gain_loaded")
        GAIN_LOADS = 3 * DEPTH + 2
        prep = sem("prep")
        x_tr = sem("x_tr")
        gain_tr = sem("gain_tr")
        gain_ok = sem("gain_ok")
        aux_loaded = sem("aux_loaded")
        u_tr, pre_tr = sem("u_tr"), sem("pre_tr")
        u_out, pre_in = sem("u_out"), sem("pre_in")
        tr_done, tr_act, tr_dve = sem("tr_done"), sem("tr_act"), sem("tr_dve")
        s_done, s_max, s_exp, p_norm = sem("s_done"), sem("s_max"), sem("s_exp"), sem("p_norm")
        pt_done, pt_evac, oa_done, oa_hi = sem("pt_done"), sem("pt_evac"), sem("oa_done"), sem("oa_hi")
        r_done, r_mask, or_own, or_done = sem("r_done"), sem("r_mask"), sem("or_own"), sem("or_done")
        o_gated, o_sqd, g_silu, q_dec_ok = sem("o_gated"), sem("o_sqd"), sem("g_silu"), sem("q_dec_ok")
        mean_done, o_std, or_ready, or_hi = sem("mean_done"), sem("o_std"), sem("or_ready"), sem("or_hi")
        vbd_ok, vbd_used, sp_done = sem("vbd_ok"), sem("vbd_used"), sem("sp_done")
        st_smp, st_prm = sem("st_smp"), sem("st_prm")
        u_ext, pool_d, pool_mm, pool_hi = sem("u_ext"), sem("pool_d"), sem("pool_mm"), sem("pool_hi")
        kown_hi_s, kown_ok = sem("kown_hi_s"), sem("kown_ok")
        y_ready = sem("y_ready")
        k_landed = [sem("k_landed0"), sem("k_landed1")]
        v_landed = [sem("v_landed0"), sem("v_landed1")]
        qp_hi, qp_ok = sem("qp_hi"), sem("qp_ok")
        kt_tr, kt_hi_s, kt_ok, sc_done = sem("kt_tr"), sem("kt_hi_s"), sem("kt_ok"), sem("sc_done")
        own_done, sm_in, sm_bias, sm_exp, sm_ok = (sem("own_done"), sem("sm_in"), sem("sm_bias"),
                                                   sem("sm_exp"), sem("sm_ok"))
        pt2_done, pt2_evac, pv_done, ys_hi = sem("pt2_done"), sem("pt2_evac"), sem("pv_done"), sem("ys_hi")
        o_evac, ot_done = sem("o_evac"), sem("ot_done")
        stored_kv, stored_st = sem("stored_kv"), sem("stored_st")
        y_fin_act, y_fin_dve, y_tr = sem("y_fin_act"), sem("y_fin_dve"), sem("y_tr")
        y_tok_act, y_tok_dve, rstd_ok, stored_y = sem("y_tok_act"), sem("y_tok_dve"), sem("rstd_ok"), sem("stored_y")
        waited = sem("waited")
        KV_STORES, ST_STORES, AUX_LOADS = 7, 8, 11

        def y_smp(buf, half, p):
            return buf[HD * half:HD * half + HD, 2:5, bass.ds(p * 16 + SEQ, 16)].rearrange("p f (b q) -> p b f q", b=2)

        def o_smp(half):
            return ps[HD * half:HD * half + HD, 7, 0:384].rearrange("p (b f x) -> p b f x", b=2, f=3)[:, :, :, 8 * half:8 * half + 8]

        def wait_apart(engine, semaphore, value):
            engine.wait_ge(semaphore, value)
            engine.sem_inc(waited, 1)

        block = ctx.enter_context(nc.Block())
        bc2 = lambda ap: ap.unsqueeze(1).to_broadcast([P, 2, TOK])

        @block.sync
        def _(sp_e):
            def load(src, slot, half, tiles, nk):
                sp_e.wait_ge(split_done, half * 2 + (slot + 1))
                dst = w_raw[:, slot, 0:tiles * P].rearrange("p (k c) -> p k c", k=nk)
                sp_e.dma_start(dst, src).then_inc(w_landed[slot], 16)

            def ffn_in_first(w, layer, half):
                for slot in range(2):
                    cols = slice(slot * FF, slot * FF + 256)
                    load(w[layer:layer + 1, :, cols].rearrange("a (k p) c -> p (a k) c", p=P), slot, half, 16, 8)

            def ffn_in(w, L, c0, start=0):
                with sp_e.Fori(start, FT // 2) as i:
                    for slot in range(2):
                        cols = bass.ds(i * 256 + slot * FF, 256)
                        load(w[bass.ds(L, 1), :, cols].rearrange("a (k p) c -> p (a k) c", p=P),
                             slot, L * (C_ALL // 2) + i + c0 // 2, 16, 8)

            def ffn_out(w, L, c0):
                with sp_e.Fori(0, 2) as i:
                    for g in range(2):
                        for n, (a, b) in enumerate(OUT_K):
                            c = 3 * g + n
                            src = w[bass.ds(L, 1), a * P:b * P, bass.ds(i * 512 + 256 * g, 256)]
                            load(src.rearrange("a (k p) c -> p (a k) c", p=P), c % 2,
                                 L * (C_ALL // 2) + i * 3 + (c0 + c) // 2, 2 * (b - a), b - a)

            def square(w, L, c0, at_c, slot, cols=256):
                src = w[bass.ds(L, 1), :, at_c].rearrange("a (k p) c -> p (a k) c", p=P)
                load(src, slot, c0, 8 * cols // P, 8)

            sp_e.dma_start(ident[:], C["ident"]).then_inc(x_loaded, 16)
            for t in range(2):
                sp_e.dma_start(x_tok[:, t, :], A["x_prompt"][0, t * P:t * P + P, :]).then_inc(x_loaded, 16)
            sp_e.dma_start(x_tok[0:SMP, 2, :], A["x_sample"].rearrange("b t d -> (b t) d")).then_inc(x_loaded, 16)
            ffn_in_first(A["ffn1_w_in"], 0, 0)
            with sp_e.Fori(0, DEPTH) as L:
                half0 = L * (C_ALL // 2)
                ffn_in(A["ffn1_w_in"], L, C_F1I, 1)
                ffn_out(A["ffn1_w_out"], L, C_F1O)
                with sp_e.Fori(0, 5) as i:
                    for slot in range(2):
                        square(A["w_in"], L, half0 + i + C_MIX // 2, bass.ds(i * 512 + 256 * slot, 256), slot)
                square(A["w_in"], L, half0 + (C_MIX // 2 + 5), slice(2560, 2816), 0)
                square(A["w_in"], L, half0 + (C_MIX // 2 + 5), slice(2816, 2944), 1, cols=P)
                for slot in range(2):
                    square(A["w_out"], L, half0 + C_WO // 2, slice(256 * slot, 256 * slot + 256), slot)
                sp_e.wait_ge(u_out, 2 * L + 2)
                sp_e.dma_start(O["pool_prompt"][bass.ds(L, 1), 0].rearrange("a t c -> (a t) c"),
                               u_tok[P - PAST:P, 0, :]).then_inc(stored_kv, 16)
                sp_e.dma_start(O["pool_sample"][bass.ds(L, 1), :, PAST - NT:PAST, :].rearrange("a b t c -> (a b) t c"),
                               u_tok[0:SMP, 1, :]).then_inc(stored_kv, 16)
                sp_e.dma_start(O["pool_sample"][bass.ds(L, 1), :, 0:PAST - NT, :].rearrange("a b t c -> (a b) t c"),
                               A["state_pool"][bass.ds(L, 1), :, NT:PAST, :].rearrange("a b t c -> (a b) t c")
                               ).then_inc(stored_kv, 16)
                sp_e.wait_ge(tr_act, 9 * L + 9)
                for name, src, own in (("k", ka_tok, ka_tok[0:SMP, 2, :]), ("v", va_tok, v_own[:, :])):
                    sp_e.dma_start(O[name + "_prompt"][bass.ds(L, 1), 0].rearrange("a (t p) h d -> p (a t) (h d)", p=P),
                                   src[:, 0:2, :]).then_inc(stored_kv, 16)
                    sp_e.dma_start(O[name + "_sample"][bass.ds(L, 1)].rearrange("a b t h d -> (a b t) (h d)"),
                                   own).then_inc(stored_kv, 16)

                def load_v(p, first):
                    for bb in range(2):
                        if not first:
                            wait_apart(sp_e, pv_done, L * NB + p * 2 + (bb - 1))
                        for j in range(PAGES):
                            page = sp_e.value_load(pages[0:1, bass.ds(p * 16 + (8 * bb + j), 1)],
                                                   min_val=0, max_val=POOL_PAGES - 1)
                            sp_e.dma_start(vbuf[:, bb, j, :],
                                           A["cache_v"][L, page].rearrange("t h d -> t (h d)")).then_inc(v_landed[bb], 16)

                sp_e.wait_ge(kown_ok, L + 1)
                sp_e.wait_ge(pool_d, L + 1)
                wait_apart(sp_e, r_done, H * L + H)
                load_v(0, True)
                sp_e.wait_ge(st_prm, L + 1)
                for half in range(2):
                    sp_e.dma_start(O["ret_prompt"][L, 0].rearrange("(f a) d v -> a d f v", a=2)[half],
                                   sp_new[HD * half:HD * half + HD, :, :]).then_inc(stored_st, 16)
                sp_e.wait_ge(st_smp, 3 * L + 3)
                for half in range(2):
                    for f in range(3):
                        sp_e.dma_start(O["ret_sample"][L, :, 2 * f + half].rearrange("b d v -> d b v"),
                                       s0[HD * half:HD * half + HD, f, :, :]).then_inc(stored_st, 16)
                with sp_e.Fori(1, 4) as p:
                    load_v(p, False)
                for slot in range(2):
                    square(A["w_out"], L, half0 + (C_WO // 2 + 1), slice(512 + 256 * slot, 768 + 256 * slot), slot)
                ffn_in(A["ffn2_w_in"], L, C_F2I)
                ffn_out(A["ffn2_w_out"], L, C_F2O)
                ffn_in_first(A["ffn1_w_in"], DEPTH - 1, half0 + C_ALL // 2)
            for t in range(2):
                sp_e.wait_ge(y_tok_act, t + 1)
                sp_e.wait_ge(y_tok_dve, t + 1)
                sp_e.dma_start(O["y_prompt"][0, t * P:t * P + P, :], y_tok[:, t, :]).then_inc(stored_y, 16)
            sp_e.wait_ge(y_tok_act, 3)
            sp_e.wait_ge(y_tok_dve, 3)
            sp_e.dma_start(O["y_sample"].rearrange("b t d -> (b t) d"), y_tok[0:SMP, 2, :]).then_inc(stored_y, 16)
            sp_e.wait_ge(stored_y, 48)
            sp_e.wait_ge(stored_kv, 16 * KV_STORES * DEPTH)
            sp_e.wait_ge(stored_st, 16 * ST_STORES * DEPTH)

        @block.gpsimd
        def _(pool):
            pool.dma_start(pages[:], A["page_table"].rearrange("b n -> (b n)").unsqueeze(0)).then_inc(loaded, 16)
            pool.memset(wbd[:], 0.0).then_inc(prep, 1)
            pool.memset(q_hi[:].bitcast(F32), 0.0).then_inc(prep, 1)
            pool.memset(q_lo[:].bitcast(F32), 0.0).then_inc(prep, 1)

            def add_squares(q):
                for j in range(4):
                    s = sq_slot[j % 2]
                    if j == 0:
                        wait_apart(pool, sq_done, q + (j + 1))
                        pool.tensor_copy(ssq[:], s).then_inc(ssq_done, 1)
                    else:
                        pool.drain()
                        pool.wait_ge(sq_done, q + (j + 1))
                        pool.tensor_tensor(ssq[:], ssq[:], s, ALU.add).then_inc(ssq_done, 1)

            def load_k(L, g, slot, first=False):
                if not first:
                    wait_apart(pool, kt_tr, L * 48 + g * 3 - 3)
                for j in range(4):
                    page = pool.value_load(pages[0:1, bass.ds(g * 4 + j, 1)], min_val=0, max_val=POOL_PAGES - 1)
                    pool.dma_start(kbuf[:, slot, j, :],
                                   A["cache_k"][L, page].rearrange("t h d -> t (h d)")).then_inc(k_landed[slot], 16)

            add_squares(0)
            for n in C:
                if n != "ident":
                    pool.dma_start(cst[n][:], C[n]).then_inc(loaded, 16)
            with pool.Fori(0, DEPTH) as L:
                add_squares(L * 12 + 4)
                pool.wait_ge(chunk_used, L * C_ALL + (C_MIX + 2))
                for t in range(2):
                    for a in range(2):
                        o = HD * a
                        pool.dma_start(wbd[o:o + HD, t, o:o + HD], A["pool_w"][L, 2 * t + a]).then_inc(aux_loaded, 16)
                for half in range(2):
                    for f in range(3):
                        pool.dma_start(s0[HD * half:HD * half + HD, f, :, :],
                                       A["state_ret"][L, :, 2 * f + half].rearrange("b d v -> d b v")).then_inc(aux_loaded, 16)
                pool.dma_start(pre_tok[:], A["state_pool"][L].rearrange("b t c -> (b t) c")).then_inc(aux_loaded, 16)
                wait_apart(pool, chunk_used, L * C_ALL + (C_MIX + 7))
                load_k(L, 0, 0, True)
                load_k(L, 1, 1, True)

                ep = ext[:, 0:542].rearrange("p (t n) -> p t n", t=2)
                es = ext[:, 542:910].rearrange("p (t b n) -> p t b n", t=2, b=NB)
                sums = [(tmp[:, a:a + 542].rearrange("p (t n) -> p t n", t=2),
                         tmp[:, a + 542:a + 910].rearrange("p (t b n) -> p t b n", t=2, b=NB)) for a in (0, 910)]
                dm = tmp[:, 1820:2460].rearrange("p (t n) -> p t n", t=2)
                wait_apart(pool, evac_done, L * G_ALL + (GROUPS0 + G_MIX + 12))
                pool.memset(ep[:, :, 0:PAST], 0.0)
                pool.tensor_copy(ep[:, :, PAST:], z[:, ZU:ZU + 2, 0:SEQ])
                for t in range(2):
                    pool.tensor_copy(es[:, t, :, PAST:], z[:, ZU + t, SEQ:].rearrange("p (b n) -> p b n", b=NB)).then_inc(u_ext, 1)
                wait_apart(pool, pre_in, L + 1)
                src_p, src_s = ep, es
                for n, w in enumerate(WINDOWS):
                    s = w // 2
                    dst_p, dst_s = sums[n % 2]
                    pool.drain()
                    pool.tensor_tensor(dst_p[:, :, w - 1:], src_p[:, :, w - 1:], src_p[:, :, w - 1 - s:PAST + SEQ - s], ALU.add)
                    for t in range(2):
                        pool.tensor_tensor(dst_s[:, t, :, w - 1:], src_s[:, t, :, w - 1:],
                                           src_s[:, t, :, w - 1 - s:PAST + NT - s], ALU.add)
                    pool.drain()
                    o, t = HD * (n % 2), n // 2
                    d_p, d_s = dm[o:o + HD, t, 0:SEQ], dm[o:o + HD, t, SEQ:]
                    pool.tensor_tensor(d_p, dst_p[o:o + HD, t, PAST:], cst["inv_cnt"][o:o + HD, t, :], ALU.mult)
                    d_s3 = d_s.rearrange("p (b n) -> p b n", b=NB)
                    pool.tensor_scalar(d_s3, dst_s[o:o + HD, t, :, PAST:], 1.0 / w, None, ALU.mult)
                    pool.drain()
                    pool.tensor_tensor(d_p, d_p, z[o:o + HD, ZU + t, 0:SEQ], ALU.subtract)
                    ins = pool.tensor_tensor(d_s, d_s, z[o:o + HD, ZU + t, SEQ:], ALU.subtract)
                    src_p, src_s = dst_p, dst_s
                ins.then_inc(pool_d, 1)
                pool.wait_ge(tr_act, 9 * L + 9)
                for h in range(H):
                    if h:
                        pool.wait_ge(vbd_used, H * L + h)
                    pool.tensor_tensor(v_bd[:], vr_tok[0:SMP, 2, h * HD:h * HD + HD].unsqueeze(1).to_broadcast([SMP, NB, HD]),
                                       cst["own_b"][:].unsqueeze(2).to_broadcast([SMP, NB, HD]), ALU.mult).then_inc(vbd_ok, 1)
                with pool.Fori(1, 8) as i:
                    for slot in range(2):
                        load_k(L, i * 2 + slot, slot)
                add_squares(L * 12 + 8)
                add_squares(L * 12 + 12)

        @block.scalar
        def _(act):
            def hi_split(half, slot):
                act.wait_ge(w_landed[slot], half * 16 + 16)
                act.wait_ge(chunk_used, half * 2 + (slot + 1))
                act.activation(w_hi[:, slot, :], w_raw[:, slot, :], ACT.Copy).then_inc(hi_done, 1)

            def ffn_in(L, c0, g0, f):
                with act.Fori(0, FT // 2) as i:
                    half = L * (C_ALL // 2) + i + (c0 // 2 + 1)
                    n = f * (FT // 2) + i + 1
                    hi_split(half, 0)
                    act.wait_ge(evac_done, L * G_ALL + i * 2 + (GROUPS0 + g0 + 1))
                    act.activation(t_sil, t_gate, ACT.Silu).then_inc(silu_ready, 1)
                    hi_split(half, 1)
                    act.wait_ge(a_ready, n)
                    act.activation(act_hi[:, bass.ds(i * 2, 2), :], t_up, ACT.Copy).then_inc(a_hi, 1)

            def gx_pair(dst, norm, o, groups):
                act.wait_ge(evac_done, groups)
                for k in (2 * o, 2 * o + 1):
                    ins = act.activation(dst[:, k, :], x[:, k, :], ACT.Copy, scale=gains[:, bass.ds(norm * KT + k, 1)])
                ins.then_inc(g_hi_done, 1)

            def squares(norm, o):
                if o >= 2:
                    act.wait_ge(ssq_done, norm * 4 + (o - 1))
                act.activation(sq_slot[o % 2], x[:, 2 * o:2 * o + 2, :], ACT.Square).then_inc(sq_done, 1)

            def root(n):
                act.wait_ge(stat_done, n)
                act.activation(rstd[:], ps[:, 4, 0:TOK], ACT.Sqrt, scale=1.0 / D, bias=eps[:, 0:1]).then_inc(std_done, 1)

            def ffn_out(L, c0, g0, norm, dst):
                for g in range(4):
                    for n in range(3):
                        if n == 2:
                            gx_pair(dst, norm, g, L * G_ALL + (GROUPS0 + g0 + g + 1))
                            squares(norm, g)
                        c = 3 * g + n + 2
                        hi_split(L * (C_ALL // 2) + (c0 + c) // 2, c % 2)

            for layer in range(DEPTH):
                for n, name in enumerate(("norm_ffn1", "norm_mix", "norm_ffn2")):
                    r0 = (3 * layer + n) * KT
                    act.dma_start(g_rows[r0:r0 + KT, :], A[name][layer].rearrange("(k p) -> k p", p=P)).then_inc(gain_loaded, 16)
            act.dma_start(g_rows[NORMS * KT - KT:NORMS * KT, :],
                          A["norm_final"].rearrange("(k p) -> k p", p=P)).then_inc(gain_loaded, 16)
            act.dma_start(g_rows[NORMS * KT:NORMS * KT + 4, :],
                          A["pool_scale"].rearrange("l (k p) -> (l k) p", p=P)).then_inc(gain_loaded, 16)
            act.wait_ge(gain_ok, 1)
            for j in range(4):
                gx_pair(h_hi, 0, j, j + 1)
                squares(0, j)
                if j % 2:
                    hi_split(0, j // 2)
            with act.Fori(0, DEPTH) as L:
                half0 = L * (C_ALL // 2)
                norm = L * 3
                root(norm + 1)
                ffn_in(L, C_F1I, G_F1I, L * 2)
                ffn_out(L, C_F1O, G_F1O, norm + 1, h_hi)
                root(norm + 2)
                with act.Fori(0, 5) as i:
                    for slot in range(2):
                        hi_split(half0 + i + (C_MIX // 2 + 1), slot)
                hi_split(half0 + C_WO // 2, 0)

                def tokens(t):
                    n = P if t < 2 else SMP
                    for kind, bank, dst in ((0, 4, ka_tok[0:n, t, :]),
                                            (1, 5, va_tok[:, t, :] if t < 2 else v_own[:, :]),
                                            (3, 7, vr_tok[0:n, t, :])):
                        act.wait_ge(tr_done, 12 * L + (4 * t + kind + 1))
                        act.activation(dst, ps[0:n, bank, 0:HDIM], ACT.Copy).then_inc(tr_act, 1)

                act.wait_ge(u_tr, L + 1)
                act.activation(u_tok[:, 0, :], ps[:, 3, 0:POOL], ACT.Copy).then_inc(u_out, 1)
                act.activation(u_tok[0:SMP, 1, :], ps[0:SMP, 3, POOL:2 * POOL], ACT.Copy).then_inc(u_out, 1)
                tokens(0)
                tokens(1)
                act.wait_ge(evac_done, L * G_ALL + (GROUPS0 + G_MIX + 12))
                act.activation(z[:, ZG:ZG + 3, :], z[:, ZG:ZG + 3, :], ACT.Silu).then_inc(g_silu, 1)
                act.activation(k_own_hi[:], z[:, ZKA:ZKA + 3, SEQ:], ACT.Copy).then_inc(kown_hi_s, 1)
                tokens(2)

                def exp(h):
                    s = h % 2
                    act.wait_ge(s_max, H * L + (h + 1))
                    act.activation(s_p[:, s, 0:256], s_p[:, s, 0:256], ACT.Exp, scale=ATT_SCALE, bias=st[:, 0 + 2 * s:1 + 2 * s],
                                   accum_out=st[:, 4 + 2 * s:5 + 2 * s])
                    act.activation(s_p[:, s, 256:384], s_p[:, s, 256:384], ACT.Exp, scale=ATT_SCALE, bias=st[:, 1 + 2 * s:2 + 2 * s],
                                   accum_out=st[:, 5 + 2 * s:6 + 2 * s]).then_inc(s_exp, 1)

                def att_hi(f):
                    act.wait_ge(oa_done, 3 * L + (f + 1))
                    act.activation(h_hi[:, 2 + f, 0:SEQ], ps[:, 4, 0:SEQ], ACT.Copy).then_inc(oa_hi, 1)

                exp(0)
                for h in range(H):
                    f, s = h // 2, h % 2
                    if h + 1 < H:
                        exp(h + 1)
                    if h == 0:
                        hi_split(half0 + C_WO // 2, 1)
                    act.wait_ge(pt_done, H * L + (h + 1))
                    act.activation(pt_p[:, s, :], ps[:, 2 + s, 0:384], ACT.Copy).then_inc(pt_evac, 1)
                    if s:
                        act.wait_ge(o_gated, 3 * L + (f + 1))
                        act.activation(o_sq[:, f, :], ps[:, 7, 0:TOK], ACT.Square).then_inc(o_sqd, 1)
                    elif f:
                        att_hi(f - 1)
                act.wait_ge(sp_done, L + 1)
                act.activation(sp_new[:], ps[:, 7, 320:512].rearrange("p (f v) -> p f v", f=3), ACT.Copy).then_inc(st_prm, 1)
                for t in range(2):
                    act.wait_ge(pool_mm, 2 * L + (t + 1))
                    act.activation(h_hi[:, t, :], ps[:, (5, 0)[t], 0:TOK], ACT.Copy, scale=gains[:, bass.ds(L * 2 + (NORMS * KT + t), 1)]).then_inc(pool_hi, 1)
                att_hi(2)
                for f in range(3):
                    act.wait_ge(mean_done, 3 * L + (f + 1))
                    act.activation(o_sq[:, f, :], ps[:, 1 + f, 0:TOK], ACT.Sqrt, bias=eps[:, 0:1]).then_inc(o_std, 1)

                def or_high(f):
                    act.wait_ge(or_ready, 3 * L + (f + 1))
                    act.activation(h_hi[:, 5 + f, :], z[:, ZG + f, :], ACT.Copy).then_inc(or_hi, 1)

                def qprep(p):
                    for half in range(2):
                        for bb in range(2):
                            ins = act.activation(
                                q_hi[HD * half:HD * half + HD, :].rearrange("p (f c) -> p f c", f=3)[:, :, 8 * half + 96 * bb:8 * half + 96 * bb + 8],
                                q_smp[HD * half:HD * half + HD, :, bass.ds(p * 16 + 8 * bb, 8)], ACT.Copy)
                    ins.then_inc(qp_hi, 1)

                def kt_evac(p, i):
                    act.wait_ge(sc_done, L * 16 + p * 4 + (i + 1))
                    for f in range(3):
                        act.wait_ge(kt_tr, L * 48 + p * 12 + (3 * i + f + 1))
                        act.activation(kt_hi[:, i % 2, f, :], ps[:, 4 + f, :], ACT.Copy).then_inc(kt_hi_s, 1)

                def exps(p):
                    act.wait_ge(sm_bias, L * 4 + p + 1)
                    for n in range(5):
                        a, b = (256 * n, 256 * n + 256) if n < 4 else (PAST_LEN, PAST_LEN + SMP)
                        ins = act.activation(sp[:, a:b], sp[:, a:b], ACT.Exp, bias=ss[:, 32 + n:33 + n],
                                             accum_out=ss[:, 40 + n:41 + n])
                    ins.then_inc(sm_exp, 1)

                def probs_evac(p):
                    act.wait_ge(pt2_done, L * 8 + p * 2 + 2)
                    act.activation(pt_s[:, 0:5, :], ps[:, 3, 0:480].rearrange("p (n c) -> p n c", c=96), ACT.Copy).then_inc(pt2_evac, 1)
                    act.wait_ge(pt2_done, L * 8 + p * 2 + 3)
                    act.activation(pt_s[:, 5:8, :], ps[:, 2, 0:288].rearrange("p (n c) -> p n c", c=96), ACT.Copy)
                    act.activation(pt_s[0:SMP, 8, :], ps[0:SMP, 2, 288:384], ACT.Copy).then_inc(pt2_evac, 1)

                def out_evac(p, bb):
                    act.wait_ge(pv_done, L * NB + p * 2 + (bb + 1))
                    act.activation(o_tok[:, bb, :], ps[0:48, (7, 3)[bb], 0:HDIM], ACT.Copy).then_inc(o_evac, 1)

                def y_high(p):
                    act.wait_ge(ot_done, L * 4 + p + 1)
                    for half in range(2):
                        ins = act.activation(y_smp(h_hi, half, p), o_smp(half), ACT.Copy)
                    ins.then_inc(ys_hi, 1)

                act.wait_ge(stored_kv, L * (16 * KV_STORES) + 16 * KV_STORES)
                act.wait_ge(kown_ok, L + 1)

                qprep(0)
                kt_evac(0, 0)
                for i in range(1, 4):
                    kt_evac(0, i)
                or_high(0)

                def body(p, first):
                    act.wait_ge(own_done, L * 4 + p)
                    qprep(p)
                    kt_evac(p, 0)
                    if not first:
                        out_evac(p - 2, 1)
                    kt_evac(p, 1)
                    exps(p - 1)
                    if not first:
                        y_high(p - 2)
                    kt_evac(p, 2)
                    probs_evac(p - 1)
                    kt_evac(p, 3)
                    out_evac(p - 1, 0)
                body(1, True)
                or_high(1)
                or_high(2)
                with act.Fori(2, 4) as p:
                    body(p, False)
                exps(3)
                out_evac(2, 1)
                y_high(2)
                probs_evac(3)
                out_evac(3, 0)
                out_evac(3, 1)
                y_high(3)

                for g in range(4):
                    gx_pair(g_hi, norm + 2, g, L * G_ALL + (GROUPS0 + G_WO + 1 + g))
                    squares(norm + 2, g)
                    hi_split(half0 + (C_WO // 2 + 1 + g // 2), g % 2)
                root(norm + 3)
                ffn_in(L, C_F2I, G_F2I, L * 2 + 1)
                ffn_out(L, C_F2O, G_F2O, norm + 3, h_hi)
            act.wait_ge(evac_done, GROUPS0 + DEPTH * G_ALL)
            for k in range(KT // 2):
                c = (NORMS - 1) * KT + k
                ins = act.activation(y_fin[:, k, :], x[:, k, :], ACT.Copy, scale=gains[:, c:c + 1])
            ins.then_inc(y_fin_act, 1)
            act.wait_ge(stat_done, NORMS)
            act.activation(rstd_tok[:, 0:2], ps[:, 6, 0:2], ACT.Sqrt, scale=1.0 / D, bias=eps[:, 0:1])
            act.activation(rstd_tok[0:SMP, 2:3], ps[0:SMP, 6, 2:3], ACT.Sqrt, scale=1.0 / D, bias=eps[0:SMP, 0:1]).then_inc(std_done, 1)
            act.wait_ge(rstd_ok, 1)
            for t in range(3):
                n = P if t < 2 else SMP
                act.wait_ge(y_tr, t + 1)
                act.activation(y_tok[0:n, t, 0:512], ps[0:n, 2 * t, :], ACT.Copy, scale=rstd_tok[0:n, t:t + 1]).then_inc(y_tok_act, 1)

        @block.vector
        def _(dve):
            def lo_split(half, slot):
                dve.wait_ge(hi_done, half * 2 + (slot + 1))
                dve.tensor_tensor(w_lo[:, slot, :], w_raw[:, slot, :], w_hi[:, slot, :].bitcast(F32),
                                  ALU.subtract).then_inc(split_done, 1)

            def gx_pair(hi, lo, norm, o):
                dve.wait_ge(g_hi_done, norm * 4 + (o + 1))
                for k in (2 * o, 2 * o + 1):
                    ins = dve.scalar_tensor_tensor(out=lo[:, k, :], in0=x[:, k, :], scalar=gains[:, bass.ds(norm * KT + k, 1)],
                                                   in1=hi[:, k, :].bitcast(F32), op0=ALU.mult, op1=ALU.subtract)
                ins.then_inc(gx_ready, 1)

            def invert(n):
                dve.wait_ge(std_done, n)
                dve.reciprocal(rstd[:], rstd[:])
                dve.drain()

            def ffn_in(L, c0, g0, f):
                with dve.Fori(0, FT // 2) as i:
                    half = L * (C_ALL // 2) + i + (c0 // 2 + 1)
                    n = f * (FT // 2) + i + 1
                    dve.wait_ge(chunk_used, L * C_ALL + i * 2 + (c0 + 3))
                    dve.tensor_tensor(t_gate, ps[:, 0:2, 0:TOK], bc2(rstd[:]), ALU.mult).then_inc(evac_done, 1)
                    lo_split(half, 0)
                    dve.drain()
                    dve.wait_ge(chunk_used, L * C_ALL + i * 2 + (c0 + 4))
                    dve.tensor_tensor(t_up, ps[:, 2:4, 0:TOK], bc2(rstd[:]), ALU.mult).then_inc(evac_done, 1)
                    dve.drain()
                    dve.wait_ge(silu_ready, n)
                    dve.tensor_tensor(t_up, t_up, t_sil, ALU.mult).then_inc(a_ready, 1)
                    lo_split(half, 1)
                    dve.wait_ge(a_hi, n)
                    dve.tensor_tensor(act_lo[:, bass.ds(i * 2, 2), :], t_up, act_hi[:, bass.ds(i * 2, 2), :].bitcast(F32),
                                      ALU.subtract).then_inc(act_ready, 1)

            def add_to_x(L, g, chunks, scale):
                dve.wait_ge(chunk_used, L * C_ALL + (chunks + 2))
                b = 2 * (g % 2)
                dve.scalar_tensor_tensor(out=x[:, 2 * g:2 * g + 2, :], in0=ps[:, b:b + 2, 0:TOK], scalar=scale,
                                         in1=x[:, 2 * g:2 * g + 2, :], op0=ALU.mult, op1=ALU.add).then_inc(evac_done, 1)
                dve.drain()

            def ffn_out(L, c0, norm):
                for g in range(4):
                    for n in range(3):
                        if n == 2:
                            add_to_x(L, g, c0 + 3 * g + 3, 0.5)
                            gx_pair(h_hi, h_lo, norm, g)
                        c = 3 * g + n + 2
                        lo_split(L * (C_ALL // 2) + (c0 + c) // 2, c % 2)

            dve.memset(ones[:], 1.0).then_inc(prep, 1)
            dve.memset(eps[:], EPS).then_inc(prep, 1)
            dve.memset(ss[:], 0.0).then_inc(prep, 1)
            dve.sem_inc(split_done, 2)
            dve.sem_inc(kt_ok, 3)
            for j in range(4):
                if j == 0:
                    dve.wait_ge(gain_tr, 1)
                    dve.tensor_copy(gains[:], ps[:, 4, 0:NORMS * KT + 4]).then_inc(gain_ok, 1)
                dve.wait_ge(x_tr, j + 1)
                b = 2 * (j % 2)
                dve.tensor_copy(x[:, 2 * j:2 * j + 2, :], ps[:, b:b + 2, 0:TOK]).then_inc(evac_done, 1)
                dve.drain()
                gx_pair(h_hi, h_lo, 0, j)
                if j % 2:
                    lo_split(0, j // 2)
            with dve.Fori(0, DEPTH) as L:
                half0 = L * (C_ALL // 2)
                norm = L * 3
                invert(norm + 1)
                ffn_in(L, C_F1I, G_F1I, L * 2)
                ffn_out(L, C_F1O, norm + 1)
                invert(norm + 2)
                with dve.Fori(0, 5) as i:
                    for slot in range(2):
                        dve.wait_ge(chunk_used, L * C_ALL + i * 2 + (C_MIX + slot + 3))
                        dve.tensor_tensor(z[:, bass.ds(i * 4 + 2 * slot, 2), :], ps[:, 2 * slot:2 * slot + 2, 0:TOK],
                                          bc2(rstd[:]), ALU.mult).then_inc(evac_done, 1)
                        lo_split(half0 + i + (C_MIX // 2 + 1), slot)

                dve.wait_ge(loaded, 16 * len(C))

                def k_tokens(t):
                    n = P if t < 2 else SMP
                    dve.wait_ge(tr_done, 12 * L + (4 * t + 3))
                    dve.tensor_tensor(kr_tok[0:n, t, :].rearrange("p (h d) -> p h d", h=H),
                                      ps[0:n, 6, 0:HDIM].rearrange("p (h d) -> p h d", h=H),
                                      cst["k_decay"][0:n, t, :].unsqueeze(2).to_broadcast([n, H, HD]), ALU.mult).then_inc(tr_dve, 1)

                dve.wait_ge(chunk_used, L * C_ALL + (C_MIX + 13))
                dve.tensor_tensor(z[:, 20:22, :], ps[:, 0:2, 0:TOK], bc2(rstd[:]), ALU.mult).then_inc(evac_done, 1)
                lo_split(half0 + (C_WO // 2), 0)
                k_tokens(0)
                dve.wait_ge(chunk_used, L * C_ALL + (C_MIX + 14))
                dve.tensor_tensor(z[:, 22, :], ps[:, 2, 0:TOK], rstd[:], ALU.mult).then_inc(evac_done, 1)
                dve.drain()

                es = ext[:, 542:910].rearrange("p (t b n) -> p t b n", t=2, b=NB)
                k_tokens(1)
                dve.wait_ge(pre_tr, L + 1)
                for t in range(2):
                    ins = dve.tensor_copy(es[:, t, :, 0:PAST], ps[:, 1, 120 * t:120 * t + 120].rearrange("p (b n) -> p b n", b=NB))
                ins.then_inc(pre_in, 1)
                dve.tensor_copy(q_smp[:], z[:, ZQA:ZQA + 3, SEQ:])
                dve.tensor_tensor(q_dec[:], z[:, ZQR:ZQR + 3, SEQ:], cst["q_decay"][:], ALU.mult).then_inc(q_dec_ok, 1)
                dve.wait_ge(kown_hi_s, L + 1)
                dve.tensor_tensor(k_own_lo[:], z[:, ZKA:ZKA + 3, SEQ:], k_own_hi[:].bitcast(F32), ALU.subtract).then_inc(kown_ok, 1)
                k_tokens(2)

                def smax(h):
                    s = h % 2
                    dve.wait_ge(s_done, H * L + (h + 1))
                    if h >= 2:
                        dve.wait_ge(pt_done, H * L + (h - 1))
                    dve.scalar_tensor_tensor(out=s_p[:, s, :], in0=cst["dist_p"][:], scalar=-SLOPES[h] / ATT_SCALE,
                                             in1=ps[:, s, 0:384], op0=ALU.mult, op1=ALU.add)
                    dve.drain()
                    dve.tensor_reduce(st[:, 8:9], s_p[:, s, 0:256], AX, ALU.max)
                    dve.tensor_reduce(st[:, 9:10], s_p[:, s, 256:384], AX, ALU.max)
                    dve.drain()
                    dve.tensor_scalar(st[:, 2 * s:2 * s + 2], st[:, 8:10], -ATT_SCALE, None, ALU.mult).then_inc(s_max, 1)

                def decay_mask(h):
                    dve.wait_ge(r_done, H * L + (h + 1))
                    p, s = att_p[h % 2], att_s[h % 2]
                    dve.tensor_tensor(p[:, 0:256], ps[:, 5, 0:256], cst["decay_p"][:, h, :], ALU.mult)
                    dve.tensor_tensor(p[:, 256:384], ps[:, 5, 256:384], cst["decay_p"][:, h, 0:P], ALU.mult)
                    dve.tensor_tensor(s[:], ps[0:SMP, 5, 384:448], cst["decay_s"][:, h, :], ALU.mult).then_inc(r_mask, 1)

                def normalise(h):
                    s = h % 2
                    dve.wait_ge(s_exp, H * L + (h + 1))
                    dve.reciprocal(st[:, 12:14], st[:, 4 + 2 * s:6 + 2 * s])
                    dve.drain()
                    dve.tensor_scalar(s_p[:, s, 0:256], s_p[:, s, 0:256], st[:, 12:13], None, ALU.mult)
                    dve.tensor_scalar(s_p[:, s, 256:384], s_p[:, s, 256:384], st[:, 13:14], None, ALU.mult).then_inc(p_norm, 1)

                def gate(f):
                    dve.wait_ge(or_done, 3 * L + (f + 1))
                    dve.tensor_tensor(z[:, ZG + f, :], ps[:, 7, 0:TOK], z[:, ZG + f, :], ALU.mult).then_inc(o_gated, 1)

                def att_lo(f):
                    dve.wait_ge(oa_hi, 3 * L + (f + 1))
                    dve.tensor_tensor(h_lo[:, 2 + f, 0:SEQ], ps[:, 4, 0:SEQ], h_hi[:, 2 + f, 0:SEQ].bitcast(F32),
                                      ALU.subtract).then_inc(y_ready, 1)

                def new_state(f):
                    dve.wait_ge(vbd_used, H * L + (2 * f + 2))
                    dve.scalar_tensor_tensor(out=s0[:, f, :, :].rearrange("p b v -> p (b v)"),
                                             in0=s0[:, f, :, :].rearrange("p b v -> p (b v)"), scalar=cst["c_decay"][:, f:f + 1],
                                             in1=ps[:, 6, :], op0=ALU.mult, op1=ALU.add).then_inc(st_smp, 1)

                smax(0)
                decay_mask(0)
                for h in range(H):
                    f = h // 2
                    normalise(h)
                    if h + 1 < H:
                        dve.drain()
                        smax(h + 1)
                        decay_mask(h + 1)
                    if h == 0:
                        lo_split(half0 + (C_WO // 2), 1)
                        dve.wait_ge(g_silu, L + 1)
                    if h % 2:
                        gate(f)
                        if f:
                            new_state(f - 1)
                    elif f:
                        att_lo(f - 1)
                for t in range(2):
                    dve.wait_ge(pool_hi, 2 * L + (t + 1))
                    dve.scalar_tensor_tensor(out=h_lo[:, t, :], in0=ps[:, (5, 0)[t], 0:TOK],
                                             scalar=gains[:, bass.ds(L * 2 + (NORMS * KT + t), 1)],
                                             in1=h_hi[:, t, :].bitcast(F32), op0=ALU.mult, op1=ALU.subtract).then_inc(y_ready, 1)
                att_lo(2)
                new_state(2)

                def or_norm(f):
                    dve.wait_ge(o_std, 3 * L + (f + 1))
                    dve.reciprocal(o_sq[:, f, :], o_sq[:, f, :])
                    dve.drain()
                    dve.tensor_tensor(z[:, ZG + f, :], z[:, ZG + f, :], o_sq[:, f, :], ALU.mult).then_inc(or_ready, 1)

                def or_lo(f):
                    dve.wait_ge(or_hi, 3 * L + (f + 1))
                    dve.tensor_tensor(h_lo[:, 5 + f, :], z[:, ZG + f, :], h_hi[:, 5 + f, :].bitcast(F32),
                                      ALU.subtract).then_inc(y_ready, 1)

                def qprep(p):
                    dve.wait_ge(qp_hi, L * 4 + p + 1)
                    for half in range(2):
                        o = HD * half
                        for bb in range(2):
                            c = 8 * half + 96 * bb
                            ins = dve.tensor_tensor(q_lo[o:o + HD, :].rearrange("p (f c) -> p f c", f=3)[:, :, c:c + 8],
                                                    q_smp[o:o + HD, :, bass.ds(p * 16 + 8 * bb, 8)],
                                                    q_hi[o:o + HD, :].rearrange("p (f c) -> p f c", f=3)[:, :, c:c + 8].bitcast(F32),
                                                    ALU.subtract)
                    ins.then_inc(qp_ok, 1)

                def kt_rest(p, i):
                    for f in range(3):
                        dve.wait_ge(kt_hi_s, L * 48 + p * 12 + (3 * i + f + 1))
                        dve.tensor_tensor(kt_lo[:, i % 2, f, :], ps[:, 4 + f, :], kt_hi[:, i % 2, f, :].bitcast(F32),
                                          ALU.subtract).then_inc(kt_ok, 1)

                def soft_in(p):
                    R = slice(0, 96)
                    dve.wait_ge(own_done, L * 4 + p + 1)
                    dve.wait_ge(pt2_done, L * 8 + p * 2 + 1)
                    for c in range(2):
                        dve.tensor_reduce(ss[:, 2 * c:2 * c + 2], ps[R, c, :].rearrange("p (a n) -> p a n", a=2), AX, ALU.add)
                        dve.scalar_tensor_tensor(out=sp[:, 512 * c:512 * c + 512], in0=ps[R, c, :], scalar=ATT_SCALE,
                                                 in1=cst["alibi_s"][:, 512 * c:512 * c + 512], op0=ALU.mult, op1=ALU.add)
                    dve.scalar_tensor_tensor(out=sp[:, PAST_LEN:], in0=ps[R, 2, 0:SMP], scalar=ATT_SCALE,
                                             in1=cst["alibi_own"][:, bass.ds(p, 1), :].rearrange("p a n -> p (a n)"),
                                             op0=ALU.mult, op1=ALU.add).then_inc(sm_in, 1)
                    dve.drain()

                def soft_bias():
                    dve.tensor_reduce(ss[:, 5:6], ss[:, 0:4], AX, ALU.min)
                    dve.tensor_reduce(ss[:, 25:29], sp[:, 0:PAST_LEN].rearrange("p (a n) -> p a n", a=4), AX, ALU.max)
                    dve.tensor_reduce(ss[:, 29:30], sp[:, PAST_LEN:], AX, ALU.max)
                    dve.drain()
                    dve.tensor_scalar(ss[:, 8:12], ss[:, 0:4], ss[:, 5:6], None, ALU.is_le)
                    dve.drain()
                    dve.tensor_tensor(ss[:, 12:16], ss[:, 8:12], cst["rank"][:], ALU.mult)
                    dve.drain()
                    dve.tensor_reduce(ss[:, 16:17], ss[:, 12:16], AX, ALU.max)
                    dve.drain()
                    dve.tensor_scalar(ss[:, 20:24], ss[:, 12:16], ss[:, 16:17], -BIG, ALU.is_equal, ALU.mult)
                    dve.drain()
                    dve.tensor_tensor(ss[:, 25:30], ss[:, 25:30], ss[:, 20:25], ALU.add)
                    dve.drain()
                    dve.tensor_reduce(ss[:, 30:31], ss[:, 25:30], AX, ALU.max)
                    dve.drain()
                    dve.tensor_scalar(ss[:, 32:37], ss[:, 20:25], ss[:, 30:31], None, ALU.subtract).then_inc(sm_bias, 1)

                def soft_b(p):
                    dve.wait_ge(sm_exp, L * 4 + p + 1)
                    dve.tensor_reduce(ss[:, 45:46], ss[:, 40:45], AX, ALU.add)
                    dve.drain()
                    dve.reciprocal(ss[:, 46:47], ss[:, 45:46])
                    dve.drain()
                    dve.tensor_scalar(sp[:], sp[:], ss[:, 46:47], None, ALU.mult).then_inc(sm_ok, 1)

                def y_rest(p):
                    dve.wait_ge(ys_hi, L * 4 + p + 1)
                    for half in range(2):
                        ins = dve.tensor_tensor(y_smp(h_lo, half, p), o_smp(half), y_smp(h_hi, half, p).bitcast(F32), ALU.subtract)
                    ins.then_inc(y_ready, 1)

                qprep(0)
                kt_rest(0, 0)
                kt_rest(0, 1)
                or_norm(0)
                kt_rest(0, 2)
                kt_rest(0, 3)

                def body(p, first):
                    soft_in(p - 1)
                    qprep(p)
                    kt_rest(p, 0)
                    soft_bias()
                    kt_rest(p, 1)
                    soft_b(p - 1)
                    kt_rest(p, 2)
                    if not first:
                        y_rest(p - 2)
                    kt_rest(p, 3)
                body(1, True)
                or_norm(1)
                or_norm(2)
                for f in range(3):
                    or_lo(f)
                with dve.Fori(2, 4) as p:
                    body(p, False)
                soft_in(3)
                soft_bias()
                soft_b(3)
                y_rest(2)
                y_rest(3)

                for g in range(4):
                    add_to_x(L, g, C_WO + g + 1, 1.0)
                    gx_pair(g_hi, g_lo, norm + 2, g)
                    lo_split(half0 + (C_WO // 2 + 1 + g // 2), g % 2)
                invert(norm + 3)
                ffn_in(L, C_F2I, G_F2I, L * 2 + 1)
                ffn_out(L, C_F2O, norm + 3)
            for k in range(KT // 2, KT):
                c = (NORMS - 1) * KT + k
                ins = dve.tensor_scalar(y_fin[:, k, :], x[:, k, :], gains[:, c:c + 1], None, ALU.mult)
            ins.then_inc(y_fin_dve, 1)
            dve.wait_ge(std_done, NORMS)
            dve.reciprocal(rstd_tok[:, 0:2], rstd_tok[:, 0:2])
            dve.reciprocal(rstd_tok[0:SMP, 2:3], rstd_tok[0:SMP, 2:3]).then_inc(rstd_ok, 1)
            dve.drain()
            for t in range(3):
                n = P if t < 2 else SMP
                dve.wait_ge(y_tr, t + 1)
                dve.tensor_scalar(y_tok[0:n, t, 512:D], ps[0:n, 2 * t + 1, :], rstd_tok[0:n, t:t + 1], None, ALU.mult).then_inc(y_tok_dve, 1)

        @block.tensor
        def _(pe):
            def products(slot, nk, cols, k0, k_all, hi, lo, bank, ready=None):
                for a in range(cols):
                    for kk in range(nk):
                        k = k0 + kk
                        if a == 0 and ready and kk in ready:
                            pe.wait_ge(*ready[kk])
                        w = slice((kk * cols + a) * P, (kk * cols + a + 1) * P)
                        out = ps[:, bank + a, 0:TOK]
                        pe.matmul(out, w_hi[:, slot, w], hi[:, k, :], start=(k == 0), stop=False)
                        pe.matmul(out, w_hi[:, slot, w], lo[:, k, :], start=False, stop=False)
                        ins = pe.matmul(out, w_lo[:, slot, w], hi[:, k, :], start=False, stop=(k == k_all - 1))
                ins.then_inc(chunk_used, 1)

            def chunk_split(half, slot):
                pe.wait_ge(split_done, half * 2 + (slot + 3))

            def banks_free(L, g):
                pe.wait_ge(evac_done, L * G_ALL + (GROUPS0 - 1) + g)

            def sum_squares(n):
                pe.wait_ge(ssq_done, n * 4)
                pe.matmul(ps[:, 4, 0:TOK], ones[:], ssq[:, 0, :], start=True, stop=False)
                pe.matmul(ps[:, 4, 0:TOK], ones[:], ssq[:, 1, :], start=False, stop=True).then_inc(stat_done, 1)

            def square_group(L, half, g, slot, hi, lo, ready, cols=2):
                chunk_split(half, slot)
                banks_free(L, g)
                products(slot, KT, cols, 0, KT, hi, lo, 2 * slot, ready)

            def gx(norm):
                return {2 * o: (gx_ready, norm * 4 + (o + 1)) for o in range(4)}

            def ffn_in(L, c0, g0, norm, hi, lo):
                half = L * (C_ALL // 2) + c0 // 2
                square_group(L, half, g0, 0, hi, lo, gx(norm))
                sum_squares(norm + 1)
                square_group(L, half, g0 + 1, 1, hi, lo, None)
                with pe.Fori(1, FT // 2) as i:
                    for slot in range(2):
                        square_group(L, half + i, i * 2 + (g0 + slot), slot, hi, lo, None)

            def ffn_out(L, c0, g0, f):
                with pe.Fori(0, 2) as i:
                    for g in range(2):
                        for n, (a, b) in enumerate(OUT_K):
                            c = 3 * g + n
                            chunk_split(L * (C_ALL // 2) + i * 3 + (c0 + c) // 2, c % 2)
                            pe.wait_ge(act_ready, f * (FT // 2) + (b + 1) // 2)
                            if n == 0:
                                banks_free(L, i * 2 + (g0 + g))
                            products(c % 2, b - a, 2, a, FT, act_hi, act_lo, 2 * g)

            for s, n in ((chunk_used, 2), (sc_done, 2), (pt2_done, 1)):
                pe.sem_inc(s, n)
            pe.wait_ge(x_loaded, 16 * 4)
            for j in range(4):
                if j == 1:
                    pe.wait_ge(gain_loaded, 16 * GAIN_LOADS)
                    pe.transpose(ps[:, 4, 0:NORMS * KT + 4], g_rows[:], ident[0:NORMS * KT + 4, 0:NORMS * KT + 4]).then_inc(gain_tr, 1)
                if j >= 2:
                    pe.wait_ge(evac_done, j - 1)
                for a in range(2):
                    k = 2 * j + a
                    for t in range(3):
                        n = P if t < 2 else SMP
                        ins = pe.transpose(ps[:, 2 * (j % 2) + a, t * P:t * P + n], x_tok[0:n, t, k * P:k * P + P], ident[0:n, 0:n])
                ins.then_inc(x_tr, 1)
            pe.wait_ge(prep, 6)
            with pe.Fori(0, DEPTH) as L:
                half0 = L * (C_ALL // 2)
                norm = L * 3
                ffn_in(L, C_F1I, G_F1I, norm, h_hi, h_lo)
                ffn_out(L, C_F1O, G_F1O, L * 2)
                square_group(L, half0 + C_MIX // 2, G_MIX, 0, h_hi, h_lo, gx(norm + 1))
                sum_squares(norm + 2)
                square_group(L, half0 + C_MIX // 2, G_MIX + 1, 1, h_hi, h_lo, None)
                with pe.Fori(1, 5) as i:
                    for slot in range(2):
                        square_group(L, half0 + i + C_MIX // 2, i * 2 + (G_MIX + slot), slot, h_hi, h_lo, None)
                square_group(L, half0 + (C_MIX // 2 + 5), G_MIX + 10, 0, h_hi, h_lo, None)

                def tokens(t):
                    n = P if t < 2 else SMP
                    if t:
                        wait_apart(pe, tr_act, 9 * L + 3 * t)
                        wait_apart(pe, tr_dve, 3 * L + t)
                    for kind, zt in enumerate((ZKA, ZVA, ZKR, ZVR)):
                        for f in range(3):
                            ins = pe.transpose(ps[0:n, 4 + kind, P * f:P * f + P], z[:, zt + f, P * t:P * t + n], ident[:])
                        ins.then_inc(tr_done, 1)

                pe.wait_ge(evac_done, L * G_ALL + (GROUPS0 + G_MIX + 10))
                for t in range(2):
                    pe.transpose(ps[:, 3, P * t:P * t + P], z[:, ZU + t, P:2 * P], ident[:])
                for t in range(2):
                    ins = pe.transpose(ps[0:SMP, 3, POOL + P * t:POOL + P * t + P], z[:, ZU + t, SEQ:], ident[:])
                ins.then_inc(u_tr, 1)
                tokens(0)
                square_group(L, half0 + (C_MIX // 2 + 5), G_MIX + 11, 1, h_hi, h_lo, None, cols=1)

                tokens(1)
                pe.wait_ge(evac_done, L * G_ALL + (GROUPS0 + G_MIX + 12))
                pe.wait_ge(aux_loaded, L * (16 * AUX_LOADS) + 16 * AUX_LOADS)
                for t in range(2):
                    ins = pe.transpose(ps[:, 1, 120 * t:120 * t + 120], pre_tok[:, P * t:P * t + P], ident[0:120, 0:120])
                ins.then_inc(pre_tr, 1)
                tokens(2)

                def scores(h):
                    f, o, s = h // 2, HD * (h % 2), h % 2
                    if h >= 2:
                        wait_apart(pe, s_max, H * L + (h - 1))
                    q, k = z[o:o + HD, ZQA + f, :], z[o:o + HD, ZKA + f, :]
                    pe.matmul(ps[:, s, 0:256], q[:, P:2 * P], k[:, 0:SEQ], start=True, stop=True)
                    pe.matmul(ps[:, s, 256:384], q[:, 0:P], k[:, 0:P], start=True, stop=True).then_inc(s_done, 1)

                def ret_scores(h):
                    f, o = h // 2, HD * (h % 2)
                    if h:
                        wait_apart(pe, r_mask, H * L + h)
                    q, k = z[o:o + HD, ZQR + f, :], z[o:o + HD, ZKR + f, :]
                    pe.matmul(ps[:, 5, 0:256], k[:, 0:P], q[:, 0:SEQ], start=True, stop=True)
                    pe.matmul(ps[:, 5, 256:384], k[:, P:2 * P], q[:, P:2 * P], start=True, stop=True)
                    pe.matmul(ps[0:SMP, 5, 384:448], k[:, SEQ:], q[:, SEQ:], start=True, stop=True).then_inc(r_done, 1)

                def ret_out(h):
                    f, o, c = h // 2, HD * (h % 2), slice(h * HD, h * HD + HD)
                    pe.wait_ge(r_mask, H * L + (h + 1))
                    if h % 2 == 0 and f:
                        pe.wait_ge(o_sqd, 3 * L + f)
                    for t in range(2):
                        ins = pe.matmul(ps[o:o + HD, 7, TOK + HD * f:TOK + HD * f + HD], kr_tok[:, t, c], vr_tok[:, t, c],
                                        start=(t == 0), stop=(t == 1))
                    if h == H - 1:
                        ins.then_inc(sp_done, 1)
                    probs = att_p[h % 2]
                    pe.matmul(ps[o:o + HD, 7, 0:256], vr_tok[:, 0, c], probs[:, 0:256], start=True, stop=False)
                    pe.matmul(ps[o:o + HD, 7, 128:256], vr_tok[:, 1, c], probs[:, 256:384], start=False, stop=True)
                    pe.matmul(ps[o:o + HD, 7, 256:320], vr_tok[0:SMP, 2, c], att_s[h % 2][:], start=True, stop=False).then_inc(or_own, 1)
                    wait_apart(pe, or_own, H * L + (h + 1))
                    for b in range(NB):
                        ins = pe.matmul(ps[o:o + HD, 7, 256 + 8 * b:264 + 8 * b], s0[o:o + HD, f, b, :],
                                        q_dec[o:o + HD, f, 8 * b:8 * b + 8], start=False, stop=(b == NB - 1))
                    if h % 2:
                        ins.then_inc(or_done, 1)

                def transpose_p(h):
                    s = h % 2
                    pe.wait_ge(p_norm, H * L + (h + 1))
                    if h >= 2:
                        pe.wait_ge(pt_evac, H * L + (h - 1))
                    for n, c in enumerate((256, 0, 128)):
                        ins = pe.transpose(ps[:, 2 + s, P * n:P * n + P], s_p[:, s, c:c + P], ident[:])
                    ins.then_inc(pt_done, 1)

                def att_out(h):
                    f, o, s, c = h // 2, HD * (h % 2), h % 2, slice(h * HD, h * HD + HD)
                    pe.wait_ge(pt_evac, H * L + (h + 1))
                    if s == 0 and f:
                        pe.wait_ge(y_ready, 12 * L + f)
                    pe.matmul(ps[o:o + HD, 4, 0:256], va_tok[:, 0, c], pt_p[:, s, 0:256], start=True, stop=False)
                    ins = pe.matmul(ps[o:o + HD, 4, 128:256], va_tok[:, 1, c], pt_p[:, s, 256:384], start=False, stop=True)
                    if s:
                        ins.then_inc(oa_done, 1)

                scores(0)
                pe.wait_ge(tr_act, 9 * L + 9)
                pe.wait_ge(tr_dve, 3 * L + 3)
                pe.wait_ge(q_dec_ok, L + 1)
                pe.wait_ge(u_out, 2 * L + 2)
                pe.wait_ge(pre_in, L + 1)
                ret_scores(0)

                def smp_state(h):
                    f, o, c = h // 2, HD * (h % 2), slice(h * HD, h * HD + HD)
                    wait_apart(pe, vbd_ok, H * L + (h + 1))
                    if h % 2 == 0 and f:
                        wait_apart(pe, st_smp, 3 * L + f)
                    pe.matmul(ps[o:o + HD, 6, :], kr_tok[0:SMP, 2, c], v_bd[:].rearrange("p b v -> p (b v)"),
                              start=True, stop=True).then_inc(vbd_used, 1)

                for h in range(H):
                    if h + 1 < H:
                        scores(h + 1)
                        ret_scores(h + 1)
                    ret_out(h)
                    transpose_p(h)
                    if h > 1:
                        smp_state(h - 2)
                    if h:
                        att_out(h - 1)
                pe.wait_ge(pool_d, L + 1)
                pe.wait_ge(s_max, H * L + (H - 1))
                pe.wait_ge(r_mask, H * L + H)
                for t in range(2):
                    pe.matmul(ps[:, (5, 0)[t], 0:TOK], wbd[:, t, :], tmp[:, 1820 + TOK * t:1820 + TOK * t + TOK],
                              start=True, stop=True).then_inc(pool_mm, 1)
                smp_state(H - 2)
                att_out(H - 1)
                smp_state(H - 1)
                pe.wait_ge(o_sqd, 3 * L + 3)
                pe.wait_ge(pt_evac, H * L + H)
                for f in range(3):
                    pe.matmul(ps[:, 1 + f, 0:TOK], head_mean[:], o_sq[:, f, :], start=True, stop=True).then_inc(mean_done, 1)

                def transpose_k(p, i):
                    pe.wait_ge(k_landed[i % 2], L * 512 + p * 128 + 64 * (i // 2 + 1))
                    for f in range(3):
                        pe.wait_ge(kt_ok, L * 48 + p * 12 + (3 * i + f + 1))
                        for j in range(4):
                            ins = pe.transpose(ps[:, 4 + f, P * j:P * j + P], kbuf[:, i % 2, j, P * f:P * f + P], ident[:])
                        ins.then_inc(kt_tr, 1)

                def key_scores(p, i):
                    bb, c = i // 2, i % 2
                    pe.wait_ge(kt_ok, L * 48 + p * 12 + (3 * i + 6))
                    for f in range(3):
                        q = slice(144 * f + 48 * bb, 144 * f + 48 * bb + 96)
                        out = ps[0:96, c, :]
                        pe.matmul(out, q_hi[:, q], kt_hi[:, i % 2, f, :], start=(bb == 0 and f == 0), stop=False)
                        pe.matmul(out, q_hi[:, q], kt_lo[:, i % 2, f, :], start=False, stop=False)
                        ins = pe.matmul(out, q_lo[:, q], kt_hi[:, i % 2, f, :], start=False, stop=(bb == 1 and f == 2))
                    ins.then_inc(sc_done, 1)

                def own_scores():
                    for bb in range(2):
                        for f in range(3):
                            q = slice(144 * f + 48 * bb, 144 * f + 48 * bb + 96)
                            out = ps[0:96, 2, 0:SMP]
                            pe.matmul(out, q_hi[:, q], k_own_hi[:, f, :], start=(bb == 0 and f == 0), stop=False)
                            pe.matmul(out, q_hi[:, q], k_own_lo[:, f, :], start=False, stop=False)
                            ins = pe.matmul(out, q_lo[:, q], k_own_hi[:, f, :], start=False, stop=(bb == 1 and f == 2))
                    ins.then_inc(own_done, 1)

                def transpose_probs(p):
                    pe.wait_ge(sm_ok, L * 4 + p + 1)
                    for j in range(5):
                        ins = pe.transpose(ps[:, 3, 96 * j:96 * j + 96], sp[:, P * j:P * j + P], ident[0:96, 0:96])
                    ins.then_inc(pt2_done, 1)
                    for j in range(5, 8):
                        pe.transpose(ps[:, 2, 96 * (j - 5):96 * (j - 4)], sp[:, P * j:P * j + P], ident[0:96, 0:96])
                    pe.transpose(ps[0:SMP, 2, 288:384], sp[:, PAST_LEN:], ident[0:96, 0:96]).then_inc(pt2_done, 1)

                def smp_out(p, bb, first):
                    if bb == 0:
                        pe.wait_ge(pt2_evac, L * 8 + p * 2 + 2)
                        if not first:
                            pe.wait_ge(y_ready, 12 * L + p + 8)
                    pe.wait_ge(v_landed[bb], L * 512 + p * 128 + 128)
                    out, c = ps[0:48, (7, 3)[bb], 0:HDIM], slice(48 * bb, 48 * bb + 48)
                    for j in range(PAGES):
                        pe.matmul(out, pt_s[:, j, c], vbuf[:, bb, j, :], start=(j == 0), stop=False)
                    pe.matmul(out, pt_s[0:SMP, 8, c], v_own[:, :], start=False, stop=True).then_inc(pv_done, 1)

                def transpose_out(p):
                    for bb in range(2):
                        wait_apart(pe, o_evac, L * NB + p * 2 + (bb + 1))
                        for f in range(3):
                            c = 192 * bb + 48 * f
                            ins = pe.transpose(ps[:, 7, c:c + 48], o_tok[:, bb, P * f:P * f + P], ident[0:48, 0:48])
                    ins.then_inc(ot_done, 1)

                def body(p, n):
                    transpose_k(p, 0)
                    if n >= 2:
                        smp_out(p - 2, 1, False)
                    transpose_k(p, 1)
                    pe.wait_ge(qp_ok, L * 4 + p + 1)
                    if n == 0:
                        pe.wait_ge(o_std, 3 * L + 3)
                    if n >= 1:
                        pe.wait_ge(sm_in, L * 4 + p)
                    key_scores(p, 0)
                    if n >= 2:
                        transpose_out(p - 2)
                    transpose_k(p, 2)
                    key_scores(p, 1)
                    if n >= 1:
                        transpose_probs(p - 1)
                    transpose_k(p, 3)
                    key_scores(p, 2)
                    if n >= 1:
                        smp_out(p - 1, 0, n == 1)
                    key_scores(p, 3)
                    own_scores()

                pe.wait_ge(st_prm, L + 1)
                pe.wait_ge(st_smp, 3 * L + 3)
                pe.wait_ge(y_ready, 12 * L + 5)
                pe.wait_ge(kown_ok, L + 1)
                body(0, 0)
                body(1, 1)
                with pe.Fori(2, 4) as p:
                    body(p, 2)

                def out_part(slot, ks, first):
                    for a in range(2):
                        for k in ks:
                            w = slice((k * 2 + a) * P, (k * 2 + a + 1) * P)
                            out = ps[:, 2 * slot + a, 0:TOK]
                            pe.matmul(out, w_hi[:, slot, w], h_hi[:, k, :], start=(first and k == ks[0]), stop=False)
                            pe.matmul(out, w_hi[:, slot, w], h_lo[:, k, :], start=False, stop=False)
                            ins = pe.matmul(out, w_lo[:, slot, w], h_hi[:, k, :], start=False, stop=(not first and k == ks[-1]))
                    if not first:
                        ins.then_inc(chunk_used, 1)

                smp_out(2, 1, False)
                transpose_out(2)
                early, late = (0, 1, 5, 6, 7), (2, 3, 4)
                chunk_split(half0 + C_WO // 2, 1)
                pe.wait_ge(sm_in, L * 4 + 4)
                out_part(0, early, True)
                transpose_probs(3)
                smp_out(3, 0, False)
                smp_out(3, 1, False)
                transpose_out(3)
                out_part(1, early[:2], True)

                pe.wait_ge(y_ready, 12 * L + 12)
                out_part(0, late, False)
                out_part(1, early[2:] + late, False)
                for slot in range(2):
                    square_group(L, half0 + (C_WO // 2 + 1), G_WO + 2 + slot, slot, h_hi, h_lo, None)
                ffn_in(L, C_F2I, G_F2I, norm + 2, g_hi, g_lo)
                ffn_out(L, C_F2O, G_F2O, L * 2 + 1)
            pe.wait_ge(y_fin_act, 1)
            pe.wait_ge(y_fin_dve, 1)
            for t in range(3):
                n = P if t < 2 else SMP
                for k in range(KT):
                    ins = pe.transpose(ps[0:n, 2 * t + k // 4, P * (k % 4):P * (k % 4) + P], y_fin[:, k, t * P:t * P + n], ident[:])
                ins.then_inc(y_tr, 1)
                if t == 0:
                    pe.wait_ge(ssq_done, NORMS * 4)
                    for u in range(3):
                        m = P if u < 2 else SMP
                        for a in range(2):
                            ins = pe.matmul(ps[0:m, 6, u:u + 1], ssq[:, a, u * P:u * P + m], ones[:, 0:1], start=(a == 0), stop=(a == 1))
                    ins.then_inc(stat_done, 1)


_INS = ["x_prompt", "x_sample", "cache_k", "cache_v", "state_pool", "state_ret", "page_table", "norm_ffn1", "ffn1_w_in",
        "ffn1_w_out", "norm_mix", "w_in", "pool_w", "pool_scale", "w_out", "norm_ffn2", "ffn2_w_in", "ffn2_w_out",
        "norm_final"]
_OUTS = [("y_prompt", (1, SEQ, D)), ("y_sample", (NB, NT, D)),
         ("k_prompt", (DEPTH, 1, SEQ, H, HD)), ("v_prompt", (DEPTH, 1, SEQ, H, HD)),
         ("pool_prompt", (DEPTH, 1, PAST, POOL)), ("ret_prompt", (DEPTH, 1, H, HD, HD)),
         ("k_sample", (DEPTH, NB, NT, H, HD)), ("v_sample", (DEPTH, NB, NT, H, HD)),
         ("pool_sample", (DEPTH, NB, PAST, POOL)), ("ret_sample", (DEPTH, NB, H, HD, HD))]


def kernel(**inputs):
    import concourse.bacc as _bacc
    from concourse.bass_utils import run_bass_kernel_spmd as _run

    nc = _bacc.Bacc("TRN2", target_bir_lowering=False, num_devices=1)
    arrays, A, C, O = {}, {}, {}, {}
    for name in _INS:
        a = np.ascontiguousarray(inputs[name])
        arrays["in_" + name] = a
        A[name] = nc.dram_tensor("in_" + name, a.shape, mybir.dt.from_np(a.dtype), kind="ExternalInput").ap()
    for name, a in constants().items():
        arrays["c_" + name] = a
        C[name] = nc.dram_tensor("c_" + name, a.shape, F32, kind="ExternalInput").ap()
    for name, shape in _OUTS:
        O[name] = nc.dram_tensor("out_" + name, shape, F32, kind="ExternalOutput").ap()
    build(nc, A, C, O)
    r = _run(nc, [arrays], core_ids=[0])
    return tuple(r.results[0]["out_" + name] for name, _ in _OUTS)
```

```python
from contextlib import ExitStack

import numpy as np
import concourse.bass as bass
from concourse import mybir

F32 = mybir.dt.float32
F32R = mybir.dt.float32r
I32 = mybir.dt.int32
ALU = mybir.AluOpType
ACT = mybir.ActivationFunctionType
AX = mybir.AxisListType.X

P = 128
D = 1024
KT = D // P
DEPTH = 2
SEQ = 256
NB, NT = 8, 8
SMP = NB * NT
TOK = SEQ + SMP
HD = 64
H = 6
HDIM = H * HD
POOL = 256
WINDOWS = (2, 4, 8, 16)
PAST = 15
PAGE = 128
PAGES = 8
PAST_LEN = PAGE * PAGES
POOL_PAGES = 80
FF = 2816
FT = FF // P
ZT = 23
EPS = 1e-6
BIG = 1.0e30
ATT_SCALE = HD ** -0.5
SLOPES = [2.0 ** (-8.0 * (h + 1) / H) for h in range(H)]
GAMMAS = [1.0 - 2.0 ** (-5.0 - h) for h in range(H)]
NORMS = 3 * DEPTH + 1
ZU, ZQA, ZKA, ZVA, ZQR, ZKR, ZVR, ZG = 0, 2, 5, 8, 11, 14, 17, 20

OUT_K = ((0, 8), (8, 15), (15, 22))
C_F1I, C_F1O, C_MIX, C_WO, C_F2I, C_F2O, C_ALL = 0, 22, 34, 46, 50, 72, 84
G_F1I, G_F1O, G_MIX, G_WO, G_F2I, G_F2O, G_ALL = 0, 22, 26, 38, 42, 64, 68
GROUPS0 = 4


def constants():
    f = np.float32
    c = {}
    c["ident"] = np.eye(P, dtype=f)
    q = np.arange(P)[:, None]
    dist = np.zeros((P, 3 * P))
    k = np.arange(2 * P)[None, :]
    dist[:, :256] = np.where(k <= q + P, q + P - k, BIG)
    k = np.arange(P)[None, :]
    dist[:, 256:] = np.where(k <= q, q - k, BIG)
    c["dist_p"] = dist.astype(f)
    g = np.array(GAMMAS)
    i = np.arange(SEQ)[None, None, :]
    j = np.arange(P)[:, None, None]
    c["decay_p"] = np.where(i >= j, ATT_SCALE * g[None, :, None] ** np.maximum(i - j, 0), 0.0).astype(f)
    row_f, row_b, row_a, row_q = (r.ravel() for r in np.indices((H // 2, 2, 2, NT)))
    row_h = 2 * row_f + row_a
    sl = np.array(SLOPES)[row_h]
    c["alibi_s"] = (-sl[:, None] * (PAST_LEN + row_q[:, None] - np.arange(PAST_LEN)[None, :])).astype(f)
    key_b, key_j = np.divmod(np.arange(SMP), NT)
    own = np.full((2 * H * NT, NB // 2, SMP), -BIG)
    for p in range(NB // 2):
        ok = (key_b[None, :] == 2 * p + row_b[:, None]) & (key_j[None, :] <= row_q[:, None])
        own[:, p][ok] = (-sl[:, None] * (row_q[:, None] - key_j[None, :]))[ok]
    c["alibi_own"] = own.astype(f)
    same = (key_b[:, None] == key_b[None, :]) & (key_j[None, :] >= key_j[:, None])
    diff = np.maximum(key_j[None, :] - key_j[:, None], 0)
    c["decay_s"] = np.where(same[:, None, :], ATT_SCALE * g[None, :, None] ** diff[:, None, :], 0.0).astype(f)
    kd = np.zeros((P, 3, H))
    kd[:, 0] = ATT_SCALE * g[None] ** (SEQ - 1 - np.arange(P))[:, None]
    kd[:, 1] = ATT_SCALE * g[None] ** (P - 1 - np.arange(P))[:, None]
    kd[:SMP, 2] = ATT_SCALE * g[None] ** (NT - 1 - key_j)[:, None]
    c["k_decay"] = kd.astype(f)
    head = 2 * np.arange(3)[None, :] + (np.arange(P) // HD)[:, None]
    c["q_decay"] = (g[head][:, :, None] ** (key_j + 1)[None, None, :]).astype(f)
    c["c_decay"] = (g[head] ** NT).astype(f)
    c["own_b"] = (key_b[:, None] == np.arange(NB)[None, :]).astype(f)
    w = np.array(WINDOWS)[2 * np.arange(2)[None, :] + (np.arange(P) // HD)[:, None]]
    c["inv_cnt"] = (1.0 / np.minimum(w[:, :, None], np.arange(1, SEQ + 1)[None, None, :])).astype(f)
    c["rank"] = np.tile(np.arange(1, 5, dtype=f), (2 * H * NT, 1))
    hs = np.zeros((P, P), f)
    hs[:HD, :HD] = 1.0 / HD
    hs[HD:, HD:] = 1.0 / HD
    c["head_mean"] = hs
    return c


def build(nc, A, C, O):
    ctx = ExitStack()

    def sb(name, shape, dt=F32):
        return ctx.enter_context(nc.sbuf_tensor(name, shape, dt))

    def sem(name):
        return ctx.enter_context(nc.semaphore(name))

    with ctx:
        x = sb("x", [P, KT, TOK])
        h_hi = sb("h_hi", [P, KT, TOK], F32R)
        h_lo = sb("h_lo", [P, KT, TOK], F32R)
        w_raw = sb("w_raw", [P, 2, 16 * P])
        w_hi = sb("w_hi", [P, 2, 16 * P], F32R)
        w_lo = sb("w_lo", [P, 2, 16 * P], F32R)
        rstd = sb("rstd", [P, TOK])
        ssq = sb("ssq", [P, 2, TOK])
        gains = sb("gains", [P, NORMS * KT + 4])
        cst = {n: sb(n, list(C[n].shape)) for n in C}
        ident, head_mean = cst["ident"], cst["head_mean"]
        ones = sb("ones", [P, P])
        eps = sb("eps", [P, 1])
        pages = sb("pages", [1, NB * PAGES], I32)
        wbd = sb("wbd", [P, 2, P])
        q_bd = sb("q_bd", [P, 3, 2, 32])
        st = sb("st", [P, 32])
        rstd_tok = sb("rstd_tok", [P, 4])
        ss = sb("ss", [96, 48])
        tmp = sb("tmp", [P, 2460])
        t_gate = tmp[:, 0:640].rearrange("p (a n) -> p a n", a=2)
        t_up = tmp[:, 640:1280].rearrange("p (a n) -> p a n", a=2)
        t_sil = tmp[:, 1280:1920].rearrange("p (a n) -> p a n", a=2)
        sq_slot = [t_gate, t_up]

        zone_offset = (nc.sbuf_base + 31) // 32 * 32
        zone = sb("zone", [P, 5120 + 8])
        arena_offset = (nc.sbuf_base + 31) // 32 * 32
        arena = sb("arena", [P, 18496 + 8])
        zone_at, arena_at = zone_offset, arena_offset

        def at(name, shape, dt, base, kb):
            return nc.alloc_sbuf_tensor_at(name, shape, dt, offset=base + int(kb * 1024))

        kbuf = at("kbuf", [P, 2, 4, HDIM], F32, zone_at, 0)
        q_smp = at("q_smp", [P, 3, SMP], F32, zone_at, 12)
        k_own = at("k_own", [P, 3, SMP], F32, zone_at, 12.75)
        v_own = at("v_own", [SMP, HDIM], F32, zone_at, 14.25)
        sp = at("sp", [96, PAST_LEN + SMP], F32, zone_at, 15.75)
        g_hi = at("g_hi", [P, KT, TOK], F32R, zone_at, 0)
        g_lo = at("g_lo", [P, KT, TOK], F32R, zone_at, 10)

        act_hi = at("act_hi", [P, FT, TOK], F32R, arena_at, 0)
        act_lo = at("act_lo", [P, FT, TOK], F32R, arena_at, 27.5)
        z = at("z", [P, ZT, TOK], F32, arena_at, 0)
        vbuf = at("vbuf", [P, 2, PAGES, HDIM], F32, arena_at, 0)
        kr_tok = at("kr_tok", [P, 3, HDIM], F32, arena_at, 28.75)
        vr_tok = at("vr_tok", [P, 3, HDIM], F32, arena_at, 33.25)
        va_tok = at("va_tok", [P, 2, HDIM], F32, arena_at, 37.75)
        ka_tok = at("ka_tok", [P, 3, HDIM], F32, arena_at, 40.75)
        u_tok = at("u_tok", [P, 2, POOL], F32, arena_at, 45.25)
        ext = at("ext", [P, 912], F32, arena_at, 47.25)
        s_p = at("s_p", [P, 2, 3 * P], F32, arena_at, 51)
        pt_p = at("pt_p", [P, 2, 3 * P], F32, arena_at, 54)
        kt = at("kt", [P, 2, 3, 512], F32, arena_at, 28.75)
        pt_s = at("pt_s", [P, 9 * 96 + 16], F32, arena_at, 53.5)
        o_tok = at("o_tok", [96, 2, P], F32, arena_at, 57)
        v_bd = [at("v_bd0", [SMP, NB, HD], F32, arena_at, 57), at("v_bd1", [SMP, NB, HD], F32, arena_at, 47.25)]
        att_p = [at("att_p0", [P, 3 * P], F32, arena_at, 59), at("att_p1", [P, 3 * P], F32, zone_at, 17.25)]
        att_s = [at("att_s0", [SMP, SMP], F32, arena_at, 60.5), at("att_s1", [SMP, SMP], F32, zone_at, 18.75)]
        s0 = at("s0", [P, 3, NB, HD], F32, arena_at, 60.75)
        o_sq = at("o_sq", [P, 3, TOK], F32, arena_at, 66.75)
        pre_tok = at("pre_tok", [NB * PAST, POOL], F32, arena_at, 70.5)
        sp_new = at("sp_new", [P, 3, HD], F32, arena_at, 71.5)
        q_dec = at("q_dec", [P, 3, NB, 2, NT], F32, zone_at, 15.75)
        o_past = at("o_past", [P, 3, SMP], F32, zone_at, 19)
        ident_r = at("ident_r", [P, P], F32R, arena_at, 70.5)
        x_tok = at("x_tok", [P, 3, D], F32, arena_at, 0)
        g_rows = at("g_rows", [NORMS * KT + 4, P], F32, arena_at, 14)
        y_tok = at("y_tok", [P, 3, D], F32, arena_at, 14)

        ps = ctx.enter_context(nc.psum_tensor("ps", [P, 8, 512], F32))

        w_landed = [sem("w_landed0"), sem("w_landed1")]
        hi_done = sem("hi_done")
        split_done = sem("split_done")
        chunk_used = sem("chunk_used")
        evac_done = sem("evac_done")
        silu_ready = sem("silu_ready")
        a_ready = sem("a_ready")
        a_hi = sem("a_hi")
        act_ready = sem("act_ready")
        g_hi_done = sem("g_hi_done")
        gx_ready = sem("gx_ready")
        sq_done = sem("sq_done")
        ssq_done = sem("ssq_done")
        stat_done = sem("stat_done")
        std_done = sem("std_done")
        loaded = sem("loaded")
        x_loaded, gain_loaded = sem("x_loaded"), sem("gain_loaded")
        GAIN_LOADS = 5
        prep = sem("prep")
        x_tr = sem("x_tr")
        gain_tr = sem("gain_tr")
        gain_ok = sem("gain_ok")
        aux_loaded = sem("aux_loaded")
        u_tr, pre_tr = sem("u_tr"), sem("pre_tr")
        u_out, pre_in = sem("u_out"), sem("pre_in")
        tr_done, tr_act, tr_dve = sem("tr_done"), sem("tr_act"), sem("tr_dve")
        s_done, s_max, s_exp, p_norm = sem("s_done"), sem("s_max"), sem("s_exp"), sem("p_norm")
        pt_done, pt_evac, oa_done, oa_hi = sem("pt_done"), sem("pt_evac"), sem("oa_done"), sem("oa_hi")
        r_done, r_mask, or_done = sem("r_done"), sem("r_mask"), sem("or_done")
        past_done, past_ok = sem("past_done"), sem("past_ok")
        o_gated, o_sqd, g_silu, q_dec_ok = sem("o_gated"), sem("o_sqd"), sem("g_silu"), sem("q_dec_ok")
        mean_done, o_std, or_ready, or_hi = sem("mean_done"), sem("o_std"), sem("or_ready"), sem("or_hi")
        vbd_ok, vbd_used, sp_done = sem("vbd_ok"), sem("vbd_used"), sem("sp_done")
        st_smp, st_prm = sem("st_smp"), sem("st_prm")
        pool_d, pool_mm, pool_hi = sem("pool_d"), sem("pool_mm"), sem("pool_hi")
        kown_ok = sem("kown_ok")
        y_ready = sem("y_ready")
        k_landed = [sem("k_landed0"), sem("k_landed1")]
        v_landed = [sem("v_landed0"), sem("v_landed1")]
        qp_ok = sem("qp_ok")
        kt_tr, kt_ok, sc_done = sem("kt_tr"), sem("kt_ok"), sem("sc_done")
        own_done, sm_in, sm_bias, sm_exp, sm_ok = (sem("own_done"), sem("sm_in"), sem("sm_bias"),
                                                   sem("sm_exp"), sem("sm_ok"))
        pt2_done, pt2_evac, pv_done, ys_hi = sem("pt2_done"), sem("pt2_evac"), sem("pv_done"), sem("ys_hi")
        o_evac, ot_done = sem("o_evac"), sem("ot_done")
        stored_kv, stored_st = sem("stored_kv"), sem("stored_st")
        y_tr, ident_ok = sem("y_tr"), sem("ident_ok")
        y_tok_act, y_tok_dve, rstd_ok, stored_y = sem("y_tok_act"), sem("y_tok_dve"), sem("rstd_ok"), sem("stored_y")
        waited = sem("waited")
        Y_ORDER = (0, 2, 1)
        KV_STORES, ST_STORES, AUX_LOADS = 7, 8, 11

        def y_smp(buf, half, p):
            return buf[HD * half:HD * half + HD, 2:5, bass.ds(p * 16 + SEQ, 16)].rearrange("p f (b q) -> p b f q", b=2)

        def o_smp(half):
            return ps[HD * half:HD * half + HD, 7, 0:192].rearrange("p (b f x) -> p b f x", b=2, f=3)[:, :, :, 8 * half:8 * half + 8]

        def wait_apart(engine, semaphore, value):
            engine.wait_ge(semaphore, value)
            engine.sem_inc(waited, 1)

        block = ctx.enter_context(nc.Block())
        bc2 = lambda ap: ap.unsqueeze(1).to_broadcast([P, 2, TOK])

        @block.sync
        def _(sp_e):
            def load(src, slot, half, tiles, nk):
                sp_e.wait_ge(split_done, half * 2 + (slot + 1))
                dst = w_raw[:, slot, 0:tiles * P].rearrange("p (k c) -> p k c", k=nk)
                sp_e.dma_start(dst, src).then_inc(w_landed[slot], 16)

            def first_chunks(w, layer, half):
                for slot in range(2):
                    cols = slice(slot * FF, slot * FF + 256)
                    load(w[layer:layer + 1, :, cols].rearrange("a (k p) c -> p (a k) c", p=P), slot, half, 16, 8)

            def ffn_in(w, L, c0, start=0):
                with sp_e.Fori(start, FT // 2) as i:
                    for slot in range(2):
                        cols = bass.ds(i * 256 + slot * FF, 256)
                        load(w[bass.ds(L, 1), :, cols].rearrange("a (k p) c -> p (a k) c", p=P),
                             slot, L * (C_ALL // 2) + i + c0 // 2, 16, 8)

            def ffn_out(w, L, c0):
                with sp_e.Fori(0, 2) as i:
                    for g in range(2):
                        for n, (a, b) in enumerate(OUT_K):
                            c = 3 * g + n
                            src = w[bass.ds(L, 1), a * P:b * P, bass.ds(i * 512 + 256 * g, 256)]
                            load(src.rearrange("a (k p) c -> p (a k) c", p=P), c % 2,
                                 L * (C_ALL // 2) + i * 3 + (c0 + c) // 2, 2 * (b - a), b - a)

            def square(w, L, c0, at_c, slot, cols=256):
                src = w[bass.ds(L, 1), :, at_c].rearrange("a (k p) c -> p (a k) c", p=P)
                load(src, slot, c0, 8 * cols // P, 8)

            sp_e.dma_start(ident[:], C["ident"]).then_inc(x_loaded, 16)
            for t in range(2):
                sp_e.dma_start(x_tok[:, t, :], A["x_prompt"][0, t * P:t * P + P, :]).then_inc(x_loaded, 16)
            sp_e.dma_start(x_tok[0:SMP, 2, :], A["x_sample"].rearrange("b t d -> (b t) d")).then_inc(x_loaded, 16)
            first_chunks(A["ffn1_w_in"], 0, 0)
            with sp_e.Fori(0, DEPTH) as L:
                half0 = L * (C_ALL // 2)
                ffn_in(A["ffn1_w_in"], L, C_F1I, 1)
                ffn_out(A["ffn1_w_out"], L, C_F1O)
                with sp_e.Fori(0, 5) as i:
                    for slot in range(2):
                        square(A["w_in"], L, half0 + i + C_MIX // 2, bass.ds(i * 512 + 256 * slot, 256), slot)
                square(A["w_in"], L, half0 + (C_MIX // 2 + 5), slice(2560, 2816), 0)
                square(A["w_in"], L, half0 + (C_MIX // 2 + 5), slice(2816, 2944), 1, cols=P)
                for slot in range(2):
                    square(A["w_out"], L, half0 + C_WO // 2, slice(256 * slot, 256 * slot + 256), slot)
                sp_e.wait_ge(u_out, 2 * L + 2)
                sp_e.dma_start(O["pool_prompt"][bass.ds(L, 1), 0].rearrange("a t c -> (a t) c"),
                               u_tok[P - PAST:P, 0, :]).then_inc(stored_kv, 16)
                sp_e.dma_start(O["pool_sample"][bass.ds(L, 1), :, PAST - NT:PAST, :].rearrange("a b t c -> (a b) t c"),
                               u_tok[0:SMP, 1, :]).then_inc(stored_kv, 16)
                sp_e.dma_start(O["pool_sample"][bass.ds(L, 1), :, 0:PAST - NT, :].rearrange("a b t c -> (a b) t c"),
                               A["state_pool"][bass.ds(L, 1), :, NT:PAST, :].rearrange("a b t c -> (a b) t c")
                               ).then_inc(stored_kv, 16)
                sp_e.wait_ge(tr_act, 9 * L + 9)
                for name, src, own in (("k", ka_tok, ka_tok[0:SMP, 2, :]), ("v", va_tok, v_own[:, :])):
                    sp_e.dma_start(O[name + "_prompt"][bass.ds(L, 1), 0].rearrange("a (t p) h d -> p (a t) (h d)", p=P),
                                   src[:, 0:2, :]).then_inc(stored_kv, 16)
                    sp_e.dma_start(O[name + "_sample"][bass.ds(L, 1)].rearrange("a b t h d -> (a b t) (h d)"),
                                   own).then_inc(stored_kv, 16)

                def load_v(p, first):
                    for bb in range(2):
                        page = [sp_e.value_load(pages[0:1, bass.ds(p * 16 + (8 * bb + j), 1)], min_val=0, max_val=POOL_PAGES - 1)
                                for j in range(PAGES)]
                        if not first:
                            wait_apart(sp_e, pv_done, L * NB + p * 2 + (bb - 1))
                        for j in range(PAGES):
                            sp_e.dma_start(vbuf[:, bb, j, :],
                                           A["cache_v"][L, page[j]].rearrange("t h d -> t (h d)")).then_inc(v_landed[bb], 16)

                sp_e.wait_ge(kown_ok, L + 1)
                sp_e.wait_ge(pool_d, L + 1)
                wait_apart(sp_e, r_done, H * L + H)
                load_v(0, True)
                sp_e.wait_ge(st_prm, L + 1)
                for half in range(2):
                    sp_e.dma_start(O["ret_prompt"][L, 0].rearrange("(f a) d v -> a d f v", a=2)[half],
                                   sp_new[HD * half:HD * half + HD, :, :]).then_inc(stored_st, 16)
                sp_e.wait_ge(st_smp, 3 * L + 3)
                for half in range(2):
                    for f in range(3):
                        sp_e.dma_start(O["ret_sample"][L, :, 2 * f + half].rearrange("b d v -> d b v"),
                                       s0[HD * half:HD * half + HD, f, :, :]).then_inc(stored_st, 16)
                with sp_e.Fori(1, 4) as p:
                    load_v(p, False)
                for slot in range(2):
                    square(A["w_out"], L, half0 + (C_WO // 2 + 1), slice(512 + 256 * slot, 768 + 256 * slot), slot)
                ffn_in(A["ffn2_w_in"], L, C_F2I)
                ffn_out(A["ffn2_w_out"], L, C_F2O)
                first_chunks(A["ffn1_w_in"], DEPTH - 1, half0 + C_ALL // 2)
            for m, t in enumerate(Y_ORDER):
                sp_e.wait_ge(y_tok_act, m + 1)
                sp_e.wait_ge(y_tok_dve, m + 1)
                if t < 2:
                    sp_e.dma_start(O["y_prompt"][0, t * P:t * P + P, :], y_tok[:, t, :]).then_inc(stored_y, 16)
                else:
                    sp_e.dma_start(O["y_sample"].rearrange("b t d -> (b t) d"), y_tok[0:SMP, 2, :]).then_inc(stored_y, 16)
            sp_e.wait_ge(stored_y, 48)
            sp_e.wait_ge(stored_kv, 16 * KV_STORES * DEPTH)
            sp_e.wait_ge(stored_st, 16 * ST_STORES * DEPTH)

        @block.gpsimd
        def _(pool):
            pool.dma_start(pages[:], A["page_table"].rearrange("b n -> (b n)").unsqueeze(0)).then_inc(loaded, 16)
            pool.memset(wbd[:], 0.0).then_inc(prep, 1)
            pool.memset(q_bd[:], 0.0).then_inc(prep, 1)

            def add_squares(q):
                for j in range(4):
                    s = sq_slot[j % 2]
                    if j == 0:
                        wait_apart(pool, sq_done, q + (j + 1))
                        pool.tensor_copy(ssq[:], s).then_inc(ssq_done, 1)
                    else:
                        pool.drain()
                        pool.wait_ge(sq_done, q + (j + 1))
                        pool.tensor_tensor(ssq[:], ssq[:], s, ALU.add).then_inc(ssq_done, 1)

            def load_k(L, g, slot, first=False):
                page = [pool.value_load(pages[0:1, bass.ds(g * 4 + j, 1)], min_val=0, max_val=POOL_PAGES - 1) for j in range(4)]
                if not first:
                    wait_apart(pool, kt_tr, L * 48 + g * 3 - 3)
                for j in range(4):
                    pool.dma_start(kbuf[:, slot, j, :],
                                   A["cache_k"][L, page[j]].rearrange("t h d -> t (h d)")).then_inc(k_landed[slot], 16)

            add_squares(0)
            for n in C:
                if n != "ident":
                    pool.dma_start(cst[n][:], C[n]).then_inc(loaded, 16)
            with pool.Fori(0, DEPTH) as L:
                add_squares(L * 12 + 4)
                pool.wait_ge(chunk_used, L * C_ALL + (C_MIX + 2))
                for t in range(2):
                    for a in range(2):
                        o = HD * a
                        pool.dma_start(wbd[o:o + HD, t, o:o + HD], A["pool_w"][L, 2 * t + a]).then_inc(aux_loaded, 16)
                for half in range(2):
                    for f in range(3):
                        pool.dma_start(s0[HD * half:HD * half + HD, f, :, :],
                                       A["state_ret"][L, :, 2 * f + half].rearrange("b d v -> d b v")).then_inc(aux_loaded, 16)
                pool.dma_start(pre_tok[:], A["state_pool"][L].rearrange("b t c -> (b t) c")).then_inc(aux_loaded, 16)
                wait_apart(pool, chunk_used, L * C_ALL + (C_MIX + 7))
                load_k(L, 0, 0, True)
                load_k(L, 1, 1, True)

                ep = ext[:, 0:542].rearrange("p (t n) -> p t n", t=2)
                es = ext[:, 542:910].rearrange("p (t b n) -> p t b n", t=2, b=NB)
                sums = [(tmp[:, a:a + 542].rearrange("p (t n) -> p t n", t=2),
                         tmp[:, a + 542:a + 910].rearrange("p (t b n) -> p t b n", t=2, b=NB)) for a in (0, 910)]
                dm = tmp[:, 1820:2460].rearrange("p (t n) -> p t n", t=2)
                wait_apart(pool, evac_done, L * G_ALL + (GROUPS0 + G_MIX + 12))
                pool.memset(ep[:, :, 0:PAST], 0.0)
                pool.tensor_copy(ep[:, :, PAST:], z[:, ZU:ZU + 2, 0:SEQ])
                for t in range(2):
                    pool.tensor_copy(es[:, t, :, PAST:], z[:, ZU + t, SEQ:].rearrange("p (b n) -> p b n", b=NB))
                wait_apart(pool, pre_in, L + 1)
                src_p, src_s = ep, es
                for n, w in enumerate(WINDOWS):
                    s = w // 2
                    dst_p, dst_s = sums[n % 2]
                    pool.drain()
                    pool.tensor_tensor(dst_p[:, :, w - 1:], src_p[:, :, w - 1:], src_p[:, :, w - 1 - s:PAST + SEQ - s], ALU.add)
                    for t in range(2):
                        pool.tensor_tensor(dst_s[:, t, :, w - 1:], src_s[:, t, :, w - 1:],
                                           src_s[:, t, :, w - 1 - s:PAST + NT - s], ALU.add)
                    pool.drain()
                    o, t = HD * (n % 2), n // 2
                    d_p, d_s = dm[o:o + HD, t, 0:SEQ], dm[o:o + HD, t, SEQ:]
                    pool.tensor_tensor(d_p, dst_p[o:o + HD, t, PAST:], cst["inv_cnt"][o:o + HD, t, :], ALU.mult)
                    d_s3 = d_s.rearrange("p (b n) -> p b n", b=NB)
                    pool.tensor_scalar(d_s3, dst_s[o:o + HD, t, :, PAST:], 1.0 / w, None, ALU.mult)
                    pool.drain()
                    pool.tensor_tensor(d_p, d_p, z[o:o + HD, ZU + t, 0:SEQ], ALU.subtract)
                    ins = pool.tensor_tensor(d_s, d_s, z[o:o + HD, ZU + t, SEQ:], ALU.subtract)
                    src_p, src_s = dst_p, dst_s
                ins.then_inc(pool_d, 1)
                pool.wait_ge(tr_act, 9 * L + 9)
                for h in range(H):
                    if h >= 2:
                        pool.wait_ge(vbd_used, H * L + (h - 1))
                    pool.tensor_tensor(v_bd[h % 2][:], vr_tok[0:SMP, 2, h * HD:h * HD + HD].unsqueeze(1).to_broadcast([SMP, NB, HD]),
                                       cst["own_b"][:].unsqueeze(2).to_broadcast([SMP, NB, HD]), ALU.mult).then_inc(vbd_ok, 1)
                with pool.Fori(1, 8) as i:
                    for slot in range(2):
                        load_k(L, i * 2 + slot, slot)
                add_squares(L * 12 + 8)
                add_squares(L * 12 + 12)

        @block.scalar
        def _(act):
            def hi_split(half, slot):
                act.wait_ge(w_landed[slot], half * 16 + 16)
                act.wait_ge(chunk_used, half * 2 + (slot + 1))
                act.activation(w_hi[:, slot, :], w_raw[:, slot, :], ACT.Copy).then_inc(hi_done, 1)

            def ffn_in(L, c0, g0, f):
                with act.Fori(0, FT // 2) as i:
                    half = L * (C_ALL // 2) + i + (c0 // 2 + 1)
                    n = f * (FT // 2) + i + 1
                    hi_split(half, 0)
                    act.wait_ge(evac_done, L * G_ALL + i * 2 + (GROUPS0 + g0 + 1))
                    act.activation(t_sil, t_gate, ACT.Silu).then_inc(silu_ready, 1)
                    hi_split(half, 1)
                    act.wait_ge(a_ready, n)
                    act.activation(act_hi[:, bass.ds(i * 2, 2), :], t_up, ACT.Copy).then_inc(a_hi, 1)

            def gx_pair(dst, norm, o, groups):
                act.wait_ge(evac_done, groups)
                for k in (2 * o, 2 * o + 1):
                    ins = act.activation(dst[:, k, :], x[:, k, :], ACT.Copy, scale=gains[:, bass.ds(norm * KT + k, 1)])
                ins.then_inc(g_hi_done, 1)

            def squares(norm, o):
                if o >= 2:
                    act.wait_ge(ssq_done, norm * 4 + (o - 1))
                act.activation(sq_slot[o % 2], x[:, 2 * o:2 * o + 2, :], ACT.Square).then_inc(sq_done, 1)

            def root(n):
                act.wait_ge(stat_done, n)
                act.activation(rstd[:], ps[:, 4, 0:TOK], ACT.Sqrt, scale=1.0 / D, bias=eps[:, 0:1]).then_inc(std_done, 1)

            def ffn_out(L, c0, g0, norm, dst):
                for g in range(4):
                    for n in range(3):
                        c = 3 * g + n + 2
                        if g < 3 or n < 2:
                            hi_split(L * (C_ALL // 2) + (c0 + c) // 2, c % 2)
                        if n == 2:
                            gx_pair(dst, norm, g, L * G_ALL + (GROUPS0 + g0 + g + 1))
                            squares(norm, g)
                        if g == 3 and n == 2:
                            hi_split(L * (C_ALL // 2) + (c0 + c) // 2, c % 2)

            for n, name in enumerate(("norm_ffn1", "norm_mix", "norm_ffn2")):
                act.dma_start(g_rows[n * DEPTH * KT:(n + 1) * DEPTH * KT, :],
                              A[name].rearrange("l (k p) -> (l k) p", p=P)).then_inc(gain_loaded, 16)
            act.dma_start(g_rows[NORMS * KT - KT:NORMS * KT, :],
                          A["norm_final"].rearrange("(k p) -> k p", p=P)).then_inc(gain_loaded, 16)
            act.dma_start(g_rows[NORMS * KT:NORMS * KT + 4, :],
                          A["pool_scale"].rearrange("l (k p) -> (l k) p", p=P)).then_inc(gain_loaded, 16)
            hi_split(0, 0)
            act.wait_ge(gain_ok, 1)
            for j in range(4):
                gx_pair(h_hi, 0, j, j + 1)
                if j:
                    squares(0, j - 1)
            squares(0, 3)
            hi_split(0, 1)
            with act.Fori(0, DEPTH) as L:
                half0 = L * (C_ALL // 2)
                norm = L * 3
                root(norm + 1)
                ffn_in(L, C_F1I, G_F1I, L * 2)
                ffn_out(L, C_F1O, G_F1O, norm + 1, h_hi)
                root(norm + 2)
                with act.Fori(0, 5) as i:
                    for slot in range(2):
                        hi_split(half0 + i + (C_MIX // 2 + 1), slot)
                hi_split(half0 + C_WO // 2, 0)

                def tokens(t):
                    n = P if t < 2 else SMP
                    for kind, bank, dst in ((0, 4, ka_tok[0:n, t, :]),
                                            (1, 5, va_tok[:, t, :] if t < 2 else v_own[:, :]),
                                            (3, 7, vr_tok[0:n, t, :])):
                        act.wait_ge(tr_done, 12 * L + (4 * t + kind + 1))
                        act.activation(dst, ps[0:n, bank, 0:HDIM], ACT.Copy).then_inc(tr_act, 1)

                act.wait_ge(u_tr, L + 1)
                act.activation(u_tok[:, 0, :], ps[:, 3, 0:POOL], ACT.Copy).then_inc(u_out, 1)
                act.activation(u_tok[0:SMP, 1, :], ps[0:SMP, 3, POOL:2 * POOL], ACT.Copy).then_inc(u_out, 1)
                tokens(0)
                tokens(1)
                act.wait_ge(evac_done, L * G_ALL + (GROUPS0 + G_MIX + 12))
                act.activation(z[:, ZG:ZG + 3, :], z[:, ZG:ZG + 3, :], ACT.Silu).then_inc(g_silu, 1)
                act.activation(k_own[:], z[:, ZKA:ZKA + 3, SEQ:], ACT.Copy).then_inc(kown_ok, 1)
                tokens(2)

                def exp(h):
                    s = h % 2
                    act.wait_ge(s_max, H * L + (h + 1))
                    act.activation(s_p[:, s, 0:256], s_p[:, s, 0:256], ACT.Exp, scale=ATT_SCALE, bias=st[:, 0 + 2 * s:1 + 2 * s],
                                   accum_out=st[:, 4 + 2 * s:5 + 2 * s])
                    act.activation(s_p[:, s, 256:384], s_p[:, s, 256:384], ACT.Exp, scale=ATT_SCALE, bias=st[:, 1 + 2 * s:2 + 2 * s],
                                   accum_out=st[:, 5 + 2 * s:6 + 2 * s]).then_inc(s_exp, 1)

                def att_hi(f):
                    act.wait_ge(oa_done, 3 * L + (f + 1))
                    act.activation(h_hi[:, 2 + f, 0:SEQ], ps[:, 4, 0:SEQ], ACT.Copy).then_inc(oa_hi, 1)

                exp(0)
                for h in range(H):
                    f, s = h // 2, h % 2
                    if h + 1 < H:
                        exp(h + 1)
                    act.wait_ge(pt_done, H * L + (h + 1))
                    act.activation(pt_p[:, s, :], ps[:, 2 + s, 0:384], ACT.Copy).then_inc(pt_evac, 1)
                    if h == 0:
                        hi_split(half0 + C_WO // 2, 1)
                    if s:
                        act.wait_ge(o_gated, 3 * L + (f + 1))
                        act.activation(o_sq[:, f, :], ps[:, 7, 0:TOK], ACT.Square).then_inc(o_sqd, 1)
                    elif f:
                        att_hi(f - 1)
                act.wait_ge(sp_done, L + 1)
                act.activation(sp_new[:], ps[:, 7, 320:512].rearrange("p (f v) -> p f v", f=3), ACT.Copy).then_inc(st_prm, 1)
                for t in range(2):
                    act.wait_ge(pool_mm, 2 * L + (t + 1))
                    act.activation(h_hi[:, t, :], ps[:, (5, 0)[t], 0:TOK], ACT.Copy, scale=gains[:, bass.ds(L * 2 + (NORMS * KT + t), 1)]).then_inc(pool_hi, 1)
                att_hi(2)

                def root_o(f):
                    act.wait_ge(mean_done, 3 * L + (f + 1))
                    act.activation(o_sq[:, f, :], ps[:, (2, 3, 7)[f], 0:TOK], ACT.Sqrt, bias=eps[:, 0:1]).then_inc(o_std, 1)

                def or_high(f):
                    act.wait_ge(or_ready, 3 * L + (f + 1))
                    act.activation(h_hi[:, 5 + f, :], z[:, ZG + f, :], ACT.Copy).then_inc(or_hi, 1)

                def qprep(p):
                    for half in range(2):
                        for bb in range(2):
                            c = 16 * bb + 8 * half
                            ins = act.activation(q_bd[HD * half:HD * half + HD, :, bb, c:c + 8],
                                                 q_smp[HD * half:HD * half + HD, :, bass.ds(p * 16 + 8 * bb, 8)], ACT.Copy)
                    ins.then_inc(qp_ok, 1)

                def kt_evac(p, i):
                    act.wait_ge(sc_done, L * 16 + p * 4 + (i + 1))
                    for f in range(3):
                        act.wait_ge(kt_tr, L * 48 + p * 12 + (3 * i + f + 1))
                        act.activation(kt[:, i % 2, f, :], ps[:, 4 + f, :], ACT.Copy).then_inc(kt_ok, 1)

                def exps(p):
                    act.wait_ge(sm_bias, L * 4 + p + 1)
                    for n in range(5):
                        a, b = (256 * n, 256 * n + 256) if n < 4 else (PAST_LEN, PAST_LEN + SMP)
                        ins = act.activation(sp[:, a:b], sp[:, a:b], ACT.Exp, bias=ss[:, 32 + n:33 + n],
                                             accum_out=ss[:, 40 + n:41 + n])
                    ins.then_inc(sm_exp, 1)

                def probs_evac(p):
                    act.wait_ge(pt2_done, L * 8 + p * 2 + 2)
                    act.activation(pt_s[:, 0:480].rearrange("p (n c) -> p n c", c=96), ps[:, 3, 0:480].rearrange("p (n c) -> p n c", c=96), ACT.Copy).then_inc(pt2_evac, 1)
                    act.wait_ge(pt2_done, L * 8 + p * 2 + 3)
                    act.activation(pt_s[:, 480:768].rearrange("p (n c) -> p n c", c=96), ps[:, 2, 0:288].rearrange("p (n c) -> p n c", c=96), ACT.Copy)
                    act.activation(pt_s[0:SMP, 768:864], ps[0:SMP, 2, 288:384], ACT.Copy).then_inc(pt2_evac, 1)

                def out_evac(p, bb):
                    act.wait_ge(pv_done, L * NB + p * 2 + (bb + 1))
                    act.activation(o_tok[:, bb, :], ps[0:96, (7, 3)[bb], 0:P], ACT.Copy).then_inc(o_evac, 1)

                def y_high(p):
                    act.wait_ge(ot_done, L * 4 + p + 1)
                    for half in range(2):
                        ins = act.activation(y_smp(h_hi, half, p), o_smp(half), ACT.Copy)
                    ins.then_inc(ys_hi, 1)

                act.wait_ge(stored_kv, L * (16 * KV_STORES) + 16 * KV_STORES)
                act.wait_ge(kown_ok, L + 1)

                qprep(0)
                kt_evac(0, 0)
                kt_evac(0, 1)
                for f in range(3):
                    root_o(f)
                kt_evac(0, 2)
                kt_evac(0, 3)
                for f in range(3):
                    or_high(f)

                def body(p, first):
                    act.wait_ge(own_done, L * 4 + p)
                    qprep(p)
                    kt_evac(p, 0)
                    if not first:
                        out_evac(p - 2, 1)
                    kt_evac(p, 1)
                    exps(p - 1)
                    if not first:
                        y_high(p - 2)
                    kt_evac(p, 2)
                    probs_evac(p - 1)
                    kt_evac(p, 3)
                    out_evac(p - 1, 0)
                body(1, True)
                with act.Fori(2, 4) as p:
                    body(p, False)
                out_evac(2, 1)
                exps(3)
                y_high(2)
                probs_evac(3)
                out_evac(3, 0)
                out_evac(3, 1)
                y_high(3)

                act.activation(ident_r[:], ident[:], ACT.Copy).then_inc(ident_ok, 1)
                for g in range(4):
                    if g < 3:
                        hi_split(half0 + (C_WO // 2 + 1 + g // 2), g % 2)
                    gx_pair(g_hi, norm + 2, g, L * G_ALL + (GROUPS0 + G_WO + 1 + g))
                    squares(norm + 2, g)
                    if g == 3:
                        hi_split(half0 + (C_WO // 2 + 1 + g // 2), g % 2)
                root(norm + 3)
                ffn_in(L, C_F2I, G_F2I, L * 2 + 1)
                ffn_out(L, C_F2O, G_F2O, norm + 3, h_hi)
            act.wait_ge(stat_done, NORMS)
            act.activation(rstd_tok[:, 0:2], ps[:, 6, 0:2], ACT.Sqrt, scale=1.0 / D, bias=eps[:, 0:1])
            act.activation(rstd_tok[0:SMP, 2:3], ps[0:SMP, 6, 2:3], ACT.Sqrt, scale=1.0 / D, bias=eps[0:SMP, 0:1]).then_inc(std_done, 1)
            act.wait_ge(rstd_ok, 1)
            for m, t in enumerate(Y_ORDER):
                n = P if t < 2 else SMP
                act.wait_ge(y_tr, m + 1)
                act.activation(y_tok[0:n, t, 0:512], ps[0:n, 2 * t, :], ACT.Copy, scale=rstd_tok[0:n, t:t + 1]).then_inc(y_tok_act, 1)

        @block.vector
        def _(dve):
            def lo_split(half, slot):
                dve.wait_ge(hi_done, half * 2 + (slot + 1))
                dve.tensor_tensor(w_lo[:, slot, :], w_raw[:, slot, :], w_hi[:, slot, :].bitcast(F32),
                                  ALU.subtract).then_inc(split_done, 1)

            def gx_pair(hi, lo, norm, o):
                dve.wait_ge(g_hi_done, norm * 4 + (o + 1))
                for k in (2 * o, 2 * o + 1):
                    ins = dve.scalar_tensor_tensor(out=lo[:, k, :], in0=x[:, k, :], scalar=gains[:, bass.ds(norm * KT + k, 1)],
                                                   in1=hi[:, k, :].bitcast(F32), op0=ALU.mult, op1=ALU.subtract)
                ins.then_inc(gx_ready, 1)

            def invert(n):
                dve.wait_ge(std_done, n)
                dve.reciprocal(rstd[:], rstd[:])
                dve.drain()

            def ffn_in(L, c0, g0, f):
                with dve.Fori(0, FT // 2) as i:
                    half = L * (C_ALL // 2) + i + (c0 // 2 + 1)
                    n = f * (FT // 2) + i + 1
                    dve.wait_ge(chunk_used, L * C_ALL + i * 2 + (c0 + 3))
                    dve.tensor_tensor(t_gate, ps[:, 0:2, 0:TOK], bc2(rstd[:]), ALU.mult).then_inc(evac_done, 1)
                    lo_split(half, 0)
                    dve.drain()
                    dve.wait_ge(chunk_used, L * C_ALL + i * 2 + (c0 + 4))
                    dve.tensor_tensor(t_up, ps[:, 2:4, 0:TOK], bc2(rstd[:]), ALU.mult).then_inc(evac_done, 1)
                    dve.drain()
                    dve.wait_ge(silu_ready, n)
                    dve.tensor_tensor(t_up, t_up, t_sil, ALU.mult).then_inc(a_ready, 1)
                    lo_split(half, 1)
                    dve.wait_ge(a_hi, n)
                    dve.tensor_tensor(act_lo[:, bass.ds(i * 2, 2), :], t_up, act_hi[:, bass.ds(i * 2, 2), :].bitcast(F32),
                                      ALU.subtract).then_inc(act_ready, 1)

            def add_to_x(L, g, chunks, scale):
                dve.wait_ge(chunk_used, L * C_ALL + (chunks + 2))
                b = 2 * (g % 2)
                dve.scalar_tensor_tensor(out=x[:, 2 * g:2 * g + 2, :], in0=ps[:, b:b + 2, 0:TOK], scalar=scale,
                                         in1=x[:, 2 * g:2 * g + 2, :], op0=ALU.mult, op1=ALU.add).then_inc(evac_done, 1)
                dve.drain()

            def ffn_out(L, c0, norm):
                for g in range(4):
                    for n in range(3):
                        if n == 2:
                            add_to_x(L, g, c0 + 3 * g + 3, 0.5)
                        c = 3 * g + n + 2
                        if g < 3 or n < 2:
                            lo_split(L * (C_ALL // 2) + (c0 + c) // 2, c % 2)
                        if n == 2:
                            gx_pair(h_hi, h_lo, norm, g)
                        if g == 3 and n == 2:
                            lo_split(L * (C_ALL // 2) + (c0 + c) // 2, c % 2)

            dve.memset(ones[:], 1.0).then_inc(prep, 1)
            dve.memset(eps[:], EPS).then_inc(prep, 1)
            dve.memset(ss[:], 0.0).then_inc(prep, 1)
            dve.sem_inc(split_done, 2)
            for j in range(4):
                dve.wait_ge(x_tr, j + 1)
                dve.tensor_copy(x[:, 2 * j:2 * j + 2, :], ps[:, 2 * j:2 * j + 2, 0:TOK]).then_inc(evac_done, 1)
                if j == 0:
                    dve.wait_ge(gain_tr, 1)
                    n = 3 * DEPTH * KT
                    dve.tensor_copy(gains[:, 0:n].rearrange("p (l n k) -> p n l k", l=DEPTH, n=3),
                                    ps[:, 0, TOK:TOK + n].rearrange("p (n l k) -> p n l k", l=DEPTH, n=3))
                    dve.tensor_copy(gains[:, n:], ps[:, 0, TOK + n:TOK + NORMS * KT + 4]).then_inc(gain_ok, 1)
                dve.drain()
                if j == 1:
                    lo_split(0, 0)
                if j:
                    gx_pair(h_hi, h_lo, 0, j - 1)
            gx_pair(h_hi, h_lo, 0, 3)
            lo_split(0, 1)
            with dve.Fori(0, DEPTH) as L:
                half0 = L * (C_ALL // 2)
                norm = L * 3
                invert(norm + 1)
                ffn_in(L, C_F1I, G_F1I, L * 2)
                ffn_out(L, C_F1O, norm + 1)
                invert(norm + 2)
                with dve.Fori(0, 5) as i:
                    for slot in range(2):
                        dve.wait_ge(chunk_used, L * C_ALL + i * 2 + (C_MIX + slot + 3))
                        dve.tensor_tensor(z[:, bass.ds(i * 4 + 2 * slot, 2), :], ps[:, 2 * slot:2 * slot + 2, 0:TOK],
                                          bc2(rstd[:]), ALU.mult).then_inc(evac_done, 1)
                        lo_split(half0 + i + (C_MIX // 2 + 1), slot)

                dve.wait_ge(loaded, 16 * len(C))

                def k_tokens(t):
                    n = P if t < 2 else SMP
                    dve.wait_ge(tr_done, 12 * L + (4 * t + 3))
                    dve.tensor_tensor(kr_tok[0:n, t, :].rearrange("p (h d) -> p h d", h=H),
                                      ps[0:n, 6, 0:HDIM].rearrange("p (h d) -> p h d", h=H),
                                      cst["k_decay"][0:n, t, :].unsqueeze(2).to_broadcast([n, H, HD]), ALU.mult).then_inc(tr_dve, 1)

                dve.memset(q_dec[:], 0.0)
                dve.drain()
                for a in range(2):
                    o = HD * a
                    for f in range(3):
                        ins = dve.tensor_tensor(q_dec[o:o + HD, f, :, 1 - a, :],
                                                z[o:o + HD, ZQR + f, SEQ:].rearrange("p (b t) -> p b t", b=NB),
                                                cst["q_decay"][o:o + HD, f, :].rearrange("p (b t) -> p b t", b=NB), ALU.mult)
                ins.then_inc(q_dec_ok, 1)
                dve.wait_ge(chunk_used, L * C_ALL + (C_MIX + 13))
                dve.tensor_tensor(z[:, 20:22, :], ps[:, 0:2, 0:TOK], bc2(rstd[:]), ALU.mult).then_inc(evac_done, 1)
                dve.wait_ge(past_done, L + 1)
                for a in range(2):
                    o = HD * a
                    ins = dve.tensor_copy(o_past[o:o + HD, :, :].rearrange("p f (b t) -> p f b t", b=NB),
                                          ps[o:o + HD, 2, 0:384].rearrange("p (f b a t) -> p f b a t", f=3, b=NB, a=2)[:, :, :, 1 - a, :])
                ins.then_inc(past_ok, 1)
                lo_split(half0 + (C_WO // 2), 0)
                k_tokens(0)
                dve.wait_ge(chunk_used, L * C_ALL + (C_MIX + 14))
                dve.tensor_tensor(z[:, 22, :], ps[:, 2, 0:TOK], rstd[:], ALU.mult).then_inc(evac_done, 1)
                dve.drain()

                es = ext[:, 542:910].rearrange("p (t b n) -> p t b n", t=2, b=NB)
                k_tokens(1)
                dve.wait_ge(pre_tr, L + 1)
                for t in range(2):
                    ins = dve.tensor_copy(es[:, t, :, 0:PAST], ps[:, 2, 120 * t:120 * t + 120].rearrange("p (b n) -> p b n", b=NB))
                ins.then_inc(pre_in, 1)
                dve.tensor_copy(q_smp[:], z[:, ZQA:ZQA + 3, SEQ:])
                k_tokens(2)

                def smax(h):
                    s = h % 2
                    dve.wait_ge(s_done, H * L + (h + 1))
                    if h >= 2:
                        dve.wait_ge(pt_done, H * L + (h - 1))
                    dve.scalar_tensor_tensor(out=s_p[:, s, :], in0=cst["dist_p"][:], scalar=-SLOPES[h] / ATT_SCALE,
                                             in1=ps[:, s, 0:384], op0=ALU.mult, op1=ALU.add)
                    dve.drain()
                    dve.tensor_reduce(st[:, 8:9], s_p[:, s, 0:256], AX, ALU.max)
                    dve.tensor_reduce(st[:, 9:10], s_p[:, s, 256:384], AX, ALU.max)
                    dve.drain()
                    dve.tensor_scalar(st[:, 2 * s:2 * s + 2], st[:, 8:10], -ATT_SCALE, None, ALU.mult).then_inc(s_max, 1)

                def decay_mask(h):
                    dve.wait_ge(r_done, H * L + (h + 1))
                    p, s = att_p[h % 2], att_s[h % 2]
                    dve.tensor_tensor(p[:, 0:256], ps[:, 5, 0:256], cst["decay_p"][:, h, :], ALU.mult)
                    dve.tensor_tensor(p[:, 256:384], ps[:, 5, 256:384], cst["decay_p"][:, h, 0:P], ALU.mult)
                    dve.tensor_tensor(s[:], ps[0:SMP, 5, 384:448], cst["decay_s"][:, h, :], ALU.mult).then_inc(r_mask, 1)

                def normalise(h):
                    s = h % 2
                    dve.wait_ge(s_exp, H * L + (h + 1))
                    dve.reciprocal(st[:, 12:14], st[:, 4 + 2 * s:6 + 2 * s])
                    dve.drain()
                    dve.tensor_scalar(s_p[:, s, 0:256], s_p[:, s, 0:256], st[:, 12:13], None, ALU.mult)
                    dve.tensor_scalar(s_p[:, s, 256:384], s_p[:, s, 256:384], st[:, 13:14], None, ALU.mult).then_inc(p_norm, 1)

                def gate(f):
                    dve.wait_ge(or_done, 3 * L + (f + 1))
                    dve.tensor_tensor(z[:, ZG + f, :], ps[:, 7, 0:TOK], z[:, ZG + f, :], ALU.mult).then_inc(o_gated, 1)

                def att_lo(f):
                    dve.wait_ge(oa_hi, 3 * L + (f + 1))
                    dve.tensor_tensor(h_lo[:, 2 + f, 0:SEQ], ps[:, 4, 0:SEQ], h_hi[:, 2 + f, 0:SEQ].bitcast(F32),
                                      ALU.subtract).then_inc(y_ready, 1)

                def new_state(f):
                    dve.wait_ge(vbd_used, H * L + (2 * f + 2))
                    dve.scalar_tensor_tensor(out=s0[:, f, :, :].rearrange("p b v -> p (b v)"),
                                             in0=s0[:, f, :, :].rearrange("p b v -> p (b v)"), scalar=cst["c_decay"][:, f:f + 1],
                                             in1=ps[:, 6, :], op0=ALU.mult, op1=ALU.add).then_inc(st_smp, 1)

                smax(0)
                decay_mask(0)
                for h in range(H):
                    f = h // 2
                    normalise(h)
                    if h + 1 < H:
                        dve.drain()
                        smax(h + 1)
                        decay_mask(h + 1)
                    if h == 1:
                        lo_split(half0 + (C_WO // 2), 1)
                    if h == 0:
                        dve.wait_ge(g_silu, L + 1)
                    if h % 2:
                        gate(f)
                        if f:
                            new_state(f - 1)
                    elif f:
                        att_lo(f - 1)
                for t in range(2):
                    dve.wait_ge(pool_hi, 2 * L + (t + 1))
                    dve.scalar_tensor_tensor(out=h_lo[:, t, :], in0=ps[:, (5, 0)[t], 0:TOK],
                                             scalar=gains[:, bass.ds(L * 2 + (NORMS * KT + t), 1)],
                                             in1=h_hi[:, t, :].bitcast(F32), op0=ALU.mult, op1=ALU.subtract).then_inc(y_ready, 1)
                att_lo(2)
                new_state(2)

                def or_norm(f):
                    dve.wait_ge(o_std, 3 * L + (f + 1))
                    dve.reciprocal(o_sq[:, f, :], o_sq[:, f, :])
                    dve.drain()
                    dve.tensor_tensor(z[:, ZG + f, :], z[:, ZG + f, :], o_sq[:, f, :], ALU.mult).then_inc(or_ready, 1)

                def or_lo(f):
                    dve.wait_ge(or_hi, 3 * L + (f + 1))
                    dve.tensor_tensor(h_lo[:, 5 + f, :], z[:, ZG + f, :], h_hi[:, 5 + f, :].bitcast(F32),
                                      ALU.subtract).then_inc(y_ready, 1)

                def soft_in(p):
                    R = slice(0, 96)
                    dve.wait_ge(own_done, L * 4 + p + 1)
                    dve.wait_ge(pt2_done, L * 8 + p * 2 + 1)
                    for c in range(2):
                        dve.tensor_reduce(ss[:, 2 * c:2 * c + 2], ps[R, c, :].rearrange("p (a n) -> p a n", a=2), AX, ALU.add)
                        dve.scalar_tensor_tensor(out=sp[:, 512 * c:512 * c + 512], in0=ps[R, c, :], scalar=ATT_SCALE,
                                                 in1=cst["alibi_s"][:, 512 * c:512 * c + 512], op0=ALU.mult, op1=ALU.add)
                    dve.scalar_tensor_tensor(out=sp[:, PAST_LEN:], in0=ps[R, 2, 0:SMP], scalar=ATT_SCALE,
                                             in1=cst["alibi_own"][:, bass.ds(p, 1), :].rearrange("p a n -> p (a n)"),
                                             op0=ALU.mult, op1=ALU.add).then_inc(sm_in, 1)
                    dve.drain()

                def soft_bias():
                    dve.tensor_reduce(ss[:, 5:6], ss[:, 0:4], AX, ALU.min)
                    dve.tensor_reduce(ss[:, 25:29], sp[:, 0:PAST_LEN].rearrange("p (a n) -> p a n", a=4), AX, ALU.max)
                    dve.tensor_reduce(ss[:, 29:30], sp[:, PAST_LEN:], AX, ALU.max)
                    dve.drain()
                    dve.tensor_scalar(ss[:, 8:12], ss[:, 0:4], ss[:, 5:6], None, ALU.is_le)
                    dve.drain()
                    dve.tensor_tensor(ss[:, 12:16], ss[:, 8:12], cst["rank"][:], ALU.mult)
                    dve.drain()
                    dve.tensor_reduce(ss[:, 16:17], ss[:, 12:16], AX, ALU.max)
                    dve.drain()
                    dve.tensor_scalar(ss[:, 20:24], ss[:, 12:16], ss[:, 16:17], -BIG, ALU.is_equal, ALU.mult)
                    dve.drain()
                    dve.tensor_tensor(ss[:, 25:30], ss[:, 25:30], ss[:, 20:25], ALU.add)
                    dve.drain()
                    dve.tensor_reduce(ss[:, 30:31], ss[:, 25:30], AX, ALU.max)
                    dve.drain()
                    dve.tensor_scalar(ss[:, 32:37], ss[:, 20:25], ss[:, 30:31], None, ALU.subtract).then_inc(sm_bias, 1)

                def soft_b(p):
                    dve.wait_ge(sm_exp, L * 4 + p + 1)
                    dve.tensor_reduce(ss[:, 45:46], ss[:, 40:45], AX, ALU.add)
                    dve.drain()
                    dve.reciprocal(ss[:, 46:47], ss[:, 45:46])
                    dve.drain()
                    dve.tensor_scalar(sp[:], sp[:], ss[:, 46:47], None, ALU.mult).then_inc(sm_ok, 1)

                def y_rest(p):
                    dve.wait_ge(ys_hi, L * 4 + p + 1)
                    for half in range(2):
                        ins = dve.tensor_tensor(y_smp(h_lo, half, p), o_smp(half), y_smp(h_hi, half, p).bitcast(F32), ALU.subtract)
                    ins.then_inc(y_ready, 1)

                for f in range(3):
                    or_norm(f)
                for f in range(3):
                    or_lo(f)

                def body(p, first):
                    soft_in(p - 1)
                    if first:
                        dve.memset(pt_s[:, 768:880], 0.0)
                    soft_bias()
                    soft_b(p - 1)
                    if not first:
                        y_rest(p - 2)
                body(1, True)
                with dve.Fori(2, 4) as p:
                    body(p, False)
                soft_in(3)
                soft_bias()
                soft_b(3)
                y_rest(2)
                y_rest(3)

                for g in range(4):
                    add_to_x(L, g, C_WO + g + 1, 1.0)
                    if g < 3:
                        lo_split(half0 + (C_WO // 2 + 1 + g // 2), g % 2)
                    gx_pair(g_hi, g_lo, norm + 2, g)
                    if g == 3:
                        lo_split(half0 + (C_WO // 2 + 1 + g // 2), g % 2)
                invert(norm + 3)
                ffn_in(L, C_F2I, G_F2I, L * 2 + 1)
                ffn_out(L, C_F2O, norm + 3)
            dve.wait_ge(std_done, NORMS)
            dve.reciprocal(rstd_tok[:, 0:2], rstd_tok[:, 0:2])
            dve.reciprocal(rstd_tok[0:SMP, 2:3], rstd_tok[0:SMP, 2:3]).then_inc(rstd_ok, 1)
            dve.drain()
            for m, t in enumerate(Y_ORDER):
                n = P if t < 2 else SMP
                dve.wait_ge(y_tr, m + 1)
                dve.tensor_scalar(y_tok[0:n, t, 512:D], ps[0:n, 2 * t + 1, :], rstd_tok[0:n, t:t + 1], None, ALU.mult).then_inc(y_tok_dve, 1)

        @block.tensor
        def _(pe):
            def products(slot, nk, cols, k0, k_all, hi, lo, bank, ready=None):
                for a in range(cols):
                    for kk in range(nk):
                        k = k0 + kk
                        if a == 0 and ready and kk in ready:
                            pe.wait_ge(*ready[kk])
                        w = slice((kk * cols + a) * P, (kk * cols + a + 1) * P)
                        out = ps[:, bank + a, 0:TOK]
                        pe.matmul(out, w_hi[:, slot, w], hi[:, k, :], start=(k == 0), stop=False)
                        pe.matmul(out, w_hi[:, slot, w], lo[:, k, :], start=False, stop=False)
                        ins = pe.matmul(out, w_lo[:, slot, w], hi[:, k, :], start=False, stop=(k == k_all - 1))
                ins.then_inc(chunk_used, 1)

            def chunk_split(half, slot):
                pe.wait_ge(split_done, half * 2 + (slot + 3))

            def banks_free(L, g):
                pe.wait_ge(evac_done, L * G_ALL + (GROUPS0 - 1) + g)

            def sum_squares(n):
                pe.wait_ge(ssq_done, n * 4)
                pe.matmul(ps[:, 4, 0:TOK], ones[:], ssq[:, 0, :], start=True, stop=False)
                pe.matmul(ps[:, 4, 0:TOK], ones[:], ssq[:, 1, :], start=False, stop=True).then_inc(stat_done, 1)

            def square_group(L, half, g, slot, hi, lo, ready, cols=2):
                chunk_split(half, slot)
                banks_free(L, g)
                products(slot, KT, cols, 0, KT, hi, lo, 2 * slot, ready)

            def gx(norm):
                return {2 * o: (gx_ready, norm * 4 + (o + 1)) for o in range(4)}

            def ffn_in(L, c0, g0, norm, hi, lo):
                half = L * (C_ALL // 2) + c0 // 2
                square_group(L, half, g0, 0, hi, lo, gx(norm))
                sum_squares(norm + 1)
                square_group(L, half, g0 + 1, 1, hi, lo, None)
                with pe.Fori(1, FT // 2) as i:
                    for slot in range(2):
                        square_group(L, half + i, i * 2 + (g0 + slot), slot, hi, lo, None)

            def ffn_out(L, c0, g0, f):
                with pe.Fori(0, 2) as i:
                    for g in range(2):
                        for n, (a, b) in enumerate(OUT_K):
                            c = 3 * g + n
                            chunk_split(L * (C_ALL // 2) + i * 3 + (c0 + c) // 2, c % 2)
                            pe.wait_ge(act_ready, f * (FT // 2) + (b + 1) // 2)
                            if n == 0:
                                banks_free(L, i * 2 + (g0 + g))
                            products(c % 2, b - a, 2, a, FT, act_hi, act_lo, 2 * g)

            for s, n in ((chunk_used, 2), (sc_done, 2), (kt_ok, 3), (pt2_done, 1)):
                pe.sem_inc(s, n)
            pe.wait_ge(x_loaded, 16 * 4)
            for j in range(4):
                for a in range(2):
                    k = 2 * j + a
                    for t in range(3):
                        n = P if t < 2 else SMP
                        ins = pe.transpose(ps[:, k, t * P:t * P + n], x_tok[0:n, t, k * P:k * P + P], ident[0:n, 0:n])
                ins.then_inc(x_tr, 1)
                if j == 1:
                    pe.wait_ge(gain_loaded, 16 * GAIN_LOADS)
                    pe.wait_ge(evac_done, 1)
                    pe.transpose(ps[:, 0, TOK:TOK + NORMS * KT + 4], g_rows[:], ident[0:NORMS * KT + 4, 0:NORMS * KT + 4]).then_inc(gain_tr, 1)
            pe.wait_ge(prep, 5)
            with pe.Fori(0, DEPTH) as L:
                half0 = L * (C_ALL // 2)
                norm = L * 3
                ffn_in(L, C_F1I, G_F1I, norm, h_hi, h_lo)
                ffn_out(L, C_F1O, G_F1O, L * 2)
                square_group(L, half0 + C_MIX // 2, G_MIX, 0, h_hi, h_lo, gx(norm + 1))
                sum_squares(norm + 2)
                square_group(L, half0 + C_MIX // 2, G_MIX + 1, 1, h_hi, h_lo, None)
                with pe.Fori(1, 5) as i:
                    for slot in range(2):
                        square_group(L, half0 + i + C_MIX // 2, i * 2 + (G_MIX + slot), slot, h_hi, h_lo, None)
                square_group(L, half0 + (C_MIX // 2 + 5), G_MIX + 10, 0, h_hi, h_lo, None)

                def tokens(t):
                    n = P if t < 2 else SMP
                    if t:
                        wait_apart(pe, tr_act, 9 * L + 3 * t)
                        wait_apart(pe, tr_dve, 3 * L + t)
                    for kind, zt in enumerate((ZKA, ZVA, ZKR, ZVR)):
                        for f in range(3):
                            ins = pe.transpose(ps[0:n, 4 + kind, P * f:P * f + P], z[:, zt + f, P * t:P * t + n], ident[:])
                        ins.then_inc(tr_done, 1)

                pe.wait_ge(evac_done, L * G_ALL + (GROUPS0 + G_MIX + 10))
                pe.wait_ge(aux_loaded, L * (16 * AUX_LOADS) + 16 * AUX_LOADS)
                pe.wait_ge(q_dec_ok, L + 1)
                for f in range(3):
                    q = q_dec[:, f, :, :, :].rearrange("p b a t -> p (b a t)")
                    pe.matmul(ps[HD:P, 2, P * f:P * f + NT], s0[:, f, 0, :], q[:, 0:NT], start=True, stop=True)
                    for b in range(NB - 1):
                        c = 2 * NT * b + NT
                        pe.matmul(ps[:, 2, P * f + c:P * f + c + 2 * NT], s0[:, f, b:b + 2, :].rearrange("p b v -> p (b v)"),
                                  q[:, c:c + 2 * NT], start=True, stop=True)
                    ins = pe.matmul(ps[0:HD, 2, P * f + P - NT:P * f + P], s0[:, f, NB - 1, :], q[:, P - NT:P], start=True, stop=True)
                ins.then_inc(past_done, 1)
                for t in range(2):
                    pe.transpose(ps[:, 3, P * t:P * t + P], z[:, ZU + t, P:2 * P], ident[:])
                for t in range(2):
                    ins = pe.transpose(ps[0:SMP, 3, POOL + P * t:POOL + P * t + P], z[:, ZU + t, SEQ:], ident[:])
                ins.then_inc(u_tr, 1)
                tokens(0)
                pe.wait_ge(past_ok, L + 1)
                square_group(L, half0 + (C_MIX // 2 + 5), G_MIX + 11, 1, h_hi, h_lo, None, cols=1)

                tokens(1)
                pe.wait_ge(evac_done, L * G_ALL + (GROUPS0 + G_MIX + 12))
                for t in range(2):
                    ins = pe.transpose(ps[:, 2, 120 * t:120 * t + 120], pre_tok[:, P * t:P * t + P], ident[0:120, 0:120])
                ins.then_inc(pre_tr, 1)
                tokens(2)

                def head(h):
                    return h // 2, slice(HD * (h % 2), HD * (h % 2) + HD), slice(h * HD, h * HD + HD)

                def scores(f):
                    if f:
                        wait_apart(pe, s_max, H * L + 2 * f)
                    for part, q, k in ((slice(0, 256), slice(P, 2 * P), slice(0, SEQ)), (slice(256, 384), slice(0, P), slice(0, P))):
                        for h in (2 * f, 2 * f + 1):
                            r = head(h)[1]
                            ins = pe.matmul(ps[:, h % 2, part], z[r, ZQA + f, q], z[r, ZKA + f, k], start=True, stop=True)
                            if part.start:
                                ins.then_inc(s_done, 1)

                def ret_scores(h):
                    f, r, c = head(h)
                    if h:
                        wait_apart(pe, r_mask, H * L + h)
                    q, k = z[r, ZQR + f, :], z[r, ZKR + f, :]
                    pe.matmul(ps[:, 5, 0:256], k[:, 0:P], q[:, 0:SEQ], start=True, stop=True)
                    pe.matmul(ps[:, 5, 256:384], k[:, P:2 * P], q[:, P:2 * P], start=True, stop=True)
                    pe.matmul(ps[0:SMP, 5, 384:448], k[:, SEQ:], q[:, SEQ:], start=True, stop=True).then_inc(r_done, 1)

                def ret_out(f):
                    pe.wait_ge(r_mask, H * L + (2 * f + 2))
                    if f:
                        pe.wait_ge(o_sqd, 3 * L + f)
                    heads = [(h % 2,) + head(h)[1:] for h in (2 * f, 2 * f + 1)]
                    for t in range(2):
                        for s, r, c in heads:
                            ins = pe.matmul(ps[r, 7, TOK + HD * f:TOK + HD * f + HD], kr_tok[:, t, c], vr_tok[:, t, c],
                                            start=(t == 0), stop=(t == 1))
                    if f == 2:
                        ins.then_inc(sp_done, 1)
                    for s, r, c in heads:
                        pe.matmul(ps[r, 7, 0:256], vr_tok[:, 0, c], att_p[s][:, 0:256], start=True, stop=False)
                    for s, r, c in heads:
                        pe.matmul(ps[r, 7, 128:256], vr_tok[:, 1, c], att_p[s][:, 256:384], start=False, stop=True)
                    for s, r, c in heads:
                        pe.matmul(ps[r, 7, 256:320], ident[:, r], o_past[:, f, :], start=True, stop=False)
                    for s, r, c in heads:
                        ins = pe.matmul(ps[r, 7, 256:320], vr_tok[0:SMP, 2, c], att_s[s][:], start=False, stop=True)
                    ins.then_inc(or_done, 1)

                def transpose_p(h):
                    s = h % 2
                    pe.wait_ge(p_norm, H * L + (h + 1))
                    if h >= 2:
                        pe.wait_ge(pt_evac, H * L + (h - 1))
                    for n, c in enumerate((256, 0, 128)):
                        ins = pe.transpose(ps[:, 2 + s, P * n:P * n + P], s_p[:, s, c:c + P], ident[:])
                    ins.then_inc(pt_done, 1)

                def att_out(f):
                    pe.wait_ge(pt_evac, H * L + (2 * f + 2))
                    if f:
                        pe.wait_ge(y_ready, 12 * L + f)
                    for t, cols, p_cols in ((0, slice(0, 256), slice(0, 256)), (1, slice(128, 256), slice(256, 384))):
                        for h in (2 * f, 2 * f + 1):
                            _, r, c = head(h)
                            ins = pe.matmul(ps[r, 4, cols], va_tok[:, t, c], pt_p[:, h % 2, p_cols], start=(t == 0), stop=(t == 1))
                    ins.then_inc(oa_done, 1)

                def smp_state(f):
                    wait_apart(pe, vbd_ok, H * L + (2 * f + 2))
                    if f:
                        wait_apart(pe, st_smp, 3 * L + f)
                    for h in (2 * f, 2 * f + 1):
                        _, r, c = head(h)
                        pe.matmul(ps[r, 6, :], kr_tok[0:SMP, 2, c], v_bd[h % 2][:].rearrange("p b v -> p (b v)"),
                                  start=True, stop=True).then_inc(vbd_used, 1)

                scores(0)
                pe.wait_ge(tr_act, 9 * L + 9)
                pe.wait_ge(tr_dve, 3 * L + 3)
                pe.wait_ge(u_out, 2 * L + 2)
                pe.wait_ge(pre_in, L + 1)
                ret_scores(0)
                for f in range(3):
                    ret_scores(2 * f + 1)
                    if f:
                        att_out(f - 1)
                    transpose_p(2 * f)
                    if f:
                        smp_state(f - 1)
                    if f < 2:
                        scores(f + 1)
                    ret_out(f)
                    if f < 2:
                        ret_scores(2 * f + 2)
                    transpose_p(2 * f + 1)
                pe.wait_ge(pool_d, L + 1)
                pe.wait_ge(s_max, H * L + (H - 1))
                pe.wait_ge(r_mask, H * L + H)
                for t in range(2):
                    pe.matmul(ps[:, (5, 0)[t], 0:TOK], wbd[:, t, :], tmp[:, 1820 + TOK * t:1820 + TOK * t + TOK],
                              start=True, stop=True).then_inc(pool_mm, 1)
                smp_state(2)
                att_out(2)

                def transpose_k(p, i):
                    pe.wait_ge(k_landed[i % 2], L * 512 + p * 128 + 64 * (i // 2 + 1))
                    for f in range(3):
                        pe.wait_ge(kt_ok, L * 48 + p * 12 + (3 * i + f + 1))
                        for j in range(4):
                            ins = pe.transpose(ps[:, 4 + f, P * j:P * j + P], kbuf[:, i % 2, j, P * f:P * f + P], ident[:])
                        ins.then_inc(kt_tr, 1)

                def key_scores(p, i):
                    bb, c = i // 2, i % 2
                    pe.wait_ge(kt_ok, L * 48 + p * 12 + (3 * i + 6))
                    for f in range(3):
                        ins = pe.matmul(ps[32 * f:32 * f + 32, c, :], q_bd[:, f, bb, :], kt[:, i % 2, f, :],
                                        start=(bb == 0), stop=(bb == 1))
                    ins.then_inc(sc_done, 1)

                def own_scores():
                    for bb in range(2):
                        for f in range(3):
                            ins = pe.matmul(ps[32 * f:32 * f + 32, 2, 0:SMP], q_bd[:, f, bb, :], k_own[:, f, :],
                                            start=(bb == 0), stop=(bb == 1))
                    ins.then_inc(own_done, 1)

                def transpose_probs(p):
                    pe.wait_ge(sm_ok, L * 4 + p + 1)
                    for j in range(5):
                        ins = pe.transpose(ps[:, 3, 96 * j:96 * j + 96], sp[:, P * j:P * j + P], ident[0:96, 0:96])
                    ins.then_inc(pt2_done, 1)
                    for j in range(5, 8):
                        pe.transpose(ps[:, 2, 96 * (j - 5):96 * (j - 4)], sp[:, P * j:P * j + P], ident[0:96, 0:96])
                    pe.transpose(ps[0:SMP, 2, 288:384], sp[:, PAST_LEN:], ident[0:96, 0:96]).then_inc(pt2_done, 1)

                def smp_out(p, bb, first):
                    if bb == 0:
                        pe.wait_ge(pt2_evac, L * 8 + p * 2 + 2)
                        if not first:
                            pe.wait_ge(y_ready, 12 * L + p + 8)
                    pe.wait_ge(v_landed[bb], L * 512 + p * 128 + 128)
                    for j in range(PAGES + 1):
                        for f in range(3):
                            rows = P if j < PAGES else SMP
                            c = 96 * j + 32 * f + 16 * bb
                            v = vbuf[:, bb, j, P * f:P * f + P] if j < PAGES else v_own[:, P * f:P * f + P]
                            ins = pe.matmul(ps[32 * f:32 * f + 32, (7, 3)[bb], 0:P], pt_s[0:rows, c:c + 32], v,
                                            start=(j == 0), stop=(j == PAGES))
                    ins.then_inc(pv_done, 1)

                def transpose_out(p):
                    for bb in range(2):
                        wait_apart(pe, o_evac, L * NB + p * 2 + (bb + 1))
                        ins = pe.transpose(ps[:, 7, 96 * bb:96 * bb + 96], o_tok[:, bb, :], ident[0:96, 0:96])
                    ins.then_inc(ot_done, 1)

                def body(p, n):
                    transpose_k(p, 0)
                    if n >= 2:
                        smp_out(p - 2, 1, False)
                    transpose_k(p, 1)
                    if n == 0:
                        mean_squares()
                    pe.wait_ge(qp_ok, L * 4 + p + 1)
                    if n >= 1:
                        pe.wait_ge(sm_in, L * 4 + p)
                    key_scores(p, 0)
                    if n >= 2:
                        transpose_out(p - 2)
                    if n == 0:
                        key_scores(p, 1)
                    transpose_k(p, 2)
                    if n:
                        key_scores(p, 1)
                    if n >= 1:
                        transpose_probs(p - 1)
                    key_scores(p, 2)
                    transpose_k(p, 3)
                    if n >= 1:
                        smp_out(p - 1, 0, n == 1)
                    key_scores(p, 3)
                    if n == 0:
                        pe.wait_ge(o_std, 3 * L + 3)
                    own_scores()

                def mean_squares():
                    pe.wait_ge(o_sqd, 3 * L + 3)
                    pe.wait_ge(pt_evac, H * L + H)
                    pe.wait_ge(st_prm, L + 1)
                    for f in range(3):
                        pe.matmul(ps[:, (2, 3, 7)[f], 0:TOK], head_mean[:], o_sq[:, f, :], start=True, stop=True).then_inc(mean_done, 1)

                pe.wait_ge(st_smp, 3 * L + 3)
                pe.wait_ge(y_ready, 12 * L + 5)
                pe.wait_ge(kown_ok, L + 1)
                body(0, 0)
                body(1, 1)
                with pe.Fori(2, 4) as p:
                    body(p, 2)

                def out_part(slot, ks, first):
                    for a in range(2):
                        for k in ks:
                            w = slice((k * 2 + a) * P, (k * 2 + a + 1) * P)
                            out = ps[:, 2 * slot + a, 0:TOK]
                            pe.matmul(out, w_hi[:, slot, w], h_hi[:, k, :], start=(first and k == ks[0]), stop=False)
                            pe.matmul(out, w_hi[:, slot, w], h_lo[:, k, :], start=False, stop=False)
                            ins = pe.matmul(out, w_lo[:, slot, w], h_hi[:, k, :], start=False, stop=(not first and k == ks[-1]))
                    if not first:
                        ins.then_inc(chunk_used, 1)

                smp_out(2, 1, False)
                transpose_out(2)
                early, late = (0, 1, 5, 6, 7), (2, 3, 4)
                chunk_split(half0 + C_WO // 2, 1)
                pe.wait_ge(sm_in, L * 4 + 4)
                out_part(0, early, True)
                transpose_probs(3)
                smp_out(3, 0, False)
                smp_out(3, 1, False)
                transpose_out(3)
                out_part(1, early[:2], True)

                pe.wait_ge(y_ready, 12 * L + 12)
                out_part(0, late, False)
                out_part(1, early[2:] + late, False)
                for slot in range(2):
                    square_group(L, half0 + (C_WO // 2 + 1), G_WO + 2 + slot, slot, h_hi, h_lo, None)
                ffn_in(L, C_F2I, G_F2I, norm + 2, g_hi, g_lo)
                ffn_out(L, C_F2O, G_F2O, L * 2 + 1)
            def to_tokens(t, ks):
                n = P if t < 2 else SMP
                for k in ks:
                    out = ps[0:n, 2 * t + k // 4, P * (k % 4):P * (k % 4) + P]
                    pe.matmul(out, h_hi[:, k, t * P:t * P + n], ident_r[:], start=True, stop=False)
                    ins = pe.matmul(out, h_lo[:, k, t * P:t * P + n], ident_r[:], start=False, stop=True)
                return ins

            pe.wait_ge(ident_ok, DEPTH)
            for t in Y_ORDER[:2]:
                to_tokens(t, range(6))
            pe.wait_ge(gx_ready, NORMS * 4)
            for t in Y_ORDER[:2]:
                to_tokens(t, range(6, KT)).then_inc(y_tr, 1)
            pe.wait_ge(ssq_done, NORMS * 4)
            for u in range(3):
                m = P if u < 2 else SMP
                for a in range(2):
                    ins = pe.matmul(ps[0:m, 6, u:u + 1], ssq[:, a, u * P:u * P + m], ones[:, 0:1], start=(a == 0), stop=(a == 1))
            ins.then_inc(stat_done, 1)
            to_tokens(Y_ORDER[2], range(KT)).then_inc(y_tr, 1)


_INS = ["x_prompt", "x_sample", "cache_k", "cache_v", "state_pool", "state_ret", "page_table", "norm_ffn1", "ffn1_w_in",
        "ffn1_w_out", "norm_mix", "w_in", "pool_w", "pool_scale", "w_out", "norm_ffn2", "ffn2_w_in", "ffn2_w_out",
        "norm_final"]
_OUTS = [("y_prompt", (1, SEQ, D)), ("y_sample", (NB, NT, D)),
         ("k_prompt", (DEPTH, 1, SEQ, H, HD)), ("v_prompt", (DEPTH, 1, SEQ, H, HD)),
         ("pool_prompt", (DEPTH, 1, PAST, POOL)), ("ret_prompt", (DEPTH, 1, H, HD, HD)),
         ("k_sample", (DEPTH, NB, NT, H, HD)), ("v_sample", (DEPTH, NB, NT, H, HD)),
         ("pool_sample", (DEPTH, NB, PAST, POOL)), ("ret_sample", (DEPTH, NB, H, HD, HD))]


def kernel(**inputs):
    import concourse.bacc as _bacc
    from concourse.bass_utils import run_bass_kernel_spmd as _run

    nc = _bacc.Bacc("TRN2", target_bir_lowering=False, num_devices=1)
    arrays, A, C, O = {}, {}, {}, {}
    for name in _INS:
        a = np.ascontiguousarray(inputs[name])
        arrays["in_" + name] = a
        A[name] = nc.dram_tensor("in_" + name, a.shape, mybir.dt.from_np(a.dtype), kind="ExternalInput").ap()
    for name, a in constants().items():
        arrays["c_" + name] = a
        C[name] = nc.dram_tensor("c_" + name, a.shape, F32, kind="ExternalInput").ap()
    for name, shape in _OUTS:
        O[name] = nc.dram_tensor("out_" + name, shape, F32, kind="ExternalOutput").ap()
    build(nc, A, C, O)
    r = _run(nc, [arrays], core_ids=[0])
    return tuple(r.results[0]["out_" + name] for name, _ in _OUTS)
```
